# Optimizing a Trainium2 kernel written in Bass

```python
import math
import jax, jax.numpy as jnp
from jax import lax
import numpy as np

D_MODEL = 1024
BATCH = 1
SEQ = 512
DEPTH = 1
DEC_BATCH = 1
DEC_SEQ = 512
PAST_LEN = 128

GRID_W = 64
ROPE_THETA = 10000.0
Q_BLOCK = 128
RMS_EPS = 1e-6

GQA_HEADS = 8
GQA_KV_HEADS = 2
GQA_HEAD_DIM = 64
MLA_HEADS = 8
MLA_Q_LORA = 256
MLA_KV_LORA = 128
MLA_NOPE = 64
MLA_ROPE = 32
MLA_V = 64

D_GQA_OUT = GQA_HEADS * GQA_HEAD_DIM
D_MLA_OUT = MLA_HEADS * MLA_V
D_MIX = D_GQA_OUT + D_MLA_OUT

IN_SPLITS = (
    GQA_HEADS * GQA_HEAD_DIM,
    GQA_KV_HEADS * GQA_HEAD_DIM,
    GQA_KV_HEADS * GQA_HEAD_DIM,
    MLA_Q_LORA,
    MLA_KV_LORA,
    MLA_ROPE,
)
D_IN = sum(IN_SPLITS)

N_EXPERTS = 16
CAPACITY_FACTOR = 2
D_FF_EXPERT = 1024

kernel_name = "hybrid_gqa_mla_ec_moe_encoder"

def rms_norm(x, g):
    xf = x.astype(jnp.float32)
    y = xf * lax.rsqrt(jnp.mean(xf * xf, axis=-1, keepdims=True) + RMS_EPS)
    return (y * g.astype(jnp.float32)).astype(x.dtype)

def axial_cos_sin(seq_len, rot_dim):
    rows = seq_len // GRID_W
    half = rot_dim // 2
    inv_freq = ROPE_THETA ** (-jnp.arange(0, half, 2, dtype=jnp.float32) / half)
    row = jnp.repeat(jnp.arange(rows, dtype=jnp.float32), GRID_W)
    col = jnp.tile(jnp.arange(GRID_W, dtype=jnp.float32), rows)
    ang_r = row[:, None] * inv_freq[None, :]
    ang_c = col[:, None] * inv_freq[None, :]
    ang = jnp.concatenate([ang_r, ang_r, ang_c, ang_c], axis=-1)
    return jnp.cos(ang), jnp.sin(ang)

def apply_axial_rope(x, cos, sin):
    r = x.shape[-1]
    h = r // 2
    q = h // 2
    xf = x.astype(jnp.float32)
    rot = jnp.concatenate([-xf[..., q:h], xf[..., :q], -xf[..., h + q:], xf[..., h:h + q]], axis=-1)
    out = xf * cos[:, None, :] + rot * sin[:, None, :]
    return out.astype(x.dtype)

def block_attention(q, k, v, scale):
    b, s, h, dq = q.shape
    kv = k.shape[2]
    g = h // kv
    dv = v.shape[-1]
    nb = s // Q_BLOCK
    qb = q.reshape(b, nb, Q_BLOCK, kv, g, dq).transpose(1, 0, 2, 3, 4, 5)

    def one_block(qblk):
        sc = jnp.einsum('bqkgd,bskd->bkgqs', qblk, k).astype(jnp.float32) * scale
        p = jax.nn.softmax(sc, axis=-1).astype(v.dtype)
        return jnp.einsum('bkgqs,bskd->bqkgd', p, v)

    o = lax.map(one_block, qb)
    return o.transpose(1, 0, 2, 3, 4, 5).reshape(b, s, h * dv)

def expert_choice_moe(h, w_router, w_gate, w_up, w_down):
    b, s, d = h.shape
    n = b * s
    xf = h.reshape(n, d)
    logits = jnp.einsum('nd,de->ne', xf, w_router).astype(jnp.float32)
    aff = jax.nn.softmax(logits, axis=-1)
    cap = CAPACITY_FACTOR * n // N_EXPERTS
    gates, idx = lax.top_k(aff.T, cap)
    xe = xf[idx]
    hid = jax.nn.silu(jnp.einsum('ecd,edf->ecf', xe, w_gate)) * jnp.einsum('ecd,edf->ecf', xe, w_up)
    ye = jnp.einsum('ecf,efd->ecd', hid, w_down) * gates[..., None].astype(h.dtype)
    y = jnp.zeros_like(xf).at[idx.reshape(-1)].add(ye.reshape(-1, d))
    return y.reshape(b, s, d)

def encoder_layer(x, p):
    b, s, _ = x.shape
    cos_a, sin_a = axial_cos_sin(s, GQA_HEAD_DIM)
    cos_b, sin_b = axial_cos_sin(s, MLA_ROPE)

    hn = rms_norm(x, p['norm_attn'])
    proj = jnp.einsum('bsd,de->bse', hn, p['w_in'])
    offs = list(np.cumsum(IN_SPLITS)[:-1])
    gq, gk, gv, c_q, c_kv, k_pe = jnp.split(proj, offs, axis=-1)

    qa = rms_norm(gq.reshape(b, s, GQA_HEADS, GQA_HEAD_DIM), p['gqa_q_norm'])
    ka = rms_norm(gk.reshape(b, s, GQA_KV_HEADS, GQA_HEAD_DIM), p['gqa_k_norm'])
    va = gv.reshape(b, s, GQA_KV_HEADS, GQA_HEAD_DIM)
    qa = apply_axial_rope(qa, cos_a, sin_a)
    ka = apply_axial_rope(ka, cos_a, sin_a)
    oa = block_attention(qa, ka, va, 1.0 / math.sqrt(GQA_HEAD_DIM))

    cq = rms_norm(c_q, p['mla_q_a_norm'])
    qb = jnp.einsum('bsr,re->bse', cq, p['mla_w_uq']).reshape(b, s, MLA_HEADS, MLA_NOPE + MLA_ROPE)
    q_nope = rms_norm(qb[..., :MLA_NOPE], p['mla_q_nope_norm'])
    q_pe = rms_norm(qb[..., MLA_NOPE:], p['mla_q_pe_norm'])
    ckv = rms_norm(c_kv, p['mla_kv_a_norm'])
    kvb = jnp.einsum('bsr,re->bse', ckv, p['mla_w_ukv']).reshape(b, s, MLA_HEADS, MLA_NOPE + MLA_V)
    k_nope = rms_norm(kvb[..., :MLA_NOPE], p['mla_k_nope_norm'])
    vb = kvb[..., MLA_NOPE:]
    k_pe = rms_norm(k_pe.reshape(b, s, 1, MLA_ROPE), p['mla_k_pe_norm'])
    q_pe = apply_axial_rope(q_pe, cos_b, sin_b)
    k_pe = apply_axial_rope(k_pe, cos_b, sin_b)
    qm = jnp.concatenate([q_nope, q_pe], axis=-1)
    km = jnp.concatenate([k_nope, jnp.broadcast_to(k_pe, (b, s, MLA_HEADS, MLA_ROPE))], axis=-1)
    ob = block_attention(qm, km, vb, 1.0 / math.sqrt(MLA_NOPE + MLA_ROPE))

    o = jnp.concatenate([rms_norm(oa, p['out_norm_a']), rms_norm(ob, p['out_norm_b'])], axis=-1)
    x = x + jnp.einsum('bse,ed->bsd', o, p['w_o'])

    h2 = rms_norm(x, p['norm_ffn'])
    x = x + expert_choice_moe(h2, p['w_router'], p['w_gate'], p['w_up'], p['w_down'])
    return x

def setup_inputs(seed: int = 0) -> dict:
    key = jax.random.key(seed)
    ks = jax.random.split(key, 24)
    f32 = jnp.float32

    def nrm(k, shape, fan_in):
        return jax.random.normal(k, shape, f32) * (fan_in ** -0.5)

    def gain(k, n):
        return 1.0 + 0.02 * jax.random.normal(k, (n,), f32)

    return {
        'x_prompt': jax.random.normal(ks[0], (BATCH, SEQ, D_MODEL), f32),
        'x_sample': jax.random.normal(ks[1], (DEC_BATCH, DEC_SEQ, D_MODEL), f32),
        'norm_attn': gain(ks[2], D_MODEL),
        'w_in': nrm(ks[3], (D_MODEL, D_IN), D_MODEL),
        'gqa_q_norm': gain(ks[4], GQA_HEAD_DIM),
        'gqa_k_norm': gain(ks[5], GQA_HEAD_DIM),
        'mla_q_a_norm': gain(ks[6], MLA_Q_LORA),
        'mla_w_uq': nrm(ks[7], (MLA_Q_LORA, MLA_HEADS * (MLA_NOPE + MLA_ROPE)), MLA_Q_LORA),
        'mla_q_nope_norm': gain(ks[8], MLA_NOPE),
        'mla_q_pe_norm': gain(ks[9], MLA_ROPE),
        'mla_kv_a_norm': gain(ks[10], MLA_KV_LORA),
        'mla_w_ukv': nrm(ks[11], (MLA_KV_LORA, MLA_HEADS * (MLA_NOPE + MLA_V)), MLA_KV_LORA),
        'mla_k_nope_norm': gain(ks[12], MLA_NOPE),
        'mla_k_pe_norm': gain(ks[13], MLA_ROPE),
        'out_norm_a': gain(ks[14], D_GQA_OUT),
        'out_norm_b': gain(ks[15], D_MLA_OUT),
        'w_o': nrm(ks[16], (D_MIX, D_MODEL), D_MIX),
        'norm_ffn': gain(ks[17], D_MODEL),
        'w_router': nrm(ks[18], (D_MODEL, N_EXPERTS), D_MODEL),
        'w_gate': nrm(ks[19], (N_EXPERTS, D_MODEL, D_FF_EXPERT), D_MODEL),
        'w_up': nrm(ks[20], (N_EXPERTS, D_MODEL, D_FF_EXPERT), D_MODEL),
        'w_down': nrm(ks[21], (N_EXPERTS, D_FF_EXPERT, D_MODEL), D_FF_EXPERT),
    }

def reference(x_prompt, x_sample, norm_attn, w_in, gqa_q_norm, gqa_k_norm,
              mla_q_a_norm, mla_w_uq, mla_q_nope_norm, mla_q_pe_norm,
              mla_kv_a_norm, mla_w_ukv, mla_k_nope_norm, mla_k_pe_norm,
              out_norm_a, out_norm_b, w_o, norm_ffn, w_router, w_gate, w_up, w_down):
    p = {
        'norm_attn': norm_attn, 'w_in': w_in,
        'gqa_q_norm': gqa_q_norm, 'gqa_k_norm': gqa_k_norm,
        'mla_q_a_norm': mla_q_a_norm, 'mla_w_uq': mla_w_uq,
        'mla_q_nope_norm': mla_q_nope_norm, 'mla_q_pe_norm': mla_q_pe_norm,
        'mla_kv_a_norm': mla_kv_a_norm, 'mla_w_ukv': mla_w_ukv,
        'mla_k_nope_norm': mla_k_nope_norm, 'mla_k_pe_norm': mla_k_pe_norm,
        'out_norm_a': out_norm_a, 'out_norm_b': out_norm_b, 'w_o': w_o,
        'norm_ffn': norm_ffn, 'w_router': w_router,
        'w_gate': w_gate, 'w_up': w_up, 'w_down': w_down,
    }
    y_prompt = x_prompt
    y_sample = x_sample
    for _ in range(DEPTH):
        y_prompt = encoder_layer(y_prompt, p)
        y_sample = encoder_layer(y_sample, p)
    return (y_prompt, y_sample)


_drawn_inputs = setup_inputs


def setup_inputs(seed=0):
    import zlib

    import numpy as np

    out = dict(_drawn_inputs(seed))
    spreads = {}
    factors = {'gqa_q_norm': 4.338,
     'gqa_k_norm': 3.893,
     'mla_q_a_norm': 3.763,
     'mla_q_nope_norm': 4.543,
     'mla_q_pe_norm': 6.606,
     'mla_k_nope_norm': 4.623,
     'mla_k_pe_norm': 7.026,
     'out_norm_a': 4.165,
     'out_norm_b': 4.308,
     'norm_ffn': 4.272}
    for name, (base, spread) in spreads.items():
        noise = np.random.default_rng([zlib.crc32(name.encode()), seed]).standard_normal(out[name].shape)
        drawn = base * np.exp(spread * noise) if base else spread * noise
        out[name] = __import__('jax').numpy.asarray(drawn.astype(out[name].dtype))
    for name, factor in factors.items():
        out[name] = (out[name] * factor).astype(out[name].dtype)
    return out
```

```python
from contextlib import ExitStack

import numpy as np

import concourse.bass as bass
from concourse import mybir

F32 = mybir.dt.float32
F32R = mybir.dt.float32r
U32 = mybir.dt.uint32
ALU = mybir.AluOpType
ACT = mybir.ActivationFunctionType
AX = mybir.AxisListType

P = 128
BANK = 512
EPS = 1e-6

SETS, SEQ, D = 2, 512, 1024
GRID_W, ROPE_THETA = 64, 10000.0
TS = SEQ // P
T = SETS * TS
KD = D // P

QH, KVH, HD = 8, 2, 64
MH, Q_LORA, KV_LORA, NOPE, PE_D, VD = 8, 256, 128, 64, 32, 64
QK = NOPE + PE_D
C_K = QH * HD
C_V = C_K + KVH * HD
C_CQ = C_V + KVH * HD
C_CKV = C_CQ + Q_LORA
C_KPE = C_CKV + KV_LORA
D_IN = C_KPE + PE_D
UQ = MH * QK
UKV = MH * (NOPE + VD)
KB = NOPE + PE_D + VD
HEADS = QH + MH
GROUP = QH // KVH

EXPERTS, FF = 16, 1024
CAP = 2 * SEQ // EXPERTS
CK = 4
CHUNK = CK * BANK
CHUNKS = 12
RING = 6

G_ATTN, G_QA, G_KVA, G_OUT, G_QN, G_KN, G_ROWS = 0, 8, 10, 11, 19, 20, 21
TAB = 2 * (HD + PE_D)
STATS = QH + KVH + 3


def rotary_tables():
    out = []
    for rot in (HD, PE_D):
        half = rot // 2
        inv = (ROPE_THETA ** (-np.arange(0, half, 2, dtype=np.float32) / half)).astype(np.float32)
        row = np.repeat(np.arange(SEQ // GRID_W, dtype=np.float32), GRID_W)
        col = np.tile(np.arange(GRID_W, dtype=np.float32), SEQ // GRID_W)
        r, c = row[:, None] * inv[None, :], col[:, None] * inv[None, :]
        angle = np.concatenate([r, r, c, c], axis=-1)
        sign = np.repeat(np.array([-1, 1, -1, 1], np.float32), rot // 4)
        out += [np.cos(angle), np.sin(angle) * sign]
    return np.concatenate(out, axis=1).astype(np.float32)


def inverse_counts():
    a = [1 / HD] * (QH + KVH) + [1 / Q_LORA, 1 / KV_LORA, 1 / PE_D] + [1 / NOPE] * MH + [1 / PE_D] * MH
    return np.tile(np.array(a, np.float32), (P, 1))


class Phase:

    def __init__(self, nc, suffix):
        self.nc, self.suffix, self.sems = nc, suffix, []

    def __enter__(self):
        return self

    def sem(self, name):
        self.sems.append(self.nc.alloc_semaphore(f"{name}_{self.suffix}"))
        return self.sems[-1]

    def __exit__(self, *failure):
        if failure[0] is None:
            self.nc.clear_and_free_semaphores(self.sems)
            self.nc.all_engine_barrier()


class Steps:

    def __init__(self, engine, sem):
        self.engine, self.sem, self.n = engine, sem, 0

    def did(self, instruction):
        instruction.then_inc(self.sem, 1)
        self.n += 1

    def wait(self):
        self.engine.wait_ge(self.sem, self.n)


def build(nc, a, out):
    x_dram = a["x"].rearrange("(t p) d -> t p d", p=P)
    out_rows = out.rearrange("(t p) d -> t p d", p=P)
    o_dram = nc.dram_tensor("attention_out", [T * P, D], F32).ap()
    o_rows = o_dram.rearrange("(t p) d -> t p d", p=P)
    h2_dram = nc.dram_tensor("h2", [T * P, D], F32).ap()
    h2_rows = h2_dram.rearrange("(t p) d -> t p d", p=P)

    with ExitStack() as ctx:
        sb = lambda name, shape, dt=F32: ctx.enter_context(nc.sbuf_tensor(name, shape, dt))
        ps = ctx.enter_context(nc.psum_tensor("ps", [P, 8, BANK], F32))

        def banks(first, n):
            return ps[:, first:first + n, :].rearrange("p b c -> p (b c)")

        k = {}
        k["ident"] = sb("ident", [P, P])
        k["tab"] = sb("tab", [P, TS, TAB])
        k["gq"] = sb("gq", [P, TS, 2, HD])
        k["gk"] = sb("gk", [P, TS, 2, HD])
        k["gqp"] = sb("gqp", [P, TS, 2, PE_D])
        k["gkp"] = sb("gkp", [P, TS, 2, PE_D])
        k["gcol"] = sb("gcol", [P, G_ROWS])
        k["invn"] = sb("invn", [P, STATS + 2 * MH])
        k["minus_half"] = sb("minus_half", [P, 16])
        k["affT"] = sb("affT", [EXPERTS, T * P])
        k["gates"] = sb("gates", [EXPERTS, SETS * CAP])
        k["idx8"] = sb("idx8", [EXPERTS, SETS * CAP], U32)

        arena = (nc.sbuf_base + 63) // 64 * 64
        used = {"n": 0}

        class Map:
            def __init__(self, at):
                self.at = at

            def __call__(self, name, shape, dt=F32):
                free = int(np.prod(shape[1:])) * 4
                t = nc.alloc_sbuf_tensor_at(name, shape, dt, offset=self.at)
                self.at += (free + 63) // 64 * 64
                return t

        rows = Map(arena)
        pj = rows("pj", [P, TS, D_IN])
        q_rows = rows("q_rows", [P, TS, MH, QK])
        kv_rows = rows("kv_rows", [P, TS, MH, KB])
        temps_at = rows.at
        stage = Map(arena)
        w_raw = stage("w_raw", [P, KD, D_IN])
        uq_raw = stage("uq_raw", [P, 2, UQ])
        ukv_raw = stage("ukv_raw", [P, UKV])
        assert stage.at <= temps_at
        tm = Map(temps_at)
        temps = {}
        temps["x"] = [tm(f"x{i}", [P, D]) for i in range(2)]
        temps["xhi"] = tm("xhi", [P, KD, P], F32R)
        temps["xlo"] = tm("xlo", [P, KD, P], F32R)
        temps["chi"] = tm("chi", [P, 3, P], F32R)
        temps["clo"] = tm("clo", [P, 3, P], F32R)
        temps["sq"] = tm("sq", [P, D_IN])
        temps["ra"] = tm("ra", [P, (QH + KVH) * HD])
        temps["gb"] = tm("gb", [P, TAB])
        temps["grow"] = tm("grow", [G_ROWS, P])
        temps["small"] = tm("small", [P, 128])
        weights_at = max(tm.at, temps_at + 33 * 1024 + 256)
        wm = Map(weights_at)
        w = {}
        w["whi"] = wm("whi", [P, KD, D_IN], F32R)
        w["wlo"] = wm("wlo", [P, KD, D_IN], F32R)
        w["uqhi"] = wm("uqhi", [P, 2, UQ], F32R)
        w["uqlo"] = wm("uqlo", [P, 2, UQ], F32R)
        w["ukvhi"] = wm("ukvhi", [P, UKV], F32R)
        w["ukvlo"] = wm("ukvlo", [P, UKV], F32R)
        end = nc.sbuf_usable_end
        assert wm.at <= end, (wm.at, end)

        am = Map(temps_at)
        att = {}
        att["hi"] = [[am(f"{n}hi{i}", [P, SEQ], F32R) for i in range(2)] for n in "qk"]
        att["lo"] = [[am(f"{n}lo{i}", [P, SEQ], F32R) for i in range(2)] for n in "qk"]
        att["p"] = [am(f"prob{i}", [P, SEQ]) for i in range(2)]
        att["pt"] = [am(f"probT{i}", [P, TS, P]) for i in range(2)]
        att["nmax"] = am("nmax", [P, HEADS * TS])
        att["sum"] = am("psum", [P, HEADS * TS])
        att["rsum"] = am("rsum", [P, HEADS * TS])
        assert am.at <= weights_at

        om = Map(weights_at)
        wo = {}
        wo["hi"] = om("wohi", [P, KD, D], F32R)
        wo["lo"] = om("wolo", [P, KD, D], F32R)
        wo["raw"] = om("woraw", [P, KD, D])
        assert om.at <= end
        om2 = Map(om.at - KD * D * 4)
        wo["othi"] = [om2(f"othi{i}", [P, KD, P], F32R) for i in range(2)]
        wo["otlo"] = [om2(f"otlo{i}", [P, KD, P], F32R) for i in range(2)]
        wo["x1"] = [om2(f"x1_{i}", [P, D]) for i in range(2)]
        wo["h2T"] = om2("h2T", [P, KD, P])
        assert om2.at <= end
        om3 = Map(temps_at)
        wo["o"] = [om3(f"o{i}", [P, D]) for i in range(2)]
        wo["x"] = [om3(f"xr{i}", [P, D]) for i in range(2)]
        wo["h2"] = [om3(f"h2_{i}", [P, D]) for i in range(2)]
        wo["gffn"] = om3("gffn", [P, D])
        wo["sq"] = om3("sqo", [P, D])
        wo["wr"] = om3("wr", [P, KD, EXPERTS])
        wo["small"] = om3("smallo", [P, 128])
        assert om3.at <= weights_at, (om3.at - weights_at)

        mm = Map(arena)
        moe = {}
        moe["raw"] = [mm(f"raw{i}", [P, CHUNK]) for i in range(RING)]
        assert mm.at <= temps_at
        mm = Map(temps_at)
        moe["hi"] = [mm(f"hi{i}", [P, CHUNK], F32R) for i in range(RING)]
        moe["lo"] = [mm(f"lo{i}", [P, CHUNK], F32R) for i in range(RING)]
        moe["xe"] = mm("xe", [P, D])
        moe["xehi"] = mm("xehi", [P, KD, P], F32R)
        moe["xelo"] = mm("xelo", [P, KD, P], F32R)
        moe["silu"] = mm("silu", [P, FF])
        moe["h"] = mm("h", [P, FF])
        moe["hthi"] = mm("hthi", [P, KD, P], F32R)
        moe["htlo"] = mm("htlo", [P, KD, P], F32R)
        moe["y"] = mm("y", [P, D])
        moe["gT"] = mm("gT", [P, EXPERTS])
        moe["idxf"] = mm("idxf", [EXPERTS, SETS * CAP])
        moe["idxT"] = mm("idxT", [P, EXPERTS], U32)
        moe["take"] = mm("take", [P, 1], U32)
        moe["give"] = mm("give", [P, 1], U32)
        assert mm.at <= end, (mm.at, end)

        raw_loaded = [ctx.enter_context(nc.semaphore(f"raw_loaded{i}")) for i in range(RING)]
        o_stored = ctx.enter_context(nc.semaphore("o_stored"))
        wo_loaded = ctx.enter_context(nc.semaphore("wo_loaded"))

        for s in range(SETS):
            project(nc, s, a, x_dram, k, temps, w, pj, q_rows, kv_rows, w_raw, uq_raw, ukv_raw, ps, banks, o_stored)
            attend(nc, s, a, k, att, wo, pj, q_rows, kv_rows, ps, banks, o_rows, o_stored, wo_loaded)
        route(nc, a, x_dram, k, wo, moe, ps, banks, o_rows, out_rows, h2_rows, raw_loaded, o_stored)
        experts(nc, a, k, moe, ps, banks, out, h2_dram, raw_loaded)


def project(nc, s, a, x_dram, k, tp, w, pj, q_rows, kv_rows, w_raw, uq_raw, ukv_raw, ps, banks, o_stored):
    first = s == 0
    x, xhi, xlo, chi, clo, sq, ra, small = (tp[n] for n in ("x", "xhi", "xlo", "chi", "clo", "sq", "ra", "small"))
    ssx, rx = small[:, 0:TS], small[:, TS:2 * TS]
    ssa, rsa = small[:, 8:8 + STATS], small[:, 24:24 + STATS]
    ssk, rsk = small[:, 40:40 + MH], small[:, 48:48 + MH]
    ssb, rsb = small[:, 56:56 + 2 * MH], small[:, 72:72 + 2 * MH]
    xt_ps = [banks(0, 1), banks(1, 1)]
    pj_ps, c_ps, u_ps = banks(2, 3)[:, 0:D_IN], banks(5, 1)[:, 0:3 * P], banks(6, 2)
    chunks = [(0, 512), (512, 1024), (1024, D_IN)]
    half = UQ // 2

    with Phase(nc, s) as phase:
        sem = phase.sem
        x_loaded = [sem("x_loaded0"), sem("x_loaded1")]
        gains_loaded, const_loaded, tables_loaded = sem("gains_loaded"), sem("const_loaded"), sem("tables_loaded")
        w_loaded, u_loaded = [sem(f"w_loaded{i}") for i in range(KD if first else 0)], sem("u_loaded")
        ident_ready, rows_set, gt_ready, gcol_ready = sem("ident_ready"), sem("rows_set"), sem("gt_ready"), sem("gcol_ready")
        whi_done, wlo_done = sem("whi_done"), sem("wlo_done")
        ssx_done, rx_done = sem("ssx_done"), sem("rx_done")
        xt_ready, xhi_done, xlo_done = sem("xt_ready"), sem("xhi_done"), sem("xlo_done")
        proj_done, pj_done, c_normed = sem("proj_done"), sem("pj_done"), sem("c_normed")
        ct_ready, chi_done, clo_done = sem("ct_ready"), sem("chi_done"), sem("clo_done")
        uq_done, q_copied = sem("uq_done"), sem("q_copied")
        ukv_done, kn_done, v_done = sem("ukv_done"), sem("kn_done"), sem("v_done")
        stat_a, stat_k, stat_b = sem("stat_a"), sem("stat_k"), sem("stat_b")
        ra_done, rk_done, rb_done = sem("ra_done"), sem("rk_done"), sem("rb_done")
        vsteps, psteps = sem("vector_steps"), sem("pool_steps")
        with nc.Block() as block:

            @block.sync
            def _(sp):
                sp.dma_start(x[0][:], x_dram[TS * s]).then_inc(x_loaded[0], 16)
                if first:
                    sp.wait_ge(rows_set, 1)
                    for row, name, n in ((G_ATTN, "norm_attn", D), (G_QA, "mla_q_a_norm", Q_LORA),
                                         (G_KVA, "mla_kv_a_norm", KV_LORA), (G_OUT, "out_norm_a", C_K),
                                         (G_OUT + C_K // P, "out_norm_b", MH * VD)):
                        sp.dma_start(tp["grow"][row:row + n // P, :], a[name].rearrange("(r c) -> r c", c=P)).then_inc(gains_loaded, 16)
                    for row, name in ((G_QN, "mla_q_nope_norm"), (G_KN, "mla_k_nope_norm")):
                        sp.dma_start(tp["grow"][row:row + 1, 0:NOPE], a[name].rearrange("(r c) -> r c", r=1)).then_inc(gains_loaded, 16)
                    for i in range(KD):
                        sp.dma_start(w_raw[:, i, :], a["w_in"][i * P:(i + 1) * P, :]).then_inc(w_loaded[i], 16)
                    sp.dma_start(uq_raw[:], a["mla_w_uq"].rearrange("(k p) n -> p k n", p=P)).then_inc(u_loaded, 16)
                    sp.dma_start(ukv_raw[:], a["mla_w_ukv"]).then_inc(u_loaded, 16)
                for t in range(1, TS):
                    if t >= 2:
                        sp.wait_ge(xt_ready, 2 * (t - 1))
                        sp.wait_ge(ssx_done, t - 1)
                    sp.dma_start(x[t % 2][:], x_dram[TS * s + t]).then_inc(x_loaded[t % 2], 16)

            @block.gpsimd
            def _(pool):
                steps = Steps(pool, psteps)
                if first:
                    pool.memset(tp["grow"][:], 1.0).then_inc(rows_set, 1)
                    pool.dma_start(k["invn"][:], a["invn"]).then_inc(const_loaded, 16)
                    pool.dma_start(k["tab"][:], a["tab"].rearrange("(i p) c -> p i c", p=P)).then_inc(tables_loaded, 16)
                    at = 0
                    for name, n in (("gqa_q_norm", HD), ("gqa_k_norm", HD), ("mla_q_pe_norm", PE_D), ("mla_k_pe_norm", PE_D)):
                        pool.dma_start(tp["gb"][:, at:at + n], a[name].partition_broadcast(P)).then_inc(tables_loaded, 16)
                        at += n
                    steps.did(pool.memset(k["minus_half"][:], -0.5))
                    steps.did(pool.memset(k["ident"][:], 0.0))
                    steps.wait()
                    pool.affine_select(out=k["ident"][:], in_=k["ident"][:], compare_op=ALU.not_equal, fill=1.0,
                                       base=0, pattern=[[-1, P]], channel_multiplier=1).then_inc(ident_ready, 1)
                    pool.wait_ge(const_loaded, 16)

                def inverse_root(dst, src, done):
                    steps.did(pool.tensor_scalar(src, src, 1.0, EPS, ALU.mult, ALU.add))
                    steps.wait()
                    pool.tensor_tensor(dst, src, k["minus_half"][:, 0:src.shape[1]], ALU.pow).then_inc(done, 1)

                def mean(src, at):
                    steps.did(pool.tensor_tensor(src, src, k["invn"][:, at:at + src.shape[1]], ALU.mult))
                    steps.wait()

                for t in range(TS + 2):
                    if t < TS:
                        pool.wait_ge(ssx_done, t + 1)
                        steps.did(pool.tensor_scalar(ssx[:, t:t + 1], ssx[:, t:t + 1], 1.0 / D, 0.0, ALU.mult, ALU.add))
                        steps.wait()
                        inverse_root(rx[:, t:t + 1], ssx[:, t:t + 1], rx_done)
                    if t >= 2:
                        pool.wait_ge(stat_k, t - 1)
                        mean(ssk, 0)
                        inverse_root(rsk, ssk, rk_done)
                        pool.wait_ge(stat_b, t - 1)
                        mean(ssb, STATS)
                        inverse_root(rsb, ssb, rb_done)
                    if t < TS:
                        pool.wait_ge(stat_a, t + 1)
                        mean(ssa, 0)
                        inverse_root(rsa, ssa, ra_done)

            @block.tensor
            def _(pe):
                if first:
                    pe.wait_ge(ident_ready, 1)
                    pe.wait_ge(gains_loaded, 7 * 16)
                    pe.transpose(ps[:, 5, 0:G_ROWS], tp["grow"][:], k["ident"][0:G_ROWS, 0:G_ROWS]).then_inc(gt_ready, 1)

                for t in range(TS + 2):
                    if t < TS:
                        pe.wait_ge(x_loaded[t % 2], 16 * (t // 2 + 1))
                        if t:
                            pe.wait_ge(xlo_done, 2 * t)
                        for b in range(2):
                            for i in range(4):
                                c = 4 * b + i
                                last = pe.transpose(xt_ps[b][:, i * P:(i + 1) * P], x[t % 2][:, c * P:(c + 1) * P], k["ident"][:])
                            last.then_inc(xt_ready, 1)
                    if t >= 2:
                        u = t - 2
                        pe.wait_ge(q_copied, u + 1)
                        if first and u == 0:
                            pe.wait_ge(wlo_done, KD + 3)
                        for n in range(2):
                            cols = slice(n * BANK, (n + 1) * BANK)
                            pe.matmul(u_ps[:, cols], chi[:, 2, :], w["ukvhi"][:, cols], start=True, stop=False)
                            pe.matmul(u_ps[:, cols], chi[:, 2, :], w["ukvlo"][:, cols], start=False, stop=False)
                            last = pe.matmul(u_ps[:, cols], clo[:, 2, :], w["ukvhi"][:, cols], start=False, stop=True)
                        last.then_inc(ukv_done, 1)
                    if t < TS:
                        if t:
                            pe.wait_ge(pj_done, 2 * t)
                        for c in range(KD):
                            pe.wait_ge(xlo_done, 2 * t + c // 4 + 1)
                            if first and t == 0:
                                pe.wait_ge(wlo_done, c + 1)
                            for lhs, rhs in ((xhi, "whi"), (xhi, "wlo"), (xlo, "whi")):
                                for lo, up in chunks:
                                    last = pe.matmul(pj_ps[:, lo:up], lhs[:, c, :], w[rhs][:, c, lo:up],
                                                     start=(c == 0 and rhs == "whi" and lhs is xhi),
                                                     stop=(c == KD - 1 and lhs is xlo))
                        last.then_inc(proj_done, 1)
                    if 1 <= t <= TS:
                        u = t - 1
                        pe.wait_ge(c_normed, u + 1)
                        if u == 0 and first:
                            pe.wait_ge(gcol_ready, 1)
                        if u:
                            pe.wait_ge(clo_done, u)
                        for i in range(3):
                            last = pe.transpose(c_ps[:, i * P:(i + 1) * P], pj[:, u, C_CQ + i * P:C_CQ + (i + 1) * P], k["ident"][:])
                        last.then_inc(ct_ready, 1)
                        pe.wait_ge(clo_done, u + 1)
                        if u:
                            pe.wait_ge(kn_done, u)
                            pe.wait_ge(v_done, u)
                        if first and u == 0:
                            pe.wait_ge(wlo_done, KD + 2)
                        for n in range(2):
                            dst = u_ps[:, n * BANK:n * BANK + half]
                            for i in range(2):
                                for lhs, rhs in ((chi, "uqhi"), (chi, "uqlo"), (clo, "uqhi")):
                                    last = pe.matmul(dst, lhs[:, i, :], w[rhs][:, i, n * half:(n + 1) * half],
                                                     start=(i == 0 and rhs == "uqhi" and lhs is chi), stop=(i == 1 and lhs is clo))
                        last.then_inc(uq_done, 1)

            @block.scalar
            def _(act):
                def split_weights():
                    act.wait_ge(gcol_ready, 2)
                    for i in range(KD):
                        act.wait_ge(w_loaded[i], 16)
                        act.activation(w["whi"][:, i, :], w_raw[:, i, :], ACT.Copy,
                                       scale=k["gcol"][:, G_ATTN + i:G_ATTN + i + 1]).then_inc(whi_done, 1)
                    act.wait_ge(u_loaded, 32)
                    for i in range(2):
                        act.activation(w["uqhi"][:, i, :], uq_raw[:, i, :], ACT.Copy,
                                       scale=k["gcol"][:, G_QA + i:G_QA + i + 1]).then_inc(whi_done, 1)
                    act.activation(w["ukvhi"][:], ukv_raw[:], ACT.Copy, scale=k["gcol"][:, G_KVA:G_KVA + 1]).then_inc(whi_done, 1)

                for t in range(TS + 2):
                    if t < TS:
                        act.wait_ge(x_loaded[t % 2], 16 * (t // 2 + 1))
                        if t:
                            act.wait_ge(stat_a, t)
                            act.wait_ge(pj_done, 2 * t)
                        act.activation(sq[:, 0:D], x[t % 2][:], ACT.Square, accum_out=ssx[:, t:t + 1]).then_inc(ssx_done, 1)
                        for b in range(2):
                            act.wait_ge(xt_ready, 2 * t + b + 1)
                            if t and b == 0:
                                act.wait_ge(proj_done, t)
                            act.activation(xhi[:, 4 * b:4 * b + 4, :], xt_ps[b].rearrange("p (a c) -> p a c", a=4),
                                           ACT.Copy).then_inc(xhi_done, 1)
                        if first and t == 0:
                            split_weights()
                    if t >= 2:
                        u = t - 2
                        act.wait_ge(ukv_done, u + 1)
                        nope = u_ps.rearrange("p (h c) -> p h c", h=MH)[:, :, 0:NOPE]
                        act.activation(kv_rows[:, u, :, 0:NOPE], nope, ACT.Copy).then_inc(kn_done, 1)
                    if t < TS:
                        act.wait_ge(proj_done, t + 1)
                        act.wait_ge(rx_done, t + 1)
                        act.wait_ge(ssx_done, t + 1)
                        if t == 0:
                            if first:
                                act.wait_ge(wlo_done, KD + 3)
                            else:
                                act.wait_ge(o_stored, 16 * s)
                        act.activation(pj[:, t, :], pj_ps, ACT.Copy, scale=rx[:, t:t + 1]).then_inc(pj_done, 1)
                        act.activation(sq[:], pj_ps, ACT.Square, scale=rx[:, t:t + 1]).then_inc(pj_done, 1)
                    if 1 <= t <= TS:
                        u = t - 1
                        act.wait_ge(ct_ready, u + 1)
                        if u:
                            act.wait_ge(ukv_done, u)
                        act.activation(chi[:], c_ps.rearrange("p (a c) -> p a c", a=3), ACT.Copy).then_inc(chi_done, 1)
                        act.wait_ge(uq_done, u + 1)
                        act.activation(q_rows[:, u].rearrange("p (n h) c -> p n (h c)", n=2),
                                       ps[:, 6:8, 0:half], ACT.Copy).then_inc(q_copied, 1)

            @block.vector
            def _(dve):
                steps = Steps(dve, vsteps)

                def broadcast(col, n, m):
                    return col.unsqueeze(2).to_broadcast([P, n, m])

                def rotate(rows_ap, heads, rot, tab_ap, tmp):
                    v = rows_ap.rearrange("p h (a b q) -> p h a b q", a=2, b=2)
                    tv = tmp.rearrange("p (h a b q) -> p h a b q", h=heads, a=2, b=2)
                    sin = tab_ap[:, 1, :].rearrange("p (a b q) -> p a b q", a=2, b=2)
                    for b in range(2):
                        for i in range(2):
                            steps.did(dve.tensor_tensor(tv[:, :, i, b, :], v[:, :, i, 1 - b, :],
                                                        sin[:, i, b, :].unsqueeze(1).to_broadcast([P, heads, rot // 4]), ALU.mult))
                    steps.wait()
                    steps.did(dve.tensor_tensor(rows_ap, rows_ap, tab_ap[:, 0, :].unsqueeze(1).to_broadcast([P, heads, rot]), ALU.mult))
                    steps.wait()
                    return dve.tensor_tensor(rows_ap, rows_ap, tmp.rearrange("p (h c) -> p h c", h=heads), ALU.add)

                def split_weights():
                    for i in range(KD):
                        dve.wait_ge(whi_done, i + 1)
                        dve.scalar_tensor_tensor(out=w["wlo"][:, i, :], in0=w_raw[:, i, :], scalar=k["gcol"][:, G_ATTN + i:G_ATTN + i + 1],
                                                 in1=w["whi"][:, i, :].bitcast(F32), op0=ALU.mult, op1=ALU.subtract).then_inc(wlo_done, 1)
                    for i in range(2):
                        dve.wait_ge(whi_done, KD + 1 + i)
                        dve.scalar_tensor_tensor(out=w["uqlo"][:, i, :], in0=uq_raw[:, i, :], scalar=k["gcol"][:, G_QA + i:G_QA + i + 1],
                                                 in1=w["uqhi"][:, i, :].bitcast(F32), op0=ALU.mult, op1=ALU.subtract).then_inc(wlo_done, 1)
                    dve.wait_ge(whi_done, KD + 3)
                    dve.scalar_tensor_tensor(out=w["ukvlo"][:], in0=ukv_raw[:], scalar=k["gcol"][:, G_KVA:G_KVA + 1],
                                             in1=w["ukvhi"][:].bitcast(F32), op0=ALU.mult, op1=ALU.subtract).then_inc(wlo_done, 1)

                def tables():
                    dve.wait_ge(tables_loaded, 5 * 16)
                    at = 0
                    for name, rot, c0 in (("gq", HD, 0), ("gk", HD, 0), ("gqp", PE_D, 2 * HD), ("gkp", PE_D, 2 * HD)):
                        g = tp["gb"][:, at:at + rot]
                        gv = g.rearrange("p (a b q) -> p a b q", a=2, b=2)
                        at += rot
                        cos, sin = k["tab"][:, :, c0:c0 + rot], k["tab"][:, :, c0 + rot:c0 + 2 * rot]
                        steps.did(dve.tensor_tensor(k[name][:, :, 0, :], cos, g.unsqueeze(1).to_broadcast([P, TS, rot]), ALU.mult))
                        sv = sin.rearrange("p i (a b q) -> p i a b q", a=2, b=2)
                        ov = k[name][:, :, 1, :].rearrange("p i (a b q) -> p i a b q", a=2, b=2)
                        for i in range(2):
                            for b in range(2):
                                steps.did(dve.tensor_tensor(ov[:, :, i, b, :], sv[:, :, i, b, :],
                                                            gv[:, i, 1 - b, :].unsqueeze(1).to_broadcast([P, TS, rot // 4]), ALU.mult))
                    steps.wait()

                if first:
                    dve.wait_ge(gt_ready, 1)
                    dve.tensor_copy(k["gcol"][:], ps[:, 5, 0:G_ROWS]).then_inc(gcol_ready, 1)
                    dve.wait_ge(gcol_ready, 1)
                    dve.tensor_scalar(k["gcol"][:, G_QN:G_QN + 1], k["gcol"][:, G_QN:G_QN + 1], float(QK) ** -0.5, None,
                                      ALU.mult).then_inc(gcol_ready, 1)

                for t in range(TS + 2):
                    if t < TS:
                        for b in range(2):
                            dve.wait_ge(xhi_done, 2 * t + b + 1)
                            hi = xhi[:, 4 * b:4 * b + 4, :]
                            dve.tensor_tensor(xlo[:, 4 * b:4 * b + 4, :], xt_ps[b].rearrange("p (a c) -> p a c", a=4),
                                              hi.bitcast(F32), ALU.subtract).then_inc(xlo_done, 1)
                        if first and t == 0:
                            split_weights()
                            tables()
                    if t >= 2:
                        u = t - 2
                        dve.wait_ge(ukv_done, u + 1)
                        dve.wait_ge(kn_done, u + 1)
                        value = u_ps.rearrange("p (h c) -> p h c", h=MH)[:, :, NOPE:NOPE + VD]
                        dve.tensor_copy(kv_rows[:, u, :, QK:KB], value).then_inc(v_done, 1)
                        kn = kv_rows[:, u, :, 0:NOPE]
                        tmp = ra[:, 0:MH * NOPE].rearrange("p (h c) -> p h c", h=MH)
                        steps.wait()
                        steps.did(dve.tensor_tensor(tmp, kn, kn, ALU.mult))
                        steps.wait()
                        dve.tensor_reduce(ssk, tmp, AX.X, ALU.add).then_inc(stat_k, 1)
                        steps.did(dve.tensor_copy(kv_rows[:, u, :, NOPE:QK],
                                                  pj[:, u, C_KPE:D_IN].unsqueeze(1).to_broadcast([P, MH, PE_D])))
                        dve.wait_ge(q_copied, u + 1)
                        q = q_rows[:, u]
                        dve.wait_ge(stat_k, u + 1)
                        steps.did(dve.tensor_tensor(tmp, q[:, :, 0:NOPE], q[:, :, 0:NOPE], ALU.mult))
                        steps.wait()
                        steps.did(dve.tensor_reduce(ssb[:, 0:MH], tmp, AX.X, ALU.add))
                        steps.wait()
                        tmp2 = ra[:, 0:MH * PE_D].rearrange("p (h c) -> p h c", h=MH)
                        steps.did(dve.tensor_tensor(tmp2, q[:, :, NOPE:QK], q[:, :, NOPE:QK], ALU.mult))
                        steps.wait()
                        dve.tensor_reduce(ssb[:, MH:2 * MH], tmp2, AX.X, ALU.add).then_inc(stat_b, 1)
                        dve.wait_ge(stat_b, u + 1)
                        dve.wait_ge(rk_done, u + 1)
                        steps.did(dve.tensor_tensor(kn, kn, broadcast(rsk, MH, NOPE), ALU.mult))
                        dve.wait_ge(rb_done, u + 1)
                        steps.did(dve.tensor_tensor(q[:, :, 0:NOPE], q[:, :, 0:NOPE], broadcast(rsb[:, 0:MH], MH, NOPE), ALU.mult))
                        steps.did(dve.tensor_tensor(q[:, :, NOPE:QK], q[:, :, NOPE:QK], broadcast(rsb[:, MH:2 * MH], MH, PE_D), ALU.mult))
                        steps.wait()
                        steps.did(rotate(q[:, :, NOPE:QK], MH, PE_D, k["gqp"][:, u], ra[:, 0:MH * PE_D]))
                        steps.wait()
                    if 1 <= t <= TS:
                        u = t - 1
                        dve.wait_ge(chi_done, u + 1)
                        dve.tensor_tensor(clo[:], c_ps.rearrange("p (a c) -> p a c", a=3), chi[:].bitcast(F32),
                                          ALU.subtract).then_inc(clo_done, 1)
                    if t < TS:
                        row = pj[:, t, :]
                        dve.wait_ge(pj_done, 2 * t + 2)
                        heads = QH + KVH
                        steps.did(dve.tensor_reduce(ssa[:, heads:heads + 1], sq[:, C_CQ:C_CKV], AX.X, ALU.add))
                        steps.did(dve.tensor_reduce(ssa[:, heads + 1:heads + 2], sq[:, C_CKV:C_KPE], AX.X, ALU.add))
                        steps.did(dve.tensor_reduce(ssa[:, heads + 2:heads + 3], sq[:, C_KPE:D_IN], AX.X, ALU.add))
                        dve.tensor_reduce(ssa[:, 0:heads], sq[:, 0:C_V].rearrange("p (h c) -> p h c", h=heads),
                                          AX.X, ALU.add).then_inc(stat_a, 1)
                        dve.wait_ge(ra_done, t + 1)
                        steps.did(dve.tensor_scalar(row[:, C_CKV:C_KPE], row[:, C_CKV:C_KPE], rsa[:, heads + 1:heads + 2], None, ALU.mult))
                        dve.tensor_scalar(row[:, C_CQ:C_CKV], row[:, C_CQ:C_CKV], rsa[:, heads:heads + 1], None, ALU.mult).then_inc(c_normed, 1)
                        steps.did(dve.tensor_scalar(row[:, C_KPE:D_IN], row[:, C_KPE:D_IN], rsa[:, heads + 2:heads + 3], None, ALU.mult))
                        qk = row[:, 0:C_V].rearrange("p (h c) -> p h c", h=heads)
                        steps.did(dve.tensor_tensor(qk, qk, broadcast(rsa[:, 0:heads], heads, HD), ALU.mult))
                        steps.wait()
                        kpe = row[:, C_KPE:D_IN].rearrange("p (h c) -> p h c", h=1)
                        steps.did(rotate(kpe, 1, PE_D, k["gkp"][:, t], ra[:, 0:PE_D]))
                        steps.wait()
                        steps.did(rotate(qk[:, 0:QH], QH, HD, k["gq"][:, t], ra[:, 0:C_K]))
                        steps.did(rotate(qk[:, QH:], KVH, HD, k["gk"][:, t], ra[:, C_K:C_V]))
                        steps.wait()


def attend(nc, s, a, k, att, wo, pj, q_rows, kv_rows, ps, banks, o_rows, o_stored, wo_loaded):
    last_set = s == SETS - 1
    units = [(h, i) for h in range(HEADS) for i in range(TS)]
    NU = len(units)
    qhi, khi = att["hi"]
    qlo, klo = att["lo"]
    preps, key_of = [], {}
    for h in range(HEADS):
        if h >= QH or h % GROUP == 0:
            preps.append(("k", h))
        key_of[h] = sum(1 for kind, _ in preps if kind == "k") - 1
        preps.append(("q", h))
    prep_index = {p: n for n, p in enumerate(preps)}
    due = {}
    for kind, h in preps:
        due.setdefault(max(0, TS * (h - 1) + (1 if kind == "k" else 2)) if h else -1, []).append((kind, h))
    S_BANKS, T_BANKS, O_BANKS, PREP = (0, 1, 2), (3, 4), (5, 6), 7

    with Phase(nc, s) as phase:
        sem = phase.sem
        prep_ready, prep_hi, prep_lo = sem("prep_ready"), sem("prep_hi"), sem("prep_lo")
        score_ready, max_done, exp_done = sem("score_ready"), sem("max_done"), sem("exp_done")
        pt_ready, pt_act, pt_dve, pv_done = sem("pt_ready"), sem("pt_act"), sem("pt_dve"), sem("pv_done")
        rsum_done, o_done = sem("rsum_done"), sem("o_done")
        wo_hi, wo_lo = sem("wo_hi"), sem("wo_lo")
        with nc.Block() as block:

            def wait_pt(eng, u):
                eng.wait_ge(pt_act if u % 2 == 0 else pt_dve, u // 2 + 1)

            def copy_pt(eng, u):
                eng.wait_ge(pt_ready, u + 1)
                if u >= 2:
                    eng.wait_ge(pv_done, u - 1)
                src = ps[:, T_BANKS[u % 2], :].rearrange("p (a c) -> p a c", a=TS)
                if u % 2 == 0:
                    eng.activation(att["pt"][0][:], src, ACT.Copy).then_inc(pt_act, 1)
                else:
                    eng.tensor_copy(att["pt"][1][:], src).then_inc(pt_dve, 1)

            @block.sync
            def _(sp):
                if last_set:
                    for i in range(KD // 2):
                        sp.dma_start(wo["raw"][:, 2 * i:2 * i + 2, :],
                                     a["w_o"].rearrange("(k p) n -> p k n", p=P)[:, 2 * i:2 * i + 2, :]).then_inc(wo_loaded, 16)
                sp.wait_ge(o_done, HEADS)
                sp.dma_start(o_rows[TS * s:TS * (s + 1)].rearrange("t p d -> p t d"), pj[:, :, 0:D]).then_inc(o_stored, 16)

            @block.tensor
            def _(pe):
                def prepare(kind, h):
                    n = prep_index[kind, h]
                    if n:
                        pe.wait_ge(prep_lo, n)
                    for i in range(TS):
                        if h < QH:
                            c = h * HD if kind == "q" else C_K + h // GROUP * HD
                            src, dst = pj[:, i, c:c + HD], ps[0:HD, PREP, i * P:(i + 1) * P]
                        else:
                            src = q_rows[:, i, h - QH, :] if kind == "q" else kv_rows[:, i, h - QH, 0:QK]
                            dst = ps[0:QK, PREP, i * P:(i + 1) * P]
                        last = pe.transpose(dst, src, k["ident"][:])
                    last.then_inc(prep_ready, 1)

                def scores(u):
                    h, i = units[u]
                    if i == 0:
                        pe.wait_ge(prep_lo, prep_index["q", h] + 1)
                    if u >= 3:
                        pe.wait_ge(exp_done, u - 2)
                    dst, q, kk, cols = ps[:, S_BANKS[u % 3], :], h % 2, key_of[h] % 2, slice(i * P, (i + 1) * P)
                    if h < QH:
                        pe.matmul(dst, qhi[q][:, cols], khi[kk][:], start=True, stop=False)
                        last = pe.matmul(dst, qhi[q][:, cols], klo[kk][:], start=False, stop=True)
                    else:
                        pe.matmul(dst, qhi[q][0:QK, cols], khi[kk][0:QK, :], start=True, stop=False)
                        pe.matmul(dst, qhi[q][0:QK, cols], klo[kk][0:QK, :], start=False, stop=False)
                        last = pe.matmul(dst, qlo[q][0:QK, cols], khi[kk][0:QK, :], start=False, stop=True)
                    last.then_inc(score_ready, 1)

                def transpose_probs(u):
                    pe.wait_ge(exp_done, u + 1)
                    if u >= 2:
                        wait_pt(pe, u - 2)
                    for i in range(TS):
                        cols = slice(i * P, (i + 1) * P)
                        last = pe.transpose(ps[:, T_BANKS[u % 2], cols], att["p"][u % 2][:, cols], k["ident"][:])
                    last.then_inc(pt_ready, 1)

                def values(u):
                    h, qi = units[u]
                    wait_pt(pe, u)
                    if qi == 0 and h >= 2:
                        pe.wait_ge(o_done, h - 1)
                    for i in range(TS):
                        if h < QH:
                            c = C_V + h // GROUP * HD
                            v = pj[:, i, c:c + HD]
                        else:
                            v = kv_rows[:, i, h - QH, QK:KB]
                        last = pe.matmul(ps[:, O_BANKS[h % 2], qi * VD:(qi + 1) * VD], att["pt"][u % 2][:, i, :], v,
                                         start=(i == 0), stop=(i == TS - 1))
                    last.then_inc(pv_done, 1)

                for kind, h in due.get(-1, []):
                    prepare(kind, h)
                for u in range(NU + 3):
                    for kind, h in due.get(u, []):
                        prepare(kind, h)
                    if u < NU:
                        scores(u)
                    if 0 <= u - 2 < NU:
                        transpose_probs(u - 2)
                    if u >= 3:
                        values(u - 3)

            @block.scalar
            def _(act):
                def prepare(kind, h):
                    n = prep_index[kind, h]
                    act.wait_ge(prep_ready, n + 1)
                    if kind == "q":
                        dst = qhi[h % 2]
                        if h >= 2:
                            act.wait_ge(score_ready, TS * (h - 1))
                    else:
                        dst = khi[key_of[h] % 2]
                        if key_of[h] >= 2:
                            act.wait_ge(score_ready, TS * (h - 1))
                    src = ps[:, PREP, :]
                    if h < QH and kind == "q":
                        act.activation(dst[0:HD, :], src[0:HD, :], ACT.Copy, scale=float(HD) ** -0.5).then_inc(prep_hi, 1)
                    elif h < QH:
                        act.activation(dst[0:HD, :], src[0:HD, :], ACT.Copy)
                        act.activation(dst[HD:P, :], src[0:HD, :], ACT.Copy).then_inc(prep_hi, 1)
                    else:
                        g = G_QN if kind == "q" else G_KN
                        act.activation(dst[0:QK, :], src[0:QK, :], ACT.Copy, scale=k["gcol"][0:QK, g:g + 1]).then_inc(prep_hi, 1)

                for kind, h in due.get(-1, []):
                    prepare(kind, h)
                for u in range(NU + 2):
                    if 0 <= u - 2 < NU and u % 2 == 0:
                        copy_pt(act, u - 2)
                    if u < NU:
                        act.wait_ge(max_done, u + 1)
                        if u >= 2:
                            act.wait_ge(pt_ready, u - 1)
                        act.activation(att["p"][u % 2][:], ps[:, S_BANKS[u % 3], :], ACT.Exp, bias=att["nmax"][:, u:u + 1],
                                       accum_out=att["sum"][:, u:u + 1]).then_inc(exp_done, 1)
                    for kind, h in due.get(u, []):
                        prepare(kind, h)
                    if last_set and u % 8 == 5 and u // 8 < KD:
                        i = u // 8
                        act.wait_ge(wo_loaded, 16 * (KD // 2))
                        act.activation(wo["hi"][:, i, :], wo["raw"][:, i, :], ACT.Copy,
                                       scale=k["gcol"][:, G_OUT + i:G_OUT + i + 1]).then_inc(wo_hi, 1)

            @block.vector
            def _(dve):
                def prepare(kind, h):
                    n = prep_index[kind, h]
                    dve.wait_ge(prep_hi, n + 1)
                    src = ps[:, PREP, :]
                    if h < QH and kind == "q":
                        dst = qhi[h % 2]
                        dve.scalar_tensor_tensor(out=dst[HD:P, :], in0=src[0:HD, :], scalar=float(HD) ** -0.5,
                                                 in1=dst[0:HD, :].bitcast(F32), op0=ALU.mult, op1=ALU.subtract).then_inc(prep_lo, 1)
                    elif h < QH:
                        kk = key_of[h] % 2
                        for rows in (slice(0, HD), slice(HD, P)):
                            last = dve.tensor_tensor(klo[kk][rows, :], src[0:HD, :], khi[kk][rows, :].bitcast(F32), ALU.subtract)
                        last.then_inc(prep_lo, 1)
                    else:
                        hi, lo = (qhi[h % 2], qlo[h % 2]) if kind == "q" else (khi[key_of[h] % 2], klo[key_of[h] % 2])
                        g = G_QN if kind == "q" else G_KN
                        dve.scalar_tensor_tensor(out=lo[0:QK, :], in0=src[0:QK, :], scalar=k["gcol"][0:QK, g:g + 1],
                                                 in1=hi[0:QK, :].bitcast(F32), op0=ALU.mult, op1=ALU.subtract).then_inc(prep_lo, 1)

                for kind, h in due.get(-1, []):
                    prepare(kind, h)
                for u in range(NU + 3):
                    if u < NU:
                        dve.wait_ge(score_ready, u + 1)
                        dve.tensor_reduce(att["nmax"][:, u:u + 1], ps[:, S_BANKS[u % 3], :], AX.X, ALU.max,
                                          negate=True).then_inc(max_done, 1)
                    if 0 <= u - 2 < NU and u % 2 == 1:
                        copy_pt(dve, u - 2)
                    for kind, h in due.get(u, []):
                        prepare(kind, h)
                    if last_set and u % 8 == 5 and u // 8 < KD:
                        i = u // 8
                        dve.wait_ge(wo_hi, i + 1)
                        dve.scalar_tensor_tensor(out=wo["lo"][:, i, :], in0=wo["raw"][:, i, :], scalar=k["gcol"][:, G_OUT + i:G_OUT + i + 1],
                                                 in1=wo["hi"][:, i, :].bitcast(F32), op0=ALU.mult, op1=ALU.subtract).then_inc(wo_lo, 1)
                    if u >= 3 and (u - 3) % TS == TS - 1:
                        h = (u - 3) // TS
                        cols = slice(TS * h, TS * (h + 1))
                        dve.wait_ge(exp_done, TS * (h + 1))
                        dve.reciprocal(att["rsum"][:, cols], att["sum"][:, cols]).then_inc(rsum_done, 1)
                        dve.wait_ge(rsum_done, h + 1)
                        dve.wait_ge(pv_done, TS * (h + 1))
                        dve.tensor_tensor(pj[:, :, h * VD:(h + 1) * VD],
                                          ps[:, O_BANKS[h % 2], 0:TS * VD].rearrange("p (i c) -> p i c", i=TS),
                                          att["rsum"][:, cols].unsqueeze(2).to_broadcast([P, TS, VD]), ALU.mult).then_inc(o_done, 1)


def load_chunk(sp, a, moe, raw_loaded, e, j):
    slot = moe["raw"][j % RING]
    if j < 8:
        half, group, name = j // 4, j % 4 // 2, "w_gate" if j % 2 == 0 else "w_up"
        src = a[name][bass.ds(e, 1), group * CK * P:(group + 1) * CK * P, half * BANK:(half + 1) * BANK]
        src = src.rearrange("e (k p) n -> p (e k) n", p=P)
        dst = slot[:].rearrange("p (k n) -> p k n", k=CK)
    else:
        i = 2 * (j - 8)
        src = a["w_down"][bass.ds(e, 1), i * P:(i + 2) * P, :].rearrange("e (k p) n -> p (e k) n", p=P)
        dst = slot[:].rearrange("p (k n) -> p k n", k=2)
    sp.dma_start(dst, src).then_inc(raw_loaded[j % RING], 16)


def route(nc, a, x_dram, k, wo, moe, ps, banks, o_rows, out_rows, h2_rows, raw_loaded, o_stored):
    o, xr, h2, gffn, sq, wr, small = (wo[n] for n in ("o", "x", "h2", "gffn", "sq", "wr", "small"))
    othi, otlo, x1, h2T = (wo[n] for n in ("othi", "otlo", "x1", "h2T"))
    sso, ro = small[:, 0:2], small[:, 2:4]
    ss2, r2 = small[:, 4:5], small[:, 5:6]
    lmax, lsum, lrec = small[:, 6:7], small[:, 7:8], small[:, 8:9]
    aff = small[:, 16:16 + EXPERTS]
    OT, WO, HT, LG, AT = (0, 1), banks(2, 2), (4, 5), ps[:, 6, 0:EXPERTS], ps[0:EXPERTS, 7, 0:P]

    with Phase(nc, "m") as phase:
        sem = phase.sem
        o_loaded, xr_loaded = [sem("o_loaded0"), sem("o_loaded1")], [sem("xr_loaded0"), sem("xr_loaded1")]
        small_loaded, x1_stored, h2_stored = sem("small_loaded"), [sem("x1_stored0"), sem("x1_stored1")], [sem("h2_stored0"), sem("h2_stored1")]
        sso_done, ro_done, on_done = sem("sso_done"), sem("ro_done"), sem("on_done")
        ot_ready, othi_done, otlo_done = sem("ot_ready"), sem("othi_done"), sem("otlo_done")
        wo_done, x1_done, ss2_done, r2_done, h2_done = sem("wo_done"), sem("x1_done"), sem("ss2_done"), sem("r2_done"), sem("h2_done")
        ht_ready, ht_copied, lg_ready = sem("ht_ready"), sem("ht_copied"), sem("lg_ready")
        lmax_done, lexp_done, lrec_done, aff_done = sem("lmax_done"), sem("lexp_done"), sem("lrec_done"), sem("aff_done")
        at_ready, at_done, psteps, vsteps = sem("at_ready"), sem("at_done"), sem("pool_steps_r"), sem("vector_steps_r")
        with nc.Block() as block:

            @block.sync
            def _(sp):
                sp.wait_ge(o_stored, 16 * SETS)
                sp.dma_start(gffn[:], a["norm_ffn"].partition_broadcast(P)).then_inc(small_loaded, 16)
                sp.dma_start(wr[:], a["w_router"].rearrange("(k p) e -> p k e", p=P)).then_inc(small_loaded, 16)
                for t in range(T):
                    if t >= 2:
                        sp.wait_ge(ot_ready, 2 * (t - 1))
                        sp.wait_ge(x1_done, 2 * (t - 1))
                    sp.dma_start(o[t % 2][:], o_rows[t]).then_inc(o_loaded[t % 2], 16)
                    sp.dma_start(xr[t % 2][:], x_dram[t]).then_inc(xr_loaded[t % 2], 16)
                    if t < RING:
                        load_chunk(sp, a, moe, raw_loaded, 0, t)

            @block.gpsimd
            def _(pool):
                steps = Steps(pool, psteps)

                def inverse_root(dst, src, n, done):
                    steps.did(pool.tensor_scalar(src, src, 1.0 / n, EPS, ALU.mult, ALU.add))
                    steps.wait()
                    pool.tensor_tensor(dst, src, k["minus_half"][:, 0:src.shape[1]], ALU.pow).then_inc(done, 1)

                for t in range(T + 1):
                    if t < T:
                        pool.wait_ge(sso_done, 2 * t + 2)
                        inverse_root(ro, sso, C_K, ro_done)
                    if t >= 1:
                        u = t - 1
                        pool.wait_ge(ss2_done, u + 1)
                        inverse_root(r2, ss2, D, r2_done)
                        pool.wait_ge(x1_done, 2 * u + 2)
                        pool.dma_start(out_rows[u], x1[u % 2][:]).then_inc(x1_stored[u % 2], 16)
                        pool.wait_ge(h2_done, u + 1)
                        pool.dma_start(h2_rows[u], h2[u % 2][:]).then_inc(h2_stored[u % 2], 16)
                for i in range(2):
                    pool.wait_ge(x1_stored[i], 16 * T // 2)
                    pool.wait_ge(h2_stored[i], 16 * T // 2)

            @block.tensor
            def _(pe):
                for t in range(T + 3):
                    if t < T:
                        pe.wait_ge(on_done, 2 * t + 2)
                        if t:
                            pe.wait_ge(otlo_done, 2 * t)
                        for b in range(2):
                            for i in range(4):
                                c = 4 * b + i
                                last = pe.transpose(ps[:, OT[b], i * P:(i + 1) * P], o[t % 2][:, c * P:(c + 1) * P], k["ident"][:])
                            last.then_inc(ot_ready, 1)
                    if 1 <= t <= T:
                        u = t - 1
                        pe.wait_ge(otlo_done, 2 * u + 2)
                        if u:
                            pe.wait_ge(x1_done, 2 * u)
                        for c in range(KD):
                            for lhs, rhs in ((othi[u % 2], "hi"), (othi[u % 2], "lo"), (otlo[u % 2], "hi")):
                                for n in range(2):
                                    cols = slice(n * BANK, (n + 1) * BANK)
                                    last = pe.matmul(WO[:, cols], lhs[:, c, :], wo[rhs][:, c, cols],
                                                     start=(c == 0 and rhs == "hi" and lhs is othi[u % 2]),
                                                     stop=(c == KD - 1 and lhs is otlo[u % 2]))
                        last.then_inc(wo_done, 1)
                    if t >= 3:
                        u = t - 3
                        pe.wait_ge(aff_done, u + 1)
                        if u:
                            pe.wait_ge(at_done, u)
                        pe.transpose(AT, aff, k["ident"][:]).then_inc(at_ready, 1)
                    if 2 <= t <= T + 1:
                        u = t - 2
                        pe.wait_ge(h2_done, u + 1)
                        if u:
                            pe.wait_ge(ht_copied, 2 * u)
                        for b in range(2):
                            for i in range(4):
                                c = 4 * b + i
                                last = pe.transpose(ps[:, HT[b], i * P:(i + 1) * P], h2[u % 2][:, c * P:(c + 1) * P], k["ident"][:])
                            last.then_inc(ht_ready, 1)
                        if u == 0:
                            pe.wait_ge(small_loaded, 32)
                        else:
                            pe.wait_ge(lexp_done, u)
                        for c in range(KD):
                            pe.wait_ge(ht_copied, 2 * u + c // 4 + 1)
                            last = pe.matmul(LG, h2T[:, c, :], wr[:, c, :], start=(c == 0), stop=(c == KD - 1))
                        last.then_inc(lg_ready, 1)

            @block.scalar
            def _(act):
                for t in range(T + 2):
                    if t < T:
                        act.wait_ge(o_loaded[t % 2], 16 * (t // 2 + 1))
                        if t:
                            act.wait_ge(ro_done, t)
                            act.wait_ge(ss2_done, t - 1) if t > 1 else None
                        for n in range(2):
                            cols = slice(n * C_K, (n + 1) * C_K)
                            act.activation(sq[:, cols], o[t % 2][:, cols], ACT.Square, accum_out=sso[:, n:n + 1]).then_inc(sso_done, 1)
                        for b in range(2):
                            act.wait_ge(ot_ready, 2 * t + b + 1)
                            if t >= 2 and b == 0:
                                act.wait_ge(wo_done, t - 1)
                            act.activation(othi[t % 2][:, 4 * b:4 * b + 4, :], ps[:, OT[b], :].rearrange("p (a c) -> p a c", a=4),
                                           ACT.Copy).then_inc(othi_done, 1)
                    if 1 <= t <= T:
                        u = t - 1
                        act.wait_ge(x1_done, 2 * u + 2)
                        act.wait_ge(sso_done, 2 * min(t + 1, T))
                        if u:
                            act.wait_ge(r2_done, u)
                        act.activation(sq[:], x1[u % 2][:], ACT.Square, accum_out=ss2).then_inc(ss2_done, 1)
                    if t >= 2:
                        u = t - 2
                        for b in range(2):
                            act.wait_ge(ht_ready, 2 * u + b + 1)
                            if u and b == 0:
                                act.wait_ge(lg_ready, u)
                            act.activation(h2T[:, 4 * b:4 * b + 4, :], ps[:, HT[b], :].rearrange("p (a c) -> p a c", a=4),
                                           ACT.Copy).then_inc(ht_copied, 1)
                        act.wait_ge(lmax_done, u + 1)
                        if u:
                            act.wait_ge(at_ready, u)
                        act.activation(aff, LG, ACT.Exp, bias=lmax, accum_out=lsum).then_inc(lexp_done, 1)

            @block.vector
            def _(dve):
                steps = Steps(dve, vsteps)
                for t in range(T + 3):
                    if t < T:
                        dve.wait_ge(ro_done, t + 1)
                        for n in range(2):
                            cols = slice(n * C_K, (n + 1) * C_K)
                            dve.tensor_scalar(o[t % 2][:, cols], o[t % 2][:, cols], ro[:, n:n + 1], None, ALU.mult).then_inc(on_done, 1)
                        for b in range(2):
                            dve.wait_ge(othi_done, 2 * t + b + 1)
                            dve.tensor_tensor(otlo[t % 2][:, 4 * b:4 * b + 4, :], ps[:, OT[b], :].rearrange("p (a c) -> p a c", a=4),
                                              othi[t % 2][:, 4 * b:4 * b + 4, :].bitcast(F32), ALU.subtract).then_inc(otlo_done, 1)
                    if 1 <= t <= T:
                        u = t - 1
                        dve.wait_ge(wo_done, u + 1)
                        dve.wait_ge(xr_loaded[u % 2], 16 * (u // 2 + 1))
                        if u >= 2:
                            dve.wait_ge(x1_stored[u % 2], 16 * (u // 2))
                            dve.wait_ge(h2_stored[u % 2], 16 * (u // 2))
                        for n in range(2):
                            cols = slice(n * BANK, (n + 1) * BANK)
                            dve.tensor_tensor(x1[u % 2][:, cols], WO[:, cols], xr[u % 2][:, cols], ALU.add).then_inc(x1_done, 1)
                        if u == 0:
                            dve.wait_ge(small_loaded, 32)
                        dve.wait_ge(x1_done, 2 * u + 2)
                        dve.wait_ge(r2_done, u + 1)
                        dve.scalar_tensor_tensor(out=h2[u % 2][:], in0=x1[u % 2][:], scalar=r2, in1=gffn[:],
                                                 op0=ALU.mult, op1=ALU.mult).then_inc(h2_done, 1)
                    if t >= 3:
                        u = t - 3
                        dve.wait_ge(at_ready, u + 1)
                        dve.tensor_copy(k["affT"][:, u * P:(u + 1) * P], AT).then_inc(at_done, 1)
                        if u == TS - 1:
                            dve.wait_ge(at_done, u + 1)
                            top_tokens(dve, k, 0, steps)
                    if 2 <= t <= T + 1:
                        u = t - 2
                        dve.wait_ge(lg_ready, u + 1)
                        dve.tensor_reduce(lmax, LG, AX.X, ALU.max, negate=True).then_inc(lmax_done, 1)
                        dve.wait_ge(lexp_done, u + 1)
                        dve.reciprocal(lrec, lsum).then_inc(lrec_done, 1)
                        dve.wait_ge(lrec_done, u + 1)
                        dve.tensor_scalar(aff, aff, lrec, None, ALU.mult).then_inc(aff_done, 1)


def top_tokens(dve, k, s, steps):
    aff = k["affT"][:, s * SEQ:(s + 1) * SEQ]
    for r in range(CAP // 8):
        cols = slice(s * CAP + 8 * r, s * CAP + 8 * r + 8)
        steps.did(dve.max(k["gates"][:, cols], aff))
        steps.wait()
        steps.did(dve.max_index(k["idx8"][:, cols], k["gates"][:, cols], aff))
        steps.wait()
        steps.did(dve.match_replace(aff, k["gates"][:, cols], aff, -1.0))
        steps.wait()


def experts(nc, a, k, moe, ps, banks, out, h2_dram, raw_loaded):
    raw, hi, lo = moe["raw"], moe["hi"], moe["lo"]
    xe, xehi, xelo, silu, h, hthi, htlo, y = (moe[n] for n in ("xe", "xehi", "xelo", "silu", "h", "hthi", "htlo", "y"))
    X, G, U, Y = (0, 1), (2, 3), (4, 5), (6, 7)
    LAST = EXPERTS - 1

    with Phase(nc, "m") as phase:
        sem = phase.sem
        hi_done, lo_done, chunk_used = sem("hi_done"), sem("lo_done"), sem("chunk_used")
        idx_float, route_ready, gates_ready, idx_ready = sem("idx_float"), sem("route_ready"), sem("gates_ready"), sem("idx_ready")
        xe_loaded, xt_ready, xehi_done, xelo_done = sem("xe_loaded"), sem("xe_transposed"), sem("xehi_done"), sem("xelo_done")
        gu_done, silu_done, h_done = sem("gu_done"), sem("silu_done"), sem("h_done")
        ht_ready, hthi_done, htlo_done = sem("h_transposed"), sem("hthi_done"), sem("htlo_done")
        y_ready, y_done, y_free, added = sem("y_ready"), sem("y_done"), sem("y_free"), sem("added")
        vsteps, psteps = sem("vector_steps_e"), sem("pool_steps_e")
        with nc.Block() as block:

            @block.sync
            def _(sp):
                need_split = sp.alloc_register("need_split")

                def load(e, j, c):
                    sp.reg_mov(need_split, c - RING + 1)
                    sp.wait_ge(raw_loaded[0], 16)
                    sp.wait_ge(lo_done, need_split)
                    load_chunk(sp, a, moe, raw_loaded, e, j)

                with sp.Fori(0, LAST) as e:
                    for j in range(RING, CHUNKS):
                        load(e, j, e * CHUNKS + j)
                    for j in range(RING):
                        load(e + 1, j, e * CHUNKS + CHUNKS + j)
                for j in range(RING, CHUNKS):
                    load(LAST, j, LAST * CHUNKS + j)

            @block.gpsimd
            def _(pool):
                need_copied = pool.alloc_register("need_copied")

                def gather(e, turn):
                    pool.tensor_copy(moe["take"][:], moe["idxT"][:, bass.ds(e, 1)]).then_inc(psteps, 1)
                    pool.reg_mov(need_copied, turn + 1)
                    pool.wait_ge(idx_ready, 1)
                    pool.wait_ge(psteps, need_copied)
                    pool.indirect_dma_start(xe[:, :], None, h2_dram, bass.IndirectOffsetOnAxis(moe["take"][:, 0:1], 0)).then_inc(xe_loaded, 16)

                def add_rows(e):
                    pool.tensor_copy(moe["give"][:], moe["idxT"][:, bass.ds(e, 1)]).then_inc(y_free, 1)
                    pool.wait_ge(idx_ready, 1)
                    pool.wait_ge(y_free, e + 1)
                    pool.wait_ge(y_done, 2 * e + 2)
                    pool.indirect_dma_start(out, bass.IndirectOffsetOnAxis(moe["give"][:, 0:1], 0), y[:, :], None,
                                            compute_op=ALU.add).then_inc(added, 16)
                    pool.wait_ge(added, 16 * e + 16)

                pool.wait_ge(idx_ready, 1)
                gather(0, 0)
                with pool.Fori(0, LAST) as e:
                    pool.wait_ge(xt_ready, 2 * e + 2)
                    pool.wait_ge(xe_loaded, 16 * e + 16)
                    gather(e + 1, e + 1)
                    add_rows(e)
                add_rows(LAST)

            @block.tensor
            def _(pe):
                def transposes(src, bank, cols, ready):
                    for i in range(4):
                        last = pe.transpose(ps[:, bank, i * P:(i + 1) * P], src[:, cols + i * P:cols + (i + 1) * P], k["ident"][:])
                    last.then_inc(ready, 1)

                def gate_up(e, j):
                    half, group = j // 4, j % 4 // 2
                    pe.wait_ge(xelo_done, 2 * e + group + 1)
                    pe.wait_ge(lo_done, e * CHUNKS + j + 2)
                    g, u = j % RING, (j + 1) % RING
                    for i in range(CK):
                        c = group * CK + i
                        cols = slice(i * BANK, (i + 1) * BANK)
                        start, stop = c == 0, c == KD - 1
                        for bank, w in ((G[half], g), (U[half], u)):
                            pe.matmul(ps[:, bank, :], xehi[:, c, :], hi[w][:, cols], start=start, stop=False)
                            pe.matmul(ps[:, bank, :], xehi[:, c, :], lo[w][:, cols], start=False, stop=False)
                        for bank, w in ((G[half], g), (U[half], u)):
                            last = pe.matmul(ps[:, bank, :], xelo[:, c, :], hi[w][:, cols], start=False, stop=stop)
                            if i == CK - 1 and not (stop and bank == U[half]):
                                last.then_inc(chunk_used, 1)
                    if c == KD - 1:
                        last.then_inc(gu_done, 1)

                def down(e, j):
                    pe.wait_ge(lo_done, e * CHUNKS + j + 1)
                    w = j % RING
                    for i in range(2):
                        f = 2 * (j - 8) + i
                        for lhs, part in ((hthi, hi), (hthi, lo), (htlo, hi)):
                            for n in range(2):
                                cols = slice(i * D + n * BANK, i * D + (n + 1) * BANK)
                                last = pe.matmul(ps[:, Y[n], :], lhs[:, f, :], part[w][:, cols],
                                                 start=(f == 0 and part is hi and lhs is hthi), stop=(f == KD - 1 and lhs is htlo))
                    last.then_inc(y_ready if j == CHUNKS - 1 else chunk_used, 1)

                def expert(e, more):
                    gate_up(e, 0)
                    gate_up(e, 2)
                    gate_up(e, 4)
                    pe.wait_ge(h_done, 2 * e + 1)
                    transposes(h, X[0], 0, ht_ready)
                    gate_up(e, 6)
                    pe.wait_ge(htlo_done, 2 * e + 1)
                    down(e, 8)
                    pe.wait_ge(h_done, 2 * e + 2)
                    transposes(h, X[1], BANK, ht_ready)
                    down(e, 9)
                    if more:
                        pe.wait_ge(xe_loaded, 16 * e + 32)
                        transposes(xe, X[0], 0, xt_ready)
                    pe.wait_ge(htlo_done, 2 * e + 2)
                    down(e, 10)
                    if more:
                        transposes(xe, X[1], BANK, xt_ready)
                    down(e, 11)

                pe.wait_ge(route_ready, 1)
                pe.transpose(ps[:, Y[0], 0:EXPERTS], k["gates"][:], k["ident"][0:EXPERTS, 0:EXPERTS])
                pe.transpose(ps[:, Y[0], P:P + EXPERTS], moe["idxf"][:], k["ident"][0:EXPERTS, 0:EXPERTS]).then_inc(route_ready, 1)
                pe.wait_ge(xe_loaded, 16)
                transposes(xe, X[0], 0, xt_ready)
                transposes(xe, X[1], BANK, xt_ready)
                with pe.Fori(0, LAST) as e:
                    expert(e, True)
                expert(LAST, False)

            def wait_used(eng, e, j):
                c = j - RING
                if c < 0:
                    c += CHUNKS
                    e = e - 1
                if c == 3:
                    eng.wait_ge(gu_done, 2 * e + 1)
                elif c == 7:
                    eng.wait_ge(gu_done, 2 * e + 2)
                elif c == CHUNKS - 1:
                    eng.wait_ge(y_ready, e + 1)
                else:
                    n = c + 1 - (c > 3) - (c > 7)
                    eng.wait_ge(chunk_used, e * (CHUNKS - 3) + n)

            @block.scalar
            def _(act):
                def split(e, j, wait=True):
                    act.wait_ge(raw_loaded[j % RING], 16 * (e * (CHUNKS // RING) + j // RING + 1))
                    if wait:
                        wait_used(act, e, j)
                    act.activation(hi[j % RING][:], raw[j % RING][:], ACT.Copy).then_inc(hi_done, 1)

                def high(dst, b, ready, n, done):
                    act.wait_ge(ready, n)
                    act.activation(dst[:, 4 * b:4 * b + 4, :], ps[:, X[b], :].rearrange("p (a c) -> p a c", a=4), ACT.Copy).then_inc(done, 1)

                def gate(e, half):
                    act.wait_ge(gu_done, 2 * e + half + 1)
                    act.activation(silu[:, half * BANK:(half + 1) * BANK], ps[:, G[half], :], ACT.Silu).then_inc(silu_done, 1)

                def expert(e, more):
                    split(e, 6)
                    split(e, 7)
                    gate(e, 0)
                    split(e, 8)
                    split(e, 9)
                    high(hthi, 0, ht_ready, 2 * e + 1, hthi_done)
                    split(e, 10)
                    split(e, 11)
                    gate(e, 1)
                    if more:
                        split(e + 1, 0)
                        split(e + 1, 1)
                    high(hthi, 1, ht_ready, 2 * e + 2, hthi_done)
                    if more:
                        split(e + 1, 2)
                        high(xehi, 0, xt_ready, 2 * e + 3, xehi_done)
                        split(e + 1, 3)
                        high(xehi, 1, xt_ready, 2 * e + 4, xehi_done)
                        split(e + 1, 4)
                        split(e + 1, 5)
                    act.wait_ge(y_ready, e + 1)
                    act.wait_ge(y_free, e + 1)
                    for n in range(2):
                        act.activation(y[:, n * BANK:(n + 1) * BANK], ps[:, Y[n], :], ACT.Copy,
                                       scale=moe["gT"][:, bass.ds(e, 1)]).then_inc(y_done, 1)

                for j in range(RING):
                    split(0, j, wait=False)
                for b in range(2):
                    high(xehi, b, xt_ready, b + 1, xehi_done)
                act.wait_ge(gates_ready, 1)
                with act.Fori(0, LAST) as e:
                    expert(e, True)
                expert(LAST, False)

            @block.vector
            def _(dve):
                steps = Steps(dve, vsteps)

                def split(e, j):
                    dve.wait_ge(hi_done, e * CHUNKS + j + 1)
                    dve.tensor_tensor(lo[j % RING][:], raw[j % RING][:], hi[j % RING][:].bitcast(F32), ALU.subtract).then_inc(lo_done, 1)

                def low(dst, part, b, ready, n, done):
                    dve.wait_ge(ready, n)
                    cols = slice(4 * b, 4 * b + 4)
                    dve.tensor_tensor(dst[:, cols, :], ps[:, X[b], :].rearrange("p (a c) -> p a c", a=4),
                                      part[:, cols, :].bitcast(F32), ALU.subtract).then_inc(done, 1)

                def product(e, half):
                    cols = slice(half * BANK, (half + 1) * BANK)
                    dve.wait_ge(silu_done, 2 * e + half + 1)
                    dve.tensor_tensor(h[:, cols], ps[:, U[half], :], silu[:, cols], ALU.mult).then_inc(h_done, 1)

                def expert(e, more):
                    split(e, 6)
                    split(e, 7)
                    product(e, 0)
                    split(e, 8)
                    split(e, 9)
                    low(htlo, hthi, 0, hthi_done, 2 * e + 1, htlo_done)
                    split(e, 10)
                    split(e, 11)
                    product(e, 1)
                    if more:
                        split(e + 1, 0)
                        split(e + 1, 1)
                    low(htlo, hthi, 1, hthi_done, 2 * e + 2, htlo_done)
                    if more:
                        split(e + 1, 2)
                        low(xelo, xehi, 0, xehi_done, 2 * e + 3, xelo_done)
                        split(e + 1, 3)
                        low(xelo, xehi, 1, xehi_done, 2 * e + 4, xelo_done)
                        split(e + 1, 4)
                        split(e + 1, 5)

                top_tokens(dve, k, 1, steps)
                steps.did(dve.tensor_copy(moe["idxf"][:], k["idx8"][:]))
                steps.wait()
                dve.tensor_scalar(moe["idxf"][:, CAP:2 * CAP], moe["idxf"][:, CAP:2 * CAP], float(SEQ), None, ALU.add).then_inc(route_ready, 1)
                dve.wait_ge(route_ready, 2)
                dve.tensor_copy(moe["idxT"][:], ps[:, Y[0], P:P + EXPERTS]).then_inc(idx_ready, 1)
                dve.tensor_copy(moe["gT"][:], ps[:, Y[0], 0:EXPERTS]).then_inc(gates_ready, 1)
                for j in range(RING):
                    split(0, j)
                for b in range(2):
                    low(xelo, xehi, b, xehi_done, b + 1, xelo_done)
                with dve.Fori(0, LAST) as e:
                    expert(e, True)
                expert(LAST, False)


_WEIGHTS = ["norm_attn", "w_in", "gqa_q_norm", "gqa_k_norm", "mla_q_a_norm", "mla_w_uq", "mla_q_nope_norm",
            "mla_q_pe_norm", "mla_kv_a_norm", "mla_w_ukv", "mla_k_nope_norm", "mla_k_pe_norm", "out_norm_a",
            "out_norm_b", "w_o", "norm_ffn", "w_router", "w_gate", "w_up", "w_down"]


def kernel(x_prompt, x_sample, **weights):
    import numpy as _np
    import concourse.bacc as _bacc
    from concourse import mybir as _mybir
    from concourse.bass_utils import run_bass_kernel_spmd as _run

    nc = _bacc.Bacc("TRN2", target_bir_lowering=False, num_devices=1)
    named = {"x": _np.concatenate([_np.asarray(x_prompt).reshape(SEQ, D), _np.asarray(x_sample).reshape(SEQ, D)]),
             "tab": rotary_tables(), "invn": inverse_counts()}
    for name in _WEIGHTS:
        named[name] = _np.ascontiguousarray(weights[name])
    aps = {n: nc.dram_tensor(f"in_{n}", v.shape, _mybir.dt.from_np(v.dtype), kind="ExternalInput").ap() for n, v in named.items()}
    out = nc.dram_tensor("out", (SETS * SEQ, D), _mybir.dt.float32, kind="ExternalOutput").ap()
    build(nc, aps, out)
    r = _run(nc, [{f"in_{n}": v for n, v in named.items()}], core_ids=[0])
    got = r.results[0]["out"]
    return got[0:SEQ].reshape(1, SEQ, D), got[SEQ:].reshape(1, SEQ, D)
```

```python
from contextlib import ExitStack

import numpy as np

import concourse.bass as bass
from concourse import mybir

F32 = mybir.dt.float32
F32R = mybir.dt.float32r
U32 = mybir.dt.uint32
ALU = mybir.AluOpType
ACT = mybir.ActivationFunctionType
AX = mybir.AxisListType

P = 128
BANK = 512
EPS = 1e-6

SETS, SEQ, D = 2, 512, 1024
GRID_W, ROPE_THETA = 64, 10000.0
TS = SEQ // P
T = SETS * TS
KD = D // P

QH, KVH, HD = 8, 2, 64
MH, Q_LORA, KV_LORA, NOPE, PE_D, VD = 8, 256, 128, 64, 32, 64
QK = NOPE + PE_D
C_K = QH * HD
C_V = C_K + KVH * HD
C_CQ = C_V + KVH * HD
C_CKV = C_CQ + Q_LORA
C_KPE = C_CKV + KV_LORA
D_IN = C_KPE + PE_D
UQ = MH * QK
UKV = MH * (NOPE + VD)
KB = NOPE + PE_D + VD
HEADS = QH + MH
GROUP = QH // KVH

EXPERTS, FF = 16, 1024
CAP = 2 * SEQ // EXPERTS
CK = 4
CHUNK = CK * BANK
CHUNKS = 12
RING = 6

G_ATTN, G_QA, G_KVA, G_OUT, G_QN, G_KN, G_ROWS = 0, 8, 10, 11, 19, 20, 21
TAB = 2 * (HD + PE_D)
STATS = QH + KVH + 3


def rotary_tables():
    out = []
    for rot in (HD, PE_D):
        half = rot // 2
        inv = (ROPE_THETA ** (-np.arange(0, half, 2, dtype=np.float32) / half)).astype(np.float32)
        row = np.repeat(np.arange(SEQ // GRID_W, dtype=np.float32), GRID_W)
        col = np.tile(np.arange(GRID_W, dtype=np.float32), SEQ // GRID_W)
        r, c = row[:, None] * inv[None, :], col[:, None] * inv[None, :]
        angle = np.concatenate([r, r, c, c], axis=-1)
        sign = np.repeat(np.array([-1, 1, -1, 1], np.float32), rot // 4)
        out += [np.cos(angle), np.sin(angle) * sign]
    return np.concatenate(out, axis=1).astype(np.float32)


def inverse_counts():
    a = [1 / HD] * (QH + KVH) + [1 / Q_LORA, 1 / KV_LORA, 1 / PE_D] + [1 / NOPE] * MH + [1 / PE_D] * MH
    return np.tile(np.array(a, np.float32), (P, 1))


class Phase:

    def __init__(self, nc, suffix):
        self.nc, self.suffix, self.sems = nc, suffix, []

    def __enter__(self):
        return self

    def sem(self, name):
        self.sems.append(self.nc.alloc_semaphore(f"{name}_{self.suffix}"))
        return self.sems[-1]

    def __exit__(self, *failure):
        if failure[0] is None:
            self.nc.clear_and_free_semaphores(self.sems)
            self.nc.all_engine_barrier()


class Steps:

    def __init__(self, engine, sem):
        self.engine, self.sem, self.n = engine, sem, 0

    def did(self, instruction):
        instruction.then_inc(self.sem, 1)
        self.n += 1

    def wait(self):
        self.engine.wait_ge(self.sem, self.n)


def build(nc, a, out):
    x_dram = a["x"].rearrange("(t p) d -> t p d", p=P)
    out_rows = out.rearrange("(t p) d -> t p d", p=P)
    o_dram = nc.dram_tensor("attention_out", [T * P, D], F32).ap()
    o_rows = o_dram.rearrange("(t p) d -> t p d", p=P)
    h2_dram = nc.dram_tensor("h2", [T * P, D], F32).ap()
    h2_rows = h2_dram.rearrange("(t p) d -> t p d", p=P)

    with ExitStack() as ctx:
        sb = lambda name, shape, dt=F32: ctx.enter_context(nc.sbuf_tensor(name, shape, dt))
        ps = ctx.enter_context(nc.psum_tensor("ps", [P, 8, BANK], F32))

        def banks(first, n):
            return ps[:, first:first + n, :].rearrange("p b c -> p (b c)")

        k = {}
        k["ident"] = sb("ident", [P, P])
        k["tab"] = sb("tab", [P, TS, TAB])
        k["gq"] = sb("gq", [P, TS, 2, HD])
        k["gk"] = sb("gk", [P, TS, 2, HD])
        k["gqp"] = sb("gqp", [P, TS, 2, PE_D])
        k["gkp"] = sb("gkp", [P, TS, 2, PE_D])
        k["gcol"] = sb("gcol", [P, G_ROWS])
        k["invn"] = sb("invn", [P, STATS + 2 * MH])
        k["minus_half"] = sb("minus_half", [P, 16])
        k["affT"] = sb("affT", [EXPERTS, T * P])
        k["gates"] = sb("gates", [EXPERTS, SETS * CAP])
        k["idx8"] = sb("idx8", [EXPERTS, SETS * CAP], U32)

        arena = (nc.sbuf_base + 63) // 64 * 64
        used = {"n": 0}

        class Map:
            def __init__(self, at):
                self.at = at

            def __call__(self, name, shape, dt=F32):
                free = int(np.prod(shape[1:])) * 4
                t = nc.alloc_sbuf_tensor_at(name, shape, dt, offset=self.at)
                self.at += (free + 63) // 64 * 64
                return t

        rows = Map(arena)
        pj = rows("pj", [P, TS, D_IN])
        q_rows = rows("q_rows", [P, TS, MH, QK])
        kv_rows = rows("kv_rows", [P, TS, MH, KB])
        temps_at = rows.at
        stage = Map(arena)
        w_raw = stage("w_raw", [P, KD, D_IN])
        uq_raw = stage("uq_raw", [P, 2, UQ])
        ukv_raw = stage("ukv_raw", [P, UKV])
        assert stage.at <= temps_at
        tm = Map(temps_at)
        temps = {}
        temps["x"] = [tm(f"x{i}", [P, D]) for i in range(2)]
        temps["chi"] = tm("chi", [P, 3, P], F32R)
        temps["clo"] = tm("clo", [P, 3, P], F32R)
        temps["sq"] = tm("sq", [P, D_IN])
        temps["ra"] = tm("ra", [P, (QH + KVH) * HD])
        temps["gb"] = tm("gb", [P, TAB])
        temps["grow"] = tm("grow", [G_ROWS, P])
        temps["small"] = tm("small", [P, 128])
        weights_at = temps_at + 33 * 1024 + 256
        wm = Map(weights_at)
        w = {}
        w["whi"] = wm("whi", [P, KD, D_IN], F32R)
        w["wlo"] = wm("wlo", [P, KD, D_IN], F32R)
        w["uqhi"] = wm("uqhi", [P, 2, UQ], F32R)
        w["uqlo"] = wm("uqlo", [P, 2, UQ], F32R)
        w["ukvhi"] = wm("ukvhi", [P, UKV], F32R)
        w["ukvlo"] = wm("ukvlo", [P, UKV], F32R)
        end = nc.sbuf_usable_end // 64 * 64
        w_end = wm.at
        temps["xhi"] = [tm("xhi0", [P, KD, P], F32R), wm("xhi1", [P, KD, P], F32R)]
        temps["xlo"] = [tm("xlo0", [P, KD, P], F32R), wm("xlo1", [P, KD, P], F32R)]
        assert wm.at <= end and tm.at <= weights_at

        am = Map(temps_at)
        att = {}
        att["hi"] = [[am(f"{n}hi{i}", [P, SEQ], F32R) for i in range(2)] for n in "qk"]
        att["lo"] = [[am(f"{n}lo{i}", [P, SEQ], F32R) for i in range(2)] for n in "qk"]
        att["p"] = [am(f"prob{i}", [P, SEQ]) for i in range(2)]
        att["pthi"] = [am(f"probThi{i}", [P, TS, 2 * P], F32R) for i in range(2)]
        att["nmax"] = am("nmax", [P, HEADS * TS])
        att["sum"] = am("psum", [P, HEADS * TS])
        att["rsum"] = am("rsum", [P, HEADS * TS])
        att["ot"] = am("ot", [VD, SEQ])
        att["otv"] = am("otv", [VD, SEQ])
        assert am.at <= weights_at

        om = Map(weights_at)
        wo = {}
        wo["hi"] = om("wohi", [P, KD, D], F32R)
        wo["lo"] = om("wolo", [P, KD, D], F32R)
        wo["raw"] = om("woraw", [P, KD, D])
        assert om.at <= end
        am = Map(om.at)
        att["ptlo"] = [am(f"probTlo{i}", [P, TS, 2 * P], F32R) for i in range(2)]
        att["v"] = [am(f"v{i}", [P, TS, 2, VD], F32R) for i in range(2)]
        assert am.at <= end
        om2 = Map(om.at - KD * D * 4)
        wo["othi"] = [om2(f"othi{i}", [P, KD, P], F32R) for i in range(2)]
        wo["otlo"] = [om2(f"otlo{i}", [P, KD, P], F32R) for i in range(2)]
        wo["x1"] = [om2(f"x1_{i}", [P, D]) for i in range(2)]
        wo["h2T"] = om2("h2T", [P, KD, P])
        assert om2.at <= end
        om3 = Map(temps_at)
        om4 = Map(om.at)
        wo["o"] = [om3("o0", [P, D]), om3("o1", [P, D]), om4("o2", [P, D])]
        wo["x"] = [om3("xr0", [P, D]), om3("xr1", [P, D]), om4("xr2", [P, D])]
        assert om4.at <= end
        wo["h2"] = [om3(f"h2_{i}", [P, D]) for i in range(2)]
        wo["gffn"] = om3("gffn", [P, D])
        wo["sq"] = om3("sqo", [P, D])
        wo["wr"] = om3("wr", [P, KD, EXPERTS])
        wo["small"] = om3("smallo", [P, 128])
        assert om3.at <= weights_at, (om3.at - weights_at)

        mm = Map(arena)
        moe = {}
        moe["raw"] = [mm(f"raw{i}", [P, CHUNK]) for i in range(RING)]
        assert mm.at <= temps_at
        mm = Map(temps_at)
        moe["hi"] = [mm(f"hi{i}", [P, CHUNK], F32R) for i in range(RING)]
        moe["lo"] = [mm(f"lo{i}", [P, CHUNK], F32R) for i in range(RING)]
        moe["xe"] = mm("xe", [P, D])
        moe["xehi"] = mm("xehi", [P, KD, P], F32R)
        moe["xelo"] = mm("xelo", [P, KD, P], F32R)
        moe["silu"] = mm("silu", [P, FF])
        moe["h"] = mm("h", [P, FF])
        moe["hthi"] = mm("hthi", [P, KD, P], F32R)
        moe["htlo"] = mm("htlo", [P, KD, P], F32R)
        moe["y"] = mm("y", [P, D])
        moe["gT"] = mm("gT", [P, EXPERTS])
        moe["idxf"] = mm("idxf", [EXPERTS, SETS * CAP])
        moe["idxT"] = mm("idxT", [P, EXPERTS], U32)
        moe["take"] = mm("take", [P, 1], U32)
        moe["give"] = mm("give", [P, 1], U32)
        assert mm.at <= end, (mm.at, end)

        raw_loaded = [ctx.enter_context(nc.semaphore(f"raw_loaded{i}")) for i in range(RING)]
        o_stored = ctx.enter_context(nc.semaphore("o_stored"))
        wo_loaded = ctx.enter_context(nc.semaphore("wo_loaded"))

        for s in range(SETS):
            project(nc, s, a, x_dram, k, temps, w, pj, q_rows, kv_rows, w_raw, uq_raw, ukv_raw, ps, banks, o_stored)
            attend(nc, s, a, k, att, wo, pj, q_rows, kv_rows, ps, banks, o_rows, o_stored, wo_loaded)
        route(nc, a, x_dram, k, wo, moe, ps, banks, o_rows, out_rows, h2_rows, raw_loaded, o_stored)
        experts(nc, a, k, moe, ps, banks, out, h2_dram, raw_loaded)


def project(nc, s, a, x_dram, k, tp, w, pj, q_rows, kv_rows, w_raw, uq_raw, ukv_raw, ps, banks, o_stored):
    first = s == 0
    x, xhi, xlo, chi, clo, sq, ra, small = (tp[n] for n in ("x", "xhi", "xlo", "chi", "clo", "sq", "ra", "small"))
    ssx, rx = small[:, 0:TS], small[:, TS:2 * TS]
    ssa, rsa = small[:, 8:8 + STATS], small[:, 24:24 + STATS]
    ssk, rsk = small[:, 40:40 + MH], small[:, 48:48 + MH]
    ssb, rsb = small[:, 56:56 + 2 * MH], small[:, 72:72 + 2 * MH]
    xt_ps = [banks(0, 1), banks(1, 1)]
    pj_ps, c_ps, u_ps = banks(2, 3)[:, 0:D_IN], banks(5, 1)[:, 0:3 * P], banks(6, 2)
    chunks = [(0, 512), (512, 1024), (1024, D_IN)]
    half = UQ // 2

    with Phase(nc, s) as phase:
        sem = phase.sem
        x_loaded = [sem("x_loaded0"), sem("x_loaded1")]
        gains_loaded, const_loaded, tables_loaded = sem("gains_loaded"), sem("const_loaded"), sem("tables_loaded")
        w_loaded, u_loaded = [sem(f"w_loaded{i}") for i in range(KD if first else 0)], sem("u_loaded")
        ident_ready, rows_set, gt_ready, gcol_ready = sem("ident_ready"), sem("rows_set"), sem("gt_ready"), sem("gcol_ready")
        whi_done, wlo_done = sem("whi_done"), sem("wlo_done")
        ssx_done, rx_done = sem("ssx_done"), sem("rx_done")
        xt_ready, xhi_done, xlo_done = sem("xt_ready"), sem("xhi_done"), sem("xlo_done")
        proj_done, pj_done, c_normed = sem("proj_done"), sem("pj_done"), sem("c_normed")
        ct_ready, chi_done, clo_done = sem("ct_ready"), sem("chi_done"), sem("clo_done")
        uq_done, q_copied = sem("uq_done"), sem("q_copied")
        ukv_done, kn_done, v_done = sem("ukv_done"), sem("kn_done"), sem("v_done")
        stat_a, stat_k, stat_b = sem("stat_a"), sem("stat_k"), sem("stat_b")
        ra_done, rk_done, rb_done = sem("ra_done"), sem("rk_done"), sem("rb_done")
        vsteps, psteps = sem("vector_steps"), sem("pool_steps")
        with nc.Block() as block:

            @block.sync
            def _(sp):
                sp.dma_start(x[0][:], x_dram[TS * s]).then_inc(x_loaded[0], 16)
                if first:
                    sp.wait_ge(rows_set, 1)
                    for row, name, n in ((G_ATTN, "norm_attn", D), (G_QA, "mla_q_a_norm", Q_LORA),
                                         (G_KVA, "mla_kv_a_norm", KV_LORA), (G_OUT, "out_norm_a", C_K),
                                         (G_OUT + C_K // P, "out_norm_b", MH * VD)):
                        sp.dma_start(tp["grow"][row:row + n // P, :], a[name].rearrange("(r c) -> r c", c=P)).then_inc(gains_loaded, 16)
                    for row, name in ((G_QN, "mla_q_nope_norm"), (G_KN, "mla_k_nope_norm")):
                        sp.dma_start(tp["grow"][row:row + 1, 0:NOPE], a[name].rearrange("(r c) -> r c", r=1)).then_inc(gains_loaded, 16)
                    for i in range(KD):
                        sp.dma_start(w_raw[:, i, :], a["w_in"][i * P:(i + 1) * P, :]).then_inc(w_loaded[i], 16)
                    sp.dma_start(uq_raw[:], a["mla_w_uq"].rearrange("(k p) n -> p k n", p=P)).then_inc(u_loaded, 16)
                    sp.dma_start(ukv_raw[:], a["mla_w_ukv"]).then_inc(u_loaded, 16)
                for t in range(1, TS):
                    if t >= 2:
                        sp.wait_ge(xt_ready, 2 * (t - 1))
                        sp.wait_ge(ssx_done, t - 1)
                    sp.dma_start(x[t % 2][:], x_dram[TS * s + t]).then_inc(x_loaded[t % 2], 16)

            @block.gpsimd
            def _(pool):
                steps = Steps(pool, psteps)
                if first:
                    pool.memset(tp["grow"][:], 1.0).then_inc(rows_set, 1)
                    pool.dma_start(k["invn"][:], a["invn"]).then_inc(const_loaded, 16)
                    pool.dma_start(k["tab"][:], a["tab"].rearrange("(i p) c -> p i c", p=P)).then_inc(tables_loaded, 16)
                    at = 0
                    for name, n in (("gqa_q_norm", HD), ("gqa_k_norm", HD), ("mla_q_pe_norm", PE_D), ("mla_k_pe_norm", PE_D)):
                        pool.dma_start(tp["gb"][:, at:at + n], a[name].partition_broadcast(P)).then_inc(tables_loaded, 16)
                        at += n
                    steps.did(pool.memset(k["minus_half"][:], -0.5))
                    steps.did(pool.memset(k["ident"][:], 0.0))
                    steps.wait()
                    pool.affine_select(out=k["ident"][:], in_=k["ident"][:], compare_op=ALU.not_equal, fill=1.0,
                                       base=0, pattern=[[-1, P]], channel_multiplier=1).then_inc(ident_ready, 1)
                    pool.wait_ge(const_loaded, 16)

                def inverse_root(dst, src, done):
                    steps.did(pool.tensor_scalar(src, src, 1.0, EPS, ALU.mult, ALU.add))
                    steps.wait()
                    pool.tensor_tensor(dst, src, k["minus_half"][:, 0:src.shape[1]], ALU.pow).then_inc(done, 1)

                def mean(src, at):
                    steps.did(pool.tensor_tensor(src, src, k["invn"][:, at:at + src.shape[1]], ALU.mult))
                    steps.wait()

                def x_norm(t):
                    pool.wait_ge(ssx_done, t + 1)
                    steps.did(pool.tensor_scalar(ssx[:, t:t + 1], ssx[:, t:t + 1], 1.0 / D, EPS, ALU.mult, ALU.add))
                    steps.wait()
                    pool.tensor_tensor(rx[:, t:t + 1], ssx[:, t:t + 1], k["minus_half"][:, 0:1], ALU.pow).then_inc(rx_done, 1)

                x_norm(0)
                x_norm(1)
                for t in range(TS + 2):
                    if t >= 2:
                        pool.wait_ge(stat_k, t - 1)
                        mean(ssk, 0)
                        inverse_root(rsk, ssk, rk_done)
                        pool.wait_ge(stat_b, t - 1)
                        mean(ssb, STATS)
                        inverse_root(rsb, ssb, rb_done)
                    if t < TS:
                        pool.wait_ge(stat_a, t + 1)
                        mean(ssa, 0)
                        inverse_root(rsa, ssa, ra_done)
                    if t + 2 < TS:
                        x_norm(t + 2)

            @block.tensor
            def _(pe):
                if first:
                    pe.wait_ge(ident_ready, 1)
                    pe.wait_ge(gains_loaded, 7 * 16)
                    pe.transpose(ps[:, 5, 0:G_ROWS], tp["grow"][:], k["ident"][0:G_ROWS, 0:G_ROWS]).then_inc(gt_ready, 1)

                def x_transposes(t):
                    pe.wait_ge(x_loaded[t % 2], 16 * (t // 2 + 1))
                    if t:
                        pe.wait_ge(xlo_done, 2 * t)
                    for b in range(2):
                        for i in range(4):
                            c = 4 * b + i
                            last = pe.transpose(xt_ps[b][:, i * P:(i + 1) * P], x[t % 2][:, c * P:(c + 1) * P], k["ident"][:])
                        last.then_inc(xt_ready, 1)

                x_transposes(0)
                x_transposes(1)
                for t in range(TS + 2):
                    if t >= 2:
                        u = t - 2
                        pe.wait_ge(q_copied, u + 1)
                        if first and u == 0:
                            pe.wait_ge(wlo_done, KD + 3)
                        for n in range(2):
                            cols = slice(n * BANK, (n + 1) * BANK)
                            pe.matmul(u_ps[:, cols], chi[:, 2, :], w["ukvhi"][:, cols], start=True, stop=False)
                            pe.matmul(u_ps[:, cols], chi[:, 2, :], w["ukvlo"][:, cols], start=False, stop=False)
                            last = pe.matmul(u_ps[:, cols], clo[:, 2, :], w["ukvhi"][:, cols], start=False, stop=True)
                        last.then_inc(ukv_done, 1)
                    if t < TS:
                        if t:
                            pe.wait_ge(pj_done, 2 * t)
                        for c in range(KD):
                            pe.wait_ge(xlo_done, 2 * t + c // 4 + 1)
                            if first and t == 0:
                                pe.wait_ge(wlo_done, c + 1)
                            for lhs, rhs in ((xhi[t % 2], "whi"), (xhi[t % 2], "wlo"), (xlo[t % 2], "whi")):
                                for lo, up in chunks:
                                    last = pe.matmul(pj_ps[:, lo:up], lhs[:, c, :], w[rhs][:, c, lo:up],
                                                     start=(c == 0 and rhs == "whi" and lhs is xhi[t % 2]),
                                                     stop=(c == KD - 1 and lhs is xlo[t % 2]))
                        last.then_inc(proj_done, 1)
                    if 1 <= t <= TS:
                        u = t - 1
                        pe.wait_ge(c_normed, u + 1)
                        if u == 0 and first:
                            pe.wait_ge(gcol_ready, 1)
                        if u:
                            pe.wait_ge(clo_done, u)
                        for i in range(3):
                            last = pe.transpose(c_ps[:, i * P:(i + 1) * P], pj[:, u, C_CQ + i * P:C_CQ + (i + 1) * P], k["ident"][:])
                        last.then_inc(ct_ready, 1)
                    if t + 2 < TS:
                        x_transposes(t + 2)
                    if 1 <= t <= TS:
                        pe.wait_ge(clo_done, u + 1)
                        if u:
                            pe.wait_ge(kn_done, u)
                            pe.wait_ge(v_done, u)
                        if first and u == 0:
                            pe.wait_ge(wlo_done, KD + 2)
                        for n in range(2):
                            dst = u_ps[:, n * BANK:n * BANK + half]
                            for i in range(2):
                                for lhs, rhs in ((chi, "uqhi"), (chi, "uqlo"), (clo, "uqhi")):
                                    last = pe.matmul(dst, lhs[:, i, :], w[rhs][:, i, n * half:(n + 1) * half],
                                                     start=(i == 0 and rhs == "uqhi" and lhs is chi), stop=(i == 1 and lhs is clo))
                        last.then_inc(uq_done, 1)

            @block.scalar
            def _(act):
                def split_weights():
                    act.wait_ge(gcol_ready, 2)
                    for i in range(KD):
                        act.wait_ge(w_loaded[i], 16)
                        act.activation(w["whi"][:, i, :], w_raw[:, i, :], ACT.Copy,
                                       scale=k["gcol"][:, G_ATTN + i:G_ATTN + i + 1]).then_inc(whi_done, 1)
                    act.wait_ge(u_loaded, 32)
                    for i in range(2):
                        act.activation(w["uqhi"][:, i, :], uq_raw[:, i, :], ACT.Copy,
                                       scale=k["gcol"][:, G_QA + i:G_QA + i + 1]).then_inc(whi_done, 1)
                    act.activation(w["ukvhi"][:], ukv_raw[:], ACT.Copy, scale=k["gcol"][:, G_KVA:G_KVA + 1]).then_inc(whi_done, 1)

                def x_high(t):
                    act.wait_ge(x_loaded[t % 2], 16 * (t // 2 + 1))
                    for b in range(2):
                        act.wait_ge(xt_ready, 2 * t + b + 1)
                        if t >= 2 and b == 0:
                            act.wait_ge(proj_done, t - 1)
                        act.activation(xhi[t % 2][:, 4 * b:4 * b + 4, :], xt_ps[b].rearrange("p (a c) -> p a c", a=4),
                                       ACT.Copy).then_inc(xhi_done, 1)
                    if t:
                        act.wait_ge(ssx_done, t)
                    if t >= 2:
                        act.wait_ge(stat_a, t - 1)
                        act.wait_ge(pj_done, 2 * (t - 1))
                    act.activation(sq[:, 0:D], x[t % 2][:], ACT.Square, accum_out=ssx[:, t:t + 1]).then_inc(ssx_done, 1)

                x_high(0)
                if first:
                    split_weights()
                x_high(1)
                for t in range(TS + 2):
                    if t >= 2:
                        u = t - 2
                        act.wait_ge(ukv_done, u + 1)
                        nope = u_ps.rearrange("p (h c) -> p h c", h=MH)[:, :, 0:NOPE]
                        act.activation(kv_rows[:, u, :, 0:NOPE], nope, ACT.Copy).then_inc(kn_done, 1)
                    if 1 <= t <= TS:
                        u = t - 1
                        act.wait_ge(ct_ready, u + 1)
                        if u:
                            act.wait_ge(ukv_done, u)
                        act.activation(chi[:], c_ps.rearrange("p (a c) -> p a c", a=3), ACT.Copy).then_inc(chi_done, 1)
                    if t < TS:
                        act.wait_ge(proj_done, t + 1)
                        act.wait_ge(rx_done, t + 1)
                        act.wait_ge(ssx_done, min(t + 2, TS))
                        if t:
                            act.wait_ge(stat_a, t)
                        if t == 0:
                            if first:
                                act.wait_ge(wlo_done, KD + 3)
                            else:
                                act.wait_ge(o_stored, 16 * s)
                        act.activation(pj[:, t, :], pj_ps, ACT.Copy, scale=rx[:, t:t + 1]).then_inc(pj_done, 1)
                        act.activation(sq[:], pj_ps, ACT.Square, scale=rx[:, t:t + 1]).then_inc(pj_done, 1)
                    if t + 2 < TS:
                        x_high(t + 2)
                    if 1 <= t <= TS:
                        u = t - 1
                        act.wait_ge(uq_done, u + 1)
                        act.activation(q_rows[:, u].rearrange("p (n h) c -> p n (h c)", n=2),
                                       ps[:, 6:8, 0:half], ACT.Copy).then_inc(q_copied, 1)

            @block.vector
            def _(dve):
                steps = Steps(dve, vsteps)

                def broadcast(col, n, m):
                    return col.unsqueeze(2).to_broadcast([P, n, m])

                def rotate(rows_ap, heads, rot, tab_ap, tmp):
                    v = rows_ap.rearrange("p h (a b q) -> p h a b q", a=2, b=2)
                    tv = tmp.rearrange("p (h a b q) -> p h a b q", h=heads, a=2, b=2)
                    sin = tab_ap[:, 1, :].rearrange("p (a b q) -> p a b q", a=2, b=2)
                    for b in range(2):
                        for i in range(2):
                            steps.did(dve.tensor_tensor(tv[:, :, i, b, :], v[:, :, i, 1 - b, :],
                                                        sin[:, i, b, :].unsqueeze(1).to_broadcast([P, heads, rot // 4]), ALU.mult))
                    steps.wait()
                    steps.did(dve.tensor_tensor(rows_ap, rows_ap, tab_ap[:, 0, :].unsqueeze(1).to_broadcast([P, heads, rot]), ALU.mult))
                    steps.wait()
                    return dve.tensor_tensor(rows_ap, rows_ap, tmp.rearrange("p (h c) -> p h c", h=heads), ALU.add)

                def split_weights():
                    for i in range(KD):
                        dve.wait_ge(whi_done, i + 1)
                        dve.scalar_tensor_tensor(out=w["wlo"][:, i, :], in0=w_raw[:, i, :], scalar=k["gcol"][:, G_ATTN + i:G_ATTN + i + 1],
                                                 in1=w["whi"][:, i, :].bitcast(F32), op0=ALU.mult, op1=ALU.subtract).then_inc(wlo_done, 1)
                    for i in range(2):
                        dve.wait_ge(whi_done, KD + 1 + i)
                        dve.scalar_tensor_tensor(out=w["uqlo"][:, i, :], in0=uq_raw[:, i, :], scalar=k["gcol"][:, G_QA + i:G_QA + i + 1],
                                                 in1=w["uqhi"][:, i, :].bitcast(F32), op0=ALU.mult, op1=ALU.subtract).then_inc(wlo_done, 1)
                    dve.wait_ge(whi_done, KD + 3)
                    dve.scalar_tensor_tensor(out=w["ukvlo"][:], in0=ukv_raw[:], scalar=k["gcol"][:, G_KVA:G_KVA + 1],
                                             in1=w["ukvhi"][:].bitcast(F32), op0=ALU.mult, op1=ALU.subtract).then_inc(wlo_done, 1)

                def tables():
                    dve.wait_ge(tables_loaded, 5 * 16)
                    at = 0
                    for name, rot, c0 in (("gq", HD, 0), ("gk", HD, 0), ("gqp", PE_D, 2 * HD), ("gkp", PE_D, 2 * HD)):
                        g = tp["gb"][:, at:at + rot]
                        gv = g.rearrange("p (a b q) -> p a b q", a=2, b=2)
                        at += rot
                        cos, sin = k["tab"][:, :, c0:c0 + rot], k["tab"][:, :, c0 + rot:c0 + 2 * rot]
                        steps.did(dve.tensor_tensor(k[name][:, :, 0, :], cos, g.unsqueeze(1).to_broadcast([P, TS, rot]), ALU.mult))
                        sv = sin.rearrange("p i (a b q) -> p i a b q", a=2, b=2)
                        ov = k[name][:, :, 1, :].rearrange("p i (a b q) -> p i a b q", a=2, b=2)
                        for i in range(2):
                            for b in range(2):
                                steps.did(dve.tensor_tensor(ov[:, :, i, b, :], sv[:, :, i, b, :],
                                                            gv[:, i, 1 - b, :].unsqueeze(1).to_broadcast([P, TS, rot // 4]), ALU.mult))
                    steps.wait()

                if first:
                    dve.wait_ge(gt_ready, 1)
                    dve.tensor_copy(k["gcol"][:], ps[:, 5, 0:G_ROWS]).then_inc(gcol_ready, 1)
                    dve.wait_ge(gcol_ready, 1)
                    dve.tensor_scalar(k["gcol"][:, G_QN:G_QN + 1], k["gcol"][:, G_QN:G_QN + 1], float(QK) ** -0.5, None,
                                      ALU.mult).then_inc(gcol_ready, 1)

                def x_low(t):
                    for b in range(2):
                        dve.wait_ge(xhi_done, 2 * t + b + 1)
                        cols = slice(4 * b, 4 * b + 4)
                        dve.tensor_tensor(xlo[t % 2][:, cols, :], xt_ps[b].rearrange("p (a c) -> p a c", a=4),
                                          xhi[t % 2][:, cols, :].bitcast(F32), ALU.subtract).then_inc(xlo_done, 1)

                x_low(0)
                if first:
                    split_weights()
                    tables()
                x_low(1)
                for t in range(TS + 2):
                    if t >= 2:
                        u = t - 2
                        dve.wait_ge(ukv_done, u + 1)
                        dve.wait_ge(kn_done, u + 1)
                        value = u_ps.rearrange("p (h c) -> p h c", h=MH)[:, :, NOPE:NOPE + VD]
                        dve.tensor_copy(kv_rows[:, u, :, QK:KB], value).then_inc(v_done, 1)
                        kn = kv_rows[:, u, :, 0:NOPE]
                        tmp = ra[:, 0:MH * NOPE].rearrange("p (h c) -> p h c", h=MH)
                        steps.wait()
                        steps.did(dve.tensor_tensor(tmp, kn, kn, ALU.mult))
                        steps.wait()
                        dve.tensor_reduce(ssk, tmp, AX.X, ALU.add).then_inc(stat_k, 1)
                        steps.did(dve.tensor_copy(kv_rows[:, u, :, NOPE:QK],
                                                  pj[:, u, C_KPE:D_IN].unsqueeze(1).to_broadcast([P, MH, PE_D])))
                        dve.wait_ge(q_copied, u + 1)
                        q = q_rows[:, u]
                        dve.wait_ge(stat_k, u + 1)
                        steps.did(dve.tensor_tensor(tmp, q[:, :, 0:NOPE], q[:, :, 0:NOPE], ALU.mult))
                        steps.wait()
                        steps.did(dve.tensor_reduce(ssb[:, 0:MH], tmp, AX.X, ALU.add))
                        steps.wait()
                        tmp2 = ra[:, 0:MH * PE_D].rearrange("p (h c) -> p h c", h=MH)
                        steps.did(dve.tensor_tensor(tmp2, q[:, :, NOPE:QK], q[:, :, NOPE:QK], ALU.mult))
                        steps.wait()
                        dve.tensor_reduce(ssb[:, MH:2 * MH], tmp2, AX.X, ALU.add).then_inc(stat_b, 1)
                    if 1 <= t <= TS:
                        u = t - 1
                        dve.wait_ge(chi_done, u + 1)
                        dve.tensor_tensor(clo[:], c_ps.rearrange("p (a c) -> p a c", a=3), chi[:].bitcast(F32),
                                          ALU.subtract).then_inc(clo_done, 1)
                    if t < TS:
                        row = pj[:, t, :]
                        dve.wait_ge(pj_done, 2 * t + 2)
                        heads = QH + KVH
                        steps.did(dve.tensor_reduce(ssa[:, heads:heads + 1], sq[:, C_CQ:C_CKV], AX.X, ALU.add))
                        steps.did(dve.tensor_reduce(ssa[:, heads + 1:heads + 2], sq[:, C_CKV:C_KPE], AX.X, ALU.add))
                        steps.did(dve.tensor_reduce(ssa[:, heads + 2:heads + 3], sq[:, C_KPE:D_IN], AX.X, ALU.add))
                        dve.tensor_reduce(ssa[:, 0:heads], sq[:, 0:C_V].rearrange("p (h c) -> p h c", h=heads),
                                          AX.X, ALU.add).then_inc(stat_a, 1)
                        if t + 2 < TS:
                            x_low(t + 2)
                        dve.wait_ge(ra_done, t + 1)
                        steps.did(dve.tensor_scalar(row[:, C_CKV:C_KPE], row[:, C_CKV:C_KPE], rsa[:, heads + 1:heads + 2], None, ALU.mult))
                        dve.tensor_scalar(row[:, C_CQ:C_CKV], row[:, C_CQ:C_CKV], rsa[:, heads:heads + 1], None, ALU.mult).then_inc(c_normed, 1)
                        steps.did(dve.tensor_scalar(row[:, C_KPE:D_IN], row[:, C_KPE:D_IN], rsa[:, heads + 2:heads + 3], None, ALU.mult))
                        qk = row[:, 0:C_V].rearrange("p (h c) -> p h c", h=heads)
                        steps.did(dve.tensor_tensor(qk, qk, broadcast(rsa[:, 0:heads], heads, HD), ALU.mult))
                        steps.wait()
                        kpe = row[:, C_KPE:D_IN].rearrange("p (h c) -> p h c", h=1)
                        steps.did(rotate(kpe, 1, PE_D, k["gkp"][:, t], ra[:, 0:PE_D]))
                        steps.wait()
                        steps.did(rotate(qk[:, 0:QH], QH, HD, k["gq"][:, t], ra[:, 0:C_K]))
                        steps.did(rotate(qk[:, QH:], KVH, HD, k["gk"][:, t], ra[:, C_K:C_V]))
                        steps.wait()
                    if t >= 2:
                        u = t - 2
                        kn, q = kv_rows[:, u, :, 0:NOPE], q_rows[:, u]
                        dve.wait_ge(stat_b, u + 1)
                        dve.wait_ge(rk_done, u + 1)
                        steps.did(dve.tensor_tensor(kn, kn, broadcast(rsk, MH, NOPE), ALU.mult))
                        dve.wait_ge(rb_done, u + 1)
                        steps.did(dve.tensor_tensor(q[:, :, 0:NOPE], q[:, :, 0:NOPE], broadcast(rsb[:, 0:MH], MH, NOPE), ALU.mult))
                        steps.did(dve.tensor_tensor(q[:, :, NOPE:QK], q[:, :, NOPE:QK], broadcast(rsb[:, MH:2 * MH], MH, PE_D), ALU.mult))
                        steps.wait()
                        steps.did(rotate(q[:, :, NOPE:QK], MH, PE_D, k["gqp"][:, u], ra[:, 0:MH * PE_D]))
                        steps.wait()


def attend(nc, s, a, k, att, wo, pj, q_rows, kv_rows, ps, banks, o_rows, o_stored, wo_loaded):
    last_set = s == SETS - 1
    STEPS = 7
    units = [(h, i) for h in range(HEADS) for i in range(TS)]
    NU = len(units)
    qhi, khi = att["hi"]
    qlo, klo = att["lo"]
    preps, key_of = [], {}
    for h in range(HEADS):
        if h >= QH or h % GROUP == 0:
            preps.append(("k", h))
        key_of[h] = sum(1 for kind, _ in preps if kind == "k") - 1
        preps.append(("q", h))
    prep_index = {p: n for n, p in enumerate(preps)}
    due = {}
    for kind, h in preps:
        due.setdefault(max(0, TS * (h - 1) + (0 if kind == "k" else 2)) if h else -1, []).append((kind, h))
    S_BANKS, T_BANKS, OT_BANK, O_BANK, PREP = (0, 1, 2), (3, 4), 5, 6, 7
    PAIRS = NU // 2
    pthi, ptlo, ot, otv = (att[n] for n in ("pthi", "ptlo", "ot", "otv"))

    with Phase(nc, s) as phase:
        sem = phase.sem
        prep_ready, prep_hi, prep_lo = sem("prep_ready"), sem("prep_hi"), sem("prep_lo")
        score_ready, max_done, exp_done = sem("score_ready"), sem("max_done"), sem("exp_done")
        pt_ready, pthi_done, ptlo_done, pv_done = sem("pt_ready"), sem("pthi_done"), sem("ptlo_done"), sem("pv_done")
        vhi_done, vlo_done, ot_copied, o_ready, ot_added = sem("vhi_done"), sem("vlo_done"), sem("ot_copied"), sem("o_ready"), sem("ot_added")
        rsum_done, o_done = sem("rsum_done"), sem("o_done")
        wo_hi, wo_lo = sem("wo_hi"), sem("wo_lo")
        with nc.Block() as block:

            def value_of(h):
                if h < QH:
                    c = C_V + h // GROUP * HD
                    return pj[:, :, c:c + HD]
                return kv_rows[:, :, h - QH, QK:KB]

            def pair_cols(u):
                return slice(u % 2 * P, (u % 2 + 1) * P)

            @block.sync
            def _(sp):
                if last_set:
                    for i in range(KD // 2):
                        sp.dma_start(wo["raw"][:, 2 * i:2 * i + 2, :],
                                     a["w_o"].rearrange("(k p) n -> p k n", p=P)[:, 2 * i:2 * i + 2, :]).then_inc(wo_loaded, 16)
                sp.wait_ge(o_done, HEADS)
                sp.dma_start(o_rows[TS * s:TS * (s + 1)].rearrange("t p d -> p t d"), pj[:, :, 0:D]).then_inc(o_stored, 16)

            @block.tensor
            def _(pe):
                def prepare(kind, h):
                    n = prep_index[kind, h]
                    if n:
                        pe.wait_ge(prep_lo, n)
                    for i in range(TS):
                        if h < QH:
                            c = h * HD if kind == "q" else C_K + h // GROUP * HD
                            src, dst = pj[:, i, c:c + HD], ps[0:HD, PREP, i * P:(i + 1) * P]
                        else:
                            src = q_rows[:, i, h - QH, :] if kind == "q" else kv_rows[:, i, h - QH, 0:QK]
                            dst = ps[0:QK, PREP, i * P:(i + 1) * P]
                        last = pe.transpose(dst, src, k["ident"][:])
                    last.then_inc(prep_ready, 1)

                def scores(u):
                    h, i = units[u]
                    if i == 0:
                        pe.wait_ge(prep_lo, prep_index["q", h] + 1)
                    if u >= 3:
                        pe.wait_ge(exp_done, u - 2)
                    dst, q, kk, cols = ps[:, S_BANKS[u % 3], :], h % 2, key_of[h] % 2, slice(i * P, (i + 1) * P)
                    if h < QH:
                        pe.matmul(dst, qhi[q][:, cols], khi[kk][:], start=True, stop=False)
                        last = pe.matmul(dst, qhi[q][:, cols], klo[kk][:], start=False, stop=True)
                    else:
                        pe.matmul(dst, qhi[q][0:QK, cols], khi[kk][0:QK, :], start=True, stop=False)
                        pe.matmul(dst, qhi[q][0:QK, cols], klo[kk][0:QK, :], start=False, stop=False)
                        last = pe.matmul(dst, qlo[q][0:QK, cols], khi[kk][0:QK, :], start=False, stop=True)
                    last.then_inc(score_ready, 1)

                def transpose_probs(u):
                    pe.wait_ge(exp_done, u + 1)
                    if u >= 2:
                        pe.wait_ge(ptlo_done, u - 1)
                    for i in range(TS):
                        cols = slice(i * P, (i + 1) * P)
                        last = pe.transpose(ps[:, T_BANKS[u % 2], cols], att["p"][u % 2][:, cols], k["ident"][:])
                    last.then_inc(pt_ready, 1)

                def values(m):
                    h, qi = units[2 * m]
                    pe.wait_ge(ptlo_done, 2 * m + 2)
                    if qi == 0:
                        pe.wait_ge(vlo_done, key_of[h] + 1)
                        if h:
                            pe.wait_ge(ot_added, h)
                    v = att["v"][key_of[h] % 2]
                    cols = slice(qi * P, (qi + 2) * P)
                    for part, i in [("hi", 0)] + [("lo", i) for i in range(TS)] + [("hi", i) for i in range(1, TS)]:
                        if part == "hi":
                            last = pe.matmul(ps[:, OT_BANK, cols], v[:, i].rearrange("p a c -> p (a c)"), pthi[m % 2][:, i, :],
                                             start=(i == 0), stop=(i == TS - 1))
                        else:
                            pe.matmul(ps[0:VD, OT_BANK, cols], v[:, i, 0, :], ptlo[m % 2][:, i, :], start=False, stop=False)
                    last.then_inc(pv_done, 1)

                def transpose_output(h):
                    pe.wait_ge(ot_added, h + 1)
                    if h:
                        pe.wait_ge(o_done, h)
                    for i in range(TS):
                        last = pe.transpose(ps[:, O_BANK, i * VD:(i + 1) * VD], ot[:, i * P:(i + 1) * P], k["ident"][0:VD, 0:VD])
                    last.then_inc(o_ready, 1)

                for kind, h in due.get(-1, []):
                    prepare(kind, h)
                for u in range(NU + STEPS):
                    for kind, h in due.get(u, []):
                        prepare(kind, h)
                    if u < NU:
                        scores(u)
                    if 0 <= u - 2 < NU:
                        transpose_probs(u - 2)
                    if u >= 9 and (u - 9) % TS == 0:
                        transpose_output((u - 9) // TS)
                    if u >= 5 and u % 2 == 1 and (u - 5) // 2 < PAIRS:
                        values((u - 5) // 2)

            @block.scalar
            def _(act):
                def prepare(kind, h):
                    n = prep_index[kind, h]
                    act.wait_ge(prep_ready, n + 1)
                    if kind == "q":
                        dst = qhi[h % 2]
                        if h >= 2:
                            act.wait_ge(score_ready, TS * (h - 1))
                    else:
                        dst = khi[key_of[h] % 2]
                        if key_of[h] >= 2:
                            act.wait_ge(score_ready, TS * (h - 1))
                    src = ps[:, PREP, :]
                    if h < QH and kind == "q":
                        act.activation(dst[0:HD, :], src[0:HD, :], ACT.Copy, scale=float(HD) ** -0.5).then_inc(prep_hi, 1)
                    elif h < QH:
                        act.activation(dst[0:HD, :], src[0:HD, :], ACT.Copy)
                        act.activation(dst[HD:P, :], src[0:HD, :], ACT.Copy).then_inc(prep_hi, 1)
                    else:
                        g = G_QN if kind == "q" else G_KN
                        act.activation(dst[0:QK, :], src[0:QK, :], ACT.Copy, scale=k["gcol"][0:QK, g:g + 1]).then_inc(prep_hi, 1)

                def split_values(h):
                    if key_of[h] >= 2:
                        act.wait_ge(pv_done, TS // 2 * (h - 1))
                    act.activation(att["v"][key_of[h] % 2][:, :, 0, :], value_of(h), ACT.Copy).then_inc(vhi_done, 1)

                for kind, h in due.get(-1, []):
                    prepare(kind, h)
                for u in range(NU + STEPS):
                    if u >= 8 and (u - 8) % TS == 0:
                        h = (u - 8) // TS
                        act.wait_ge(pv_done, TS // 2 * (h + 1))
                        if h:
                            act.wait_ge(ot_added, h)
                        act.activation(otv[:], ps[VD:P, OT_BANK, :], ACT.Copy).then_inc(ot_copied, 1)
                    if 0 <= u - 2 < NU:
                        v = u - 2
                        act.wait_ge(pt_ready, v + 1)
                        if v >= 4:
                            act.wait_ge(pv_done, v // 2 - 1)
                        act.activation(pthi[v // 2 % 2][:, :, pair_cols(v)],
                                       ps[:, T_BANKS[v % 2], :].rearrange("p (a c) -> p a c", a=TS), ACT.Copy).then_inc(pthi_done, 1)
                    if u < NU:
                        act.wait_ge(max_done, u + 1)
                        if u >= 2:
                            act.wait_ge(pt_ready, u - 1)
                        act.activation(att["p"][u % 2][:], ps[:, S_BANKS[u % 3], :], ACT.Exp, bias=att["nmax"][:, u:u + 1],
                                       accum_out=att["sum"][:, u:u + 1]).then_inc(exp_done, 1)
                    if u % TS == 0 and u < NU and key_of[u // TS] != (key_of[u // TS - 1] if u else -1):
                        split_values(u // TS)
                    for kind, h in due.get(u, []):
                        prepare(kind, h)
                    if last_set and u % 8 == 5 and u // 8 < KD:
                        i = u // 8
                        act.wait_ge(wo_loaded, 16 * (KD // 2))
                        act.activation(wo["hi"][:, i, :], wo["raw"][:, i, :], ACT.Copy,
                                       scale=k["gcol"][:, G_OUT + i:G_OUT + i + 1]).then_inc(wo_hi, 1)

            @block.vector
            def _(dve):
                def prepare(kind, h):
                    n = prep_index[kind, h]
                    dve.wait_ge(prep_hi, n + 1)
                    src = ps[:, PREP, :]
                    if h < QH and kind == "q":
                        dst = qhi[h % 2]
                        dve.scalar_tensor_tensor(out=dst[HD:P, :], in0=src[0:HD, :], scalar=float(HD) ** -0.5,
                                                 in1=dst[0:HD, :].bitcast(F32), op0=ALU.mult, op1=ALU.subtract).then_inc(prep_lo, 1)
                    elif h < QH:
                        kk = key_of[h] % 2
                        for rows in (slice(0, HD), slice(HD, P)):
                            last = dve.tensor_tensor(klo[kk][rows, :], src[0:HD, :], khi[kk][rows, :].bitcast(F32), ALU.subtract)
                        last.then_inc(prep_lo, 1)
                    else:
                        hi, lo = (qhi[h % 2], qlo[h % 2]) if kind == "q" else (khi[key_of[h] % 2], klo[key_of[h] % 2])
                        g = G_QN if kind == "q" else G_KN
                        dve.scalar_tensor_tensor(out=lo[0:QK, :], in0=src[0:QK, :], scalar=k["gcol"][0:QK, g:g + 1],
                                                 in1=hi[0:QK, :].bitcast(F32), op0=ALU.mult, op1=ALU.subtract).then_inc(prep_lo, 1)

                for kind, h in due.get(-1, []):
                    prepare(kind, h)
                for u in range(NU + STEPS):
                    if u < NU:
                        dve.wait_ge(score_ready, u + 1)
                        dve.tensor_reduce(att["nmax"][:, u:u + 1], ps[:, S_BANKS[u % 3], :], AX.X, ALU.max,
                                          negate=True).then_inc(max_done, 1)
                    if u >= 8 and (u - 8) % TS == 0:
                        h = (u - 8) // TS
                        dve.wait_ge(ot_copied, h + 1)
                        if h:
                            dve.wait_ge(o_ready, h)
                        dve.tensor_tensor(ot[:], ps[0:VD, OT_BANK, :], otv[:], ALU.add).then_inc(ot_added, 1)
                    if 0 <= u - 3 < NU:
                        v = u - 3
                        dve.wait_ge(pthi_done, v + 1)
                        cols = pair_cols(v)
                        dve.tensor_tensor(ptlo[v // 2 % 2][:, :, cols], ps[:, T_BANKS[v % 2], :].rearrange("p (a c) -> p a c", a=TS),
                                          pthi[v // 2 % 2][:, :, cols].bitcast(F32), ALU.subtract).then_inc(ptlo_done, 1)
                    if u % TS == 0 and u < NU and key_of[u // TS] != (key_of[u // TS - 1] if u else -1):
                        h = u // TS
                        v = att["v"][key_of[h] % 2]
                        dve.wait_ge(vhi_done, key_of[h] + 1)
                        dve.tensor_tensor(v[:, :, 1, :], value_of(h), v[:, :, 0, :].bitcast(F32), ALU.subtract).then_inc(vlo_done, 1)
                    for kind, h in due.get(u, []):
                        prepare(kind, h)
                    if last_set and u % 8 == 5 and u // 8 < KD:
                        i = u // 8
                        dve.wait_ge(wo_hi, i + 1)
                        dve.scalar_tensor_tensor(out=wo["lo"][:, i, :], in0=wo["raw"][:, i, :], scalar=k["gcol"][:, G_OUT + i:G_OUT + i + 1],
                                                 in1=wo["hi"][:, i, :].bitcast(F32), op0=ALU.mult, op1=ALU.subtract).then_inc(wo_lo, 1)
                    if u >= 9 and (u - 9) % TS == 0:
                        h = (u - 9) // TS
                        cols = slice(TS * h, TS * (h + 1))
                        dve.wait_ge(exp_done, TS * (h + 1))
                        dve.reciprocal(att["rsum"][:, cols], att["sum"][:, cols]).then_inc(rsum_done, 1)
                        dve.wait_ge(o_ready, h + 1)
                        dve.wait_ge(rsum_done, h + 1)
                        dve.tensor_tensor(pj[:, :, h * VD:(h + 1) * VD],
                                          ps[:, O_BANK, 0:TS * VD].rearrange("p (i c) -> p i c", i=TS),
                                          att["rsum"][:, cols].unsqueeze(2).to_broadcast([P, TS, VD]), ALU.mult).then_inc(o_done, 1)


def load_chunk(sp, a, moe, raw_loaded, e, j):
    slot = moe["raw"][j % RING]
    if j < 8:
        half, group, name = j // 4, j % 4 // 2, "w_gate" if j % 2 == 0 else "w_up"
        src = a[name][bass.ds(e, 1), group * CK * P:(group + 1) * CK * P, half * BANK:(half + 1) * BANK]
        src = src.rearrange("e (k p) n -> p (e k) n", p=P)
        dst = slot[:].rearrange("p (k n) -> p k n", k=CK)
    else:
        i = 2 * (j - 8)
        src = a["w_down"][bass.ds(e, 1), i * P:(i + 2) * P, :].rearrange("e (k p) n -> p (e k) n", p=P)
        dst = slot[:].rearrange("p (k n) -> p k n", k=2)
    sp.dma_start(dst, src).then_inc(raw_loaded[j % RING], 16)


def route(nc, a, x_dram, k, wo, moe, ps, banks, o_rows, out_rows, h2_rows, raw_loaded, o_stored):
    o, xr, h2, gffn, sq, wr, small = (wo[n] for n in ("o", "x", "h2", "gffn", "sq", "wr", "small"))
    othi, otlo, x1, h2T = (wo[n] for n in ("othi", "otlo", "x1", "h2T"))
    column = lambda at, t, n=1: small[:, at + n * t:at + n * t + n]
    sso, ro = (lambda t: column(0, t, 2)), (lambda t: column(16, t, 2))
    ss2, r2 = (lambda t: column(32, t)), (lambda t: column(40, t))
    lmax, lsum, lrec = (lambda t: column(48, t)), (lambda t: column(56, t)), (lambda t: column(64, t))
    aff = small[:, 72:72 + EXPERTS]
    OT, WO, HT, LG, AT = (0, 1), banks(2, 2), (4, 5), ps[:, 6, 0:EXPERTS], ps[0:EXPERTS, 7, 0:P]

    with Phase(nc, "m") as phase:
        sem = phase.sem
        o_loaded, xr_loaded = [sem(f"o_loaded{i}") for i in range(3)], [sem(f"xr_loaded{i}") for i in range(3)]
        small_loaded, x1_stored, h2_stored = sem("small_loaded"), [sem("x1_stored0"), sem("x1_stored1")], [sem("h2_stored0"), sem("h2_stored1")]
        sso_done, ro_done, on_done = sem("sso_done"), sem("ro_done"), sem("on_done")
        ot_ready, othi_done, otlo_done = sem("ot_ready"), sem("othi_done"), sem("otlo_done")
        wo_done, x1_done, ss2_done, r2_done, h2_done = sem("wo_done"), sem("x1_done"), sem("ss2_done"), sem("r2_done"), sem("h2_done")
        ht_ready, ht_copied, lg_ready = sem("ht_ready"), sem("ht_copied"), sem("lg_ready")
        lmax_done, lexp_done, lrec_done, aff_done = sem("lmax_done"), sem("lexp_done"), sem("lrec_done"), sem("aff_done")
        at_ready, at_done, psteps, vsteps = sem("at_ready"), sem("at_done"), sem("pool_steps_r"), sem("vector_steps_r")
        with nc.Block() as block:

            @block.sync
            def _(sp):
                sp.wait_ge(o_stored, 16 * SETS)
                sp.dma_start(gffn[:], a["norm_ffn"].partition_broadcast(P)).then_inc(small_loaded, 16)
                sp.dma_start(wr[:], a["w_router"].rearrange("(k p) e -> p k e", p=P)).then_inc(small_loaded, 16)
                for t in range(T):
                    if t >= 3:
                        sp.wait_ge(ot_ready, 2 * (t - 2))
                        sp.wait_ge(x1_done, 2 * (t - 2))
                    sp.dma_start(o[t % 3][:], o_rows[t]).then_inc(o_loaded[t % 3], 16)
                    sp.dma_start(xr[t % 3][:], x_dram[t]).then_inc(xr_loaded[t % 3], 16)
                    if t < RING:
                        load_chunk(sp, a, moe, raw_loaded, 0, t)

            @block.gpsimd
            def _(pool):
                steps = Steps(pool, psteps)

                def inverse_root(dst, src, n, done):
                    steps.did(pool.tensor_scalar(src, src, 1.0 / n, EPS, ALU.mult, ALU.add))
                    steps.wait()
                    pool.tensor_tensor(dst, src, k["minus_half"][:, 0:src.shape[1]], ALU.pow).then_inc(done, 1)

                def group_norm(t):
                    pool.wait_ge(sso_done, 2 * t + 2)
                    inverse_root(ro(t), sso(t), C_K, ro_done)

                group_norm(0)
                for t in range(T + 1):
                    if t + 1 < T:
                        group_norm(t + 1)
                    if t >= 1:
                        u = t - 1
                        pool.wait_ge(ss2_done, u + 1)
                        inverse_root(r2(u), ss2(u), D, r2_done)
                        pool.dma_start(out_rows[u], x1[u % 2][:]).then_inc(x1_stored[u % 2], 16)
                        pool.wait_ge(h2_done, u + 1)
                        pool.dma_start(h2_rows[u], h2[u % 2][:]).then_inc(h2_stored[u % 2], 16)
                for i in range(2):
                    pool.wait_ge(x1_stored[i], 16 * T // 2)
                    pool.wait_ge(h2_stored[i], 16 * T // 2)

            @block.tensor
            def _(pe):
                for t in range(T + 3):
                    if 1 <= t <= T:
                        u = t - 1
                        pe.wait_ge(otlo_done, 2 * u + 2)
                        if u:
                            pe.wait_ge(x1_done, 2 * u)
                        for c in range(KD):
                            for lhs, rhs in ((othi[u % 2], "hi"), (othi[u % 2], "lo"), (otlo[u % 2], "hi")):
                                for n in range(2):
                                    cols = slice(n * BANK, (n + 1) * BANK)
                                    last = pe.matmul(WO[:, cols], lhs[:, c, :], wo[rhs][:, c, cols],
                                                     start=(c == 0 and rhs == "hi" and lhs is othi[u % 2]),
                                                     stop=(c == KD - 1 and lhs is otlo[u % 2]))
                        last.then_inc(wo_done, 1)
                    if t < T:
                        pe.wait_ge(on_done, 2 * t + 2)
                        if t:
                            pe.wait_ge(otlo_done, 2 * t)
                        for b in range(2):
                            for i in range(4):
                                c = 4 * b + i
                                last = pe.transpose(ps[:, OT[b], i * P:(i + 1) * P], o[t % 3][:, c * P:(c + 1) * P], k["ident"][:])
                            last.then_inc(ot_ready, 1)
                    if t >= 3:
                        u = t - 3
                        pe.wait_ge(aff_done, u + 1)
                        if u:
                            pe.wait_ge(at_done, u)
                        pe.transpose(AT, aff, k["ident"][:]).then_inc(at_ready, 1)
                    if 2 <= t <= T + 1:
                        u = t - 2
                        pe.wait_ge(h2_done, u + 1)
                        if u:
                            pe.wait_ge(ht_copied, 2 * u)
                        for b in range(2):
                            for i in range(4):
                                c = 4 * b + i
                                last = pe.transpose(ps[:, HT[b], i * P:(i + 1) * P], h2[u % 2][:, c * P:(c + 1) * P], k["ident"][:])
                            last.then_inc(ht_ready, 1)
                        if u == 0:
                            pe.wait_ge(small_loaded, 32)
                        else:
                            pe.wait_ge(lexp_done, u)
                        for c in range(KD):
                            pe.wait_ge(ht_copied, 2 * u + c // 4 + 1)
                            last = pe.matmul(LG, h2T[:, c, :], wr[:, c, :], start=(c == 0), stop=(c == KD - 1))
                        last.then_inc(lg_ready, 1)

            @block.scalar
            def _(act):
                def squares(t):
                    act.wait_ge(o_loaded[t % 3], 16 * (t // 3 + 1))
                    if t:
                        act.wait_ge(sso_done, 2 * t)
                        if t >= 3:
                            act.wait_ge(ss2_done, t - 2)
                    for n in range(2):
                        cols = slice(n * C_K, (n + 1) * C_K)
                        act.activation(sq[:, cols], o[t % 3][:, cols], ACT.Square, accum_out=sso(t)[:, n:n + 1]).then_inc(sso_done, 1)

                squares(0)
                for t in range(T + 2):
                    if t + 1 < T:
                        squares(t + 1)
                    if t < T:
                        for b in range(2):
                            act.wait_ge(ot_ready, 2 * t + b + 1)
                            if t >= 2 and b == 0:
                                act.wait_ge(wo_done, t - 1)
                            act.activation(othi[t % 2][:, 4 * b:4 * b + 4, :], ps[:, OT[b], :].rearrange("p (a c) -> p a c", a=4),
                                           ACT.Copy).then_inc(othi_done, 1)
                    if 1 <= t <= T:
                        u = t - 1
                        act.wait_ge(x1_done, 2 * u + 2)
                        act.wait_ge(sso_done, 2 * min(t + 2, T))
                        act.activation(sq[:], x1[u % 2][:], ACT.Square, accum_out=ss2(u)).then_inc(ss2_done, 1)
                    if t >= 2:
                        u = t - 2
                        for b in range(2):
                            act.wait_ge(ht_ready, 2 * u + b + 1)
                            if u and b == 0:
                                act.wait_ge(lg_ready, u)
                            act.activation(h2T[:, 4 * b:4 * b + 4, :], ps[:, HT[b], :].rearrange("p (a c) -> p a c", a=4),
                                           ACT.Copy).then_inc(ht_copied, 1)
                        act.wait_ge(lmax_done, u + 1)
                        if u:
                            act.wait_ge(at_ready, u)
                        act.activation(aff, LG, ACT.Exp, bias=lmax(u), accum_out=lsum(u)).then_inc(lexp_done, 1)

            @block.vector
            def _(dve):
                steps = Steps(dve, vsteps)
                def group_rows(t):
                    dve.wait_ge(ro_done, t + 1)
                    for n in range(2):
                        cols = slice(n * C_K, (n + 1) * C_K)
                        dve.tensor_scalar(o[t % 3][:, cols], o[t % 3][:, cols], ro(t)[:, n:n + 1], None, ALU.mult).then_inc(on_done, 1)

                group_rows(0)
                for t in range(T + 3):
                    if 1 <= t <= T:
                        u = t - 1
                        dve.wait_ge(wo_done, u + 1)
                        dve.wait_ge(xr_loaded[u % 3], 16 * (u // 3 + 1))
                        if u >= 2:
                            dve.wait_ge(x1_stored[u % 2], 16 * (u // 2))
                            dve.wait_ge(h2_done, u - 1)
                        for n in range(2):
                            cols = slice(n * BANK, (n + 1) * BANK)
                            dve.tensor_tensor(x1[u % 2][:, cols], WO[:, cols], xr[u % 3][:, cols], ALU.add).then_inc(x1_done, 1)
                    if t < T:
                        for b in range(2):
                            dve.wait_ge(othi_done, 2 * t + b + 1)
                            dve.tensor_tensor(otlo[t % 2][:, 4 * b:4 * b + 4, :], ps[:, OT[b], :].rearrange("p (a c) -> p a c", a=4),
                                              othi[t % 2][:, 4 * b:4 * b + 4, :].bitcast(F32), ALU.subtract).then_inc(otlo_done, 1)
                    if t + 1 < T:
                        group_rows(t + 1)
                    if 1 <= t <= T:
                        if u == 0:
                            dve.wait_ge(small_loaded, 32)
                        if u >= 2:
                            dve.wait_ge(h2_stored[u % 2], 16 * (u // 2))
                        dve.wait_ge(x1_done, 2 * u + 2)
                        dve.wait_ge(r2_done, u + 1)
                        dve.scalar_tensor_tensor(out=h2[u % 2][:], in0=x1[u % 2][:], scalar=r2(u), in1=gffn[:],
                                                 op0=ALU.mult, op1=ALU.mult).then_inc(h2_done, 1)
                    if t >= 3:
                        u = t - 3
                        dve.wait_ge(at_ready, u + 1)
                        dve.tensor_copy(k["affT"][:, u * P:(u + 1) * P], AT).then_inc(at_done, 1)
                    if 2 <= t <= T + 1:
                        u = t - 2
                        dve.wait_ge(lg_ready, u + 1)
                        dve.tensor_reduce(lmax(u), LG, AX.X, ALU.max, negate=True).then_inc(lmax_done, 1)
                        dve.wait_ge(lexp_done, u + 1)
                        dve.reciprocal(lrec(u), lsum(u)).then_inc(lrec_done, 1)
                        dve.wait_ge(lrec_done, u + 1)
                        dve.tensor_scalar(aff, aff, lrec(u), None, ALU.mult).then_inc(aff_done, 1)
                    if t >= 3 and TS - 1 <= t - 3 < TS - 1 + CAP // 8:
                        dve.wait_ge(at_done, t - 2)
                        top_eight(dve, k, 0, t - 3 - (TS - 1), steps)
                for r in range(max(0, T - TS + 1), CAP // 8):
                    top_eight(dve, k, 0, r, steps)


def top_eight(dve, k, s, r, steps):
    aff = k["affT"][:, s * SEQ:(s + 1) * SEQ]
    cols = slice(s * CAP + 8 * r, s * CAP + 8 * r + 8)
    steps.did(dve.max(k["gates"][:, cols], aff))
    steps.wait()
    steps.did(dve.max_index(k["idx8"][:, cols], k["gates"][:, cols], aff))
    steps.wait()
    steps.did(dve.match_replace(aff, k["gates"][:, cols], aff, -1.0))
    steps.wait()


def experts(nc, a, k, moe, ps, banks, out, h2_dram, raw_loaded):
    raw, hi, lo = moe["raw"], moe["hi"], moe["lo"]
    xe, xehi, xelo, silu, h, hthi, htlo, y = (moe[n] for n in ("xe", "xehi", "xelo", "silu", "h", "hthi", "htlo", "y"))
    X, G, U, Y = (0, 1), (2, 3), (4, 5), (6, 7)
    LAST = EXPERTS - 1

    with Phase(nc, "m") as phase:
        sem = phase.sem
        hi_done, lo_done, chunk_used = sem("hi_done"), sem("lo_done"), sem("chunk_used")
        idx_float, route_ready, gates_ready, idx_ready = sem("idx_float"), sem("route_ready"), sem("gates_ready"), sem("idx_ready")
        xe_loaded, xt_ready, xehi_done, xelo_done = sem("xe_loaded"), sem("xe_transposed"), sem("xehi_done"), sem("xelo_done")
        gu_done, silu_done, h_done = sem("gu_done"), sem("silu_done"), sem("h_done")
        ht_ready, hthi_done, htlo_done = sem("h_transposed"), sem("hthi_done"), sem("htlo_done")
        y_ready, y_done, y_free, added = sem("y_ready"), sem("y_done"), sem("y_free"), sem("added")
        vsteps, psteps = sem("vector_steps_e"), sem("pool_steps_e")
        with nc.Block() as block:

            @block.sync
            def _(sp):
                need_split = sp.alloc_register("need_split")

                def load(e, j, c):
                    sp.reg_mov(need_split, c - RING + 1)
                    sp.wait_ge(raw_loaded[0], 16)
                    sp.wait_ge(lo_done, need_split)
                    load_chunk(sp, a, moe, raw_loaded, e, j)

                with sp.Fori(0, LAST) as e:
                    for j in range(RING, CHUNKS):
                        load(e, j, e * CHUNKS + j)
                    for j in range(RING):
                        load(e + 1, j, e * CHUNKS + CHUNKS + j)
                for j in range(RING, CHUNKS):
                    load(LAST, j, LAST * CHUNKS + j)

            @block.gpsimd
            def _(pool):
                need_copied = pool.alloc_register("need_copied")

                def gather(e, turn):
                    pool.tensor_copy(moe["take"][:], moe["idxT"][:, bass.ds(e, 1)]).then_inc(psteps, 1)
                    pool.reg_mov(need_copied, turn + 1)
                    pool.wait_ge(idx_ready, 1)
                    pool.wait_ge(psteps, need_copied)
                    pool.indirect_dma_start(xe[:, :], None, h2_dram, bass.IndirectOffsetOnAxis(moe["take"][:, 0:1], 0)).then_inc(xe_loaded, 16)

                def add_rows(e):
                    pool.tensor_copy(moe["give"][:], moe["idxT"][:, bass.ds(e, 1)]).then_inc(y_free, 1)
                    pool.wait_ge(idx_ready, 1)
                    pool.wait_ge(y_free, e + 1)
                    pool.wait_ge(y_done, 2 * e + 2)
                    pool.indirect_dma_start(out, bass.IndirectOffsetOnAxis(moe["give"][:, 0:1], 0), y[:, :], None,
                                            compute_op=ALU.add).then_inc(added, 16)
                    pool.wait_ge(added, 16 * e + 16)

                pool.wait_ge(idx_ready, 1)
                gather(0, 0)
                with pool.Fori(0, LAST) as e:
                    pool.wait_ge(xt_ready, 2 * e + 2)
                    pool.wait_ge(xe_loaded, 16 * e + 16)
                    gather(e + 1, e + 1)
                    add_rows(e)
                add_rows(LAST)

            @block.tensor
            def _(pe):
                def transposes(src, bank, cols, ready):
                    for i in range(4):
                        last = pe.transpose(ps[:, bank, i * P:(i + 1) * P], src[:, cols + i * P:cols + (i + 1) * P], k["ident"][:])
                    last.then_inc(ready, 1)

                def gate_up(e, j):
                    half, group = j // 4, j % 4 // 2
                    pe.wait_ge(xelo_done, 2 * e + group + 1)
                    pe.wait_ge(lo_done, e * CHUNKS + j + 2)
                    g, u = j % RING, (j + 1) % RING
                    for i in range(CK):
                        c = group * CK + i
                        cols = slice(i * BANK, (i + 1) * BANK)
                        start, stop = c == 0, c == KD - 1
                        for bank, w in ((G[half], g), (U[half], u)):
                            pe.matmul(ps[:, bank, :], xehi[:, c, :], hi[w][:, cols], start=start, stop=False)
                            pe.matmul(ps[:, bank, :], xehi[:, c, :], lo[w][:, cols], start=False, stop=False)
                        for bank, w in ((G[half], g), (U[half], u)):
                            last = pe.matmul(ps[:, bank, :], xelo[:, c, :], hi[w][:, cols], start=False, stop=stop)
                            if i == CK - 1 and not (stop and bank == U[half]):
                                last.then_inc(chunk_used, 1)
                    if c == KD - 1:
                        last.then_inc(gu_done, 1)

                def down(e, j):
                    pe.wait_ge(lo_done, e * CHUNKS + j + 1)
                    w = j % RING
                    for i in range(2):
                        f = 2 * (j - 8) + i
                        for lhs, part in ((hthi, hi), (hthi, lo), (htlo, hi)):
                            for n in range(2):
                                cols = slice(i * D + n * BANK, i * D + (n + 1) * BANK)
                                last = pe.matmul(ps[:, Y[n], :], lhs[:, f, :], part[w][:, cols],
                                                 start=(f == 0 and part is hi and lhs is hthi), stop=(f == KD - 1 and lhs is htlo))
                    last.then_inc(y_ready if j == CHUNKS - 1 else chunk_used, 1)

                def expert(e, more):
                    gate_up(e, 0)
                    gate_up(e, 2)
                    gate_up(e, 4)
                    pe.wait_ge(h_done, 2 * e + 1)
                    transposes(h, X[0], 0, ht_ready)
                    gate_up(e, 6)
                    pe.wait_ge(htlo_done, 2 * e + 1)
                    down(e, 8)
                    pe.wait_ge(h_done, 2 * e + 2)
                    transposes(h, X[1], BANK, ht_ready)
                    down(e, 9)
                    if more:
                        pe.wait_ge(xe_loaded, 16 * e + 32)
                        transposes(xe, X[0], 0, xt_ready)
                    pe.wait_ge(htlo_done, 2 * e + 2)
                    down(e, 10)
                    if more:
                        transposes(xe, X[1], BANK, xt_ready)
                    down(e, 11)

                pe.wait_ge(route_ready, 1)
                pe.transpose(ps[:, Y[0], 0:EXPERTS], k["gates"][:], k["ident"][0:EXPERTS, 0:EXPERTS])
                pe.transpose(ps[:, Y[0], P:P + EXPERTS], moe["idxf"][:], k["ident"][0:EXPERTS, 0:EXPERTS]).then_inc(route_ready, 1)
                pe.wait_ge(xe_loaded, 16)
                transposes(xe, X[0], 0, xt_ready)
                transposes(xe, X[1], BANK, xt_ready)
                with pe.Fori(0, LAST) as e:
                    expert(e, True)
                expert(LAST, False)

            def wait_used(eng, e, j):
                c = j - RING
                if c < 0:
                    c += CHUNKS
                    e = e - 1
                if c == 3:
                    eng.wait_ge(gu_done, 2 * e + 1)
                elif c == 7:
                    eng.wait_ge(gu_done, 2 * e + 2)
                elif c == CHUNKS - 1:
                    eng.wait_ge(y_ready, e + 1)
                else:
                    n = c + 1 - (c > 3) - (c > 7)
                    eng.wait_ge(chunk_used, e * (CHUNKS - 3) + n)

            @block.scalar
            def _(act):
                def split(e, j, wait=True):
                    act.wait_ge(raw_loaded[j % RING], 16 * (e * (CHUNKS // RING) + j // RING + 1))
                    if wait:
                        wait_used(act, e, j)
                    act.activation(hi[j % RING][:], raw[j % RING][:], ACT.Copy).then_inc(hi_done, 1)

                def high(dst, b, ready, n, done):
                    act.wait_ge(ready, n)
                    act.activation(dst[:, 4 * b:4 * b + 4, :], ps[:, X[b], :].rearrange("p (a c) -> p a c", a=4), ACT.Copy).then_inc(done, 1)

                def gate(e, half):
                    act.wait_ge(gu_done, 2 * e + half + 1)
                    act.activation(silu[:, half * BANK:(half + 1) * BANK], ps[:, G[half], :], ACT.Silu).then_inc(silu_done, 1)

                def expert(e, more):
                    split(e, 6)
                    split(e, 7)
                    gate(e, 0)
                    split(e, 8)
                    split(e, 9)
                    high(hthi, 0, ht_ready, 2 * e + 1, hthi_done)
                    split(e, 10)
                    split(e, 11)
                    gate(e, 1)
                    if more:
                        split(e + 1, 0)
                        split(e + 1, 1)
                    high(hthi, 1, ht_ready, 2 * e + 2, hthi_done)
                    if more:
                        split(e + 1, 2)
                        high(xehi, 0, xt_ready, 2 * e + 3, xehi_done)
                        split(e + 1, 3)
                        high(xehi, 1, xt_ready, 2 * e + 4, xehi_done)
                        split(e + 1, 4)
                        split(e + 1, 5)
                    act.wait_ge(y_ready, e + 1)
                    act.wait_ge(y_free, e + 1)
                    for n in range(2):
                        act.activation(y[:, n * BANK:(n + 1) * BANK], ps[:, Y[n], :], ACT.Copy,
                                       scale=moe["gT"][:, bass.ds(e, 1)]).then_inc(y_done, 1)

                for j in range(RING):
                    split(0, j, wait=False)
                for b in range(2):
                    high(xehi, b, xt_ready, b + 1, xehi_done)
                act.wait_ge(gates_ready, 1)
                with act.Fori(0, LAST) as e:
                    expert(e, True)
                expert(LAST, False)

            @block.vector
            def _(dve):
                steps = Steps(dve, vsteps)

                def split(e, j):
                    dve.wait_ge(hi_done, e * CHUNKS + j + 1)
                    dve.tensor_tensor(lo[j % RING][:], raw[j % RING][:], hi[j % RING][:].bitcast(F32), ALU.subtract).then_inc(lo_done, 1)

                def low(dst, part, b, ready, n, done):
                    dve.wait_ge(ready, n)
                    cols = slice(4 * b, 4 * b + 4)
                    dve.tensor_tensor(dst[:, cols, :], ps[:, X[b], :].rearrange("p (a c) -> p a c", a=4),
                                      part[:, cols, :].bitcast(F32), ALU.subtract).then_inc(done, 1)

                def product(e, half):
                    cols = slice(half * BANK, (half + 1) * BANK)
                    dve.wait_ge(silu_done, 2 * e + half + 1)
                    dve.tensor_tensor(h[:, cols], ps[:, U[half], :], silu[:, cols], ALU.mult).then_inc(h_done, 1)

                def expert(e, more):
                    split(e, 6)
                    split(e, 7)
                    product(e, 0)
                    split(e, 8)
                    split(e, 9)
                    low(htlo, hthi, 0, hthi_done, 2 * e + 1, htlo_done)
                    split(e, 10)
                    split(e, 11)
                    product(e, 1)
                    if more:
                        split(e + 1, 0)
                        split(e + 1, 1)
                    low(htlo, hthi, 1, hthi_done, 2 * e + 2, htlo_done)
                    if more:
                        split(e + 1, 2)
                        low(xelo, xehi, 0, xehi_done, 2 * e + 3, xelo_done)
                        split(e + 1, 3)
                        low(xelo, xehi, 1, xehi_done, 2 * e + 4, xelo_done)
                        split(e + 1, 4)
                        split(e + 1, 5)

                for r in range(CAP // 8):
                    top_eight(dve, k, 1, r, steps)
                steps.did(dve.tensor_copy(moe["idxf"][:], k["idx8"][:]))
                steps.wait()
                dve.tensor_scalar(moe["idxf"][:, CAP:2 * CAP], moe["idxf"][:, CAP:2 * CAP], float(SEQ), None, ALU.add).then_inc(route_ready, 1)
                dve.wait_ge(route_ready, 2)
                dve.tensor_copy(moe["idxT"][:], ps[:, Y[0], P:P + EXPERTS]).then_inc(idx_ready, 1)
                dve.tensor_copy(moe["gT"][:], ps[:, Y[0], 0:EXPERTS]).then_inc(gates_ready, 1)
                for j in range(RING):
                    split(0, j)
                for b in range(2):
                    low(xelo, xehi, b, xehi_done, b + 1, xelo_done)
                with dve.Fori(0, LAST) as e:
                    expert(e, True)
                expert(LAST, False)


_WEIGHTS = ["norm_attn", "w_in", "gqa_q_norm", "gqa_k_norm", "mla_q_a_norm", "mla_w_uq", "mla_q_nope_norm",
            "mla_q_pe_norm", "mla_kv_a_norm", "mla_w_ukv", "mla_k_nope_norm", "mla_k_pe_norm", "out_norm_a",
            "out_norm_b", "w_o", "norm_ffn", "w_router", "w_gate", "w_up", "w_down"]


def kernel(x_prompt, x_sample, **weights):
    import numpy as _np
    import concourse.bacc as _bacc
    from concourse import mybir as _mybir
    from concourse.bass_utils import run_bass_kernel_spmd as _run

    nc = _bacc.Bacc("TRN2", target_bir_lowering=False, num_devices=1)
    named = {"x": _np.concatenate([_np.asarray(x_prompt).reshape(SEQ, D), _np.asarray(x_sample).reshape(SEQ, D)]),
             "tab": rotary_tables(), "invn": inverse_counts()}
    for name in _WEIGHTS:
        named[name] = _np.ascontiguousarray(weights[name])
    aps = {n: nc.dram_tensor(f"in_{n}", v.shape, _mybir.dt.from_np(v.dtype), kind="ExternalInput").ap() for n, v in named.items()}
    out = nc.dram_tensor("out", (SETS * SEQ, D), _mybir.dt.float32, kind="ExternalOutput").ap()
    build(nc, aps, out)
    r = _run(nc, [{f"in_{n}": v for n, v in named.items()}], core_ids=[0])
    got = r.results[0]["out"]
    return got[0:SEQ].reshape(1, SEQ, D), got[SEQ:].reshape(1, SEQ, D)
```

```python
from contextlib import ExitStack

import numpy as np

import concourse.bass as bass
from concourse import mybir

F32 = mybir.dt.float32
F32R = mybir.dt.float32r
U32 = mybir.dt.uint32
ALU = mybir.AluOpType
ACT = mybir.ActivationFunctionType
AX = mybir.AxisListType

P = 128
BANK = 512
EPS = 1e-6

SETS, SEQ, D = 2, 512, 1024
GRID_W, ROPE_THETA = 64, 10000.0
TS = SEQ // P
T = SETS * TS
KD = D // P

QH, KVH, HD = 8, 2, 64
MH, Q_LORA, KV_LORA, NOPE, PE_D, VD = 8, 256, 128, 64, 32, 64
QK = NOPE + PE_D
C_K = QH * HD
C_V = C_K + KVH * HD
C_CQ = C_V + KVH * HD
C_CKV = C_CQ + Q_LORA
C_KPE = C_CKV + KV_LORA
D_IN = C_KPE + PE_D
UQ = MH * QK
UKV = MH * (NOPE + VD)
KB = NOPE + PE_D + VD
HEADS = QH + MH
GROUP = QH // KVH
O_PARTS = [(0, QH), (QH, QH + MH // 2), (QH + MH // 2, HEADS)]

EXPERTS, FF = 16, 1024
CAP = 2 * SEQ // EXPERTS
CK = 4
CHUNK = CK * BANK
CHUNKS = 12
RING = 6

G_ATTN, G_QA, G_KVA, G_OUT, G_QN, G_KN, G_ROWS = 0, 8, 10, 11, 19, 20, 21
TAB = 2 * (HD + PE_D)
STATS = QH + KVH + 3


def rotary_tables():
    out = []
    for rot in (HD, PE_D):
        half = rot // 2
        inv = (ROPE_THETA ** (-np.arange(0, half, 2, dtype=np.float32) / half)).astype(np.float32)
        row = np.repeat(np.arange(SEQ // GRID_W, dtype=np.float32), GRID_W)
        col = np.tile(np.arange(GRID_W, dtype=np.float32), SEQ // GRID_W)
        r, c = row[:, None] * inv[None, :], col[:, None] * inv[None, :]
        angle = np.concatenate([r, r, c, c], axis=-1)
        sign = np.repeat(np.array([-1, 1, -1, 1], np.float32), rot // 4)
        out += [np.cos(angle), np.sin(angle) * sign]
    return np.concatenate(out, axis=1).astype(np.float32)


def inverse_counts():
    a = [1 / HD] * (QH + KVH) + [1 / Q_LORA, 1 / KV_LORA, 1 / PE_D] + [1 / NOPE] * MH + [1 / PE_D] * MH
    return np.tile(np.array(a, np.float32), (P, 1))


class Phase:

    def __init__(self, nc, suffix):
        self.nc, self.suffix, self.sems = nc, suffix, []

    def __enter__(self):
        return self

    def sem(self, name):
        self.sems.append(self.nc.alloc_semaphore(f"{name}_{self.suffix}"))
        return self.sems[-1]

    def __exit__(self, *failure):
        if failure[0] is None:
            self.nc.clear_and_free_semaphores(self.sems)
            self.nc.all_engine_barrier()


class Steps:

    def __init__(self, engine, sem):
        self.engine, self.sem, self.n = engine, sem, 0

    def did(self, instruction):
        instruction.then_inc(self.sem, 1)
        self.n += 1

    def wait(self):
        self.engine.wait_ge(self.sem, self.n)


def build(nc, a, out):
    x_dram = a["x"].rearrange("(t p) d -> t p d", p=P)
    out_rows = out.rearrange("(t p) d -> t p d", p=P)
    o_dram = nc.dram_tensor("attention_out", [T * P, D], F32).ap()
    o_rows = o_dram.rearrange("(t p) d -> t p d", p=P)
    h2_dram = nc.dram_tensor("h2", [T * P, D], F32).ap()
    h2_rows = h2_dram.rearrange("(t p) d -> t p d", p=P)

    with ExitStack() as ctx:
        sb = lambda name, shape, dt=F32: ctx.enter_context(nc.sbuf_tensor(name, shape, dt))
        ps = ctx.enter_context(nc.psum_tensor("ps", [P, 8, BANK], F32))

        def banks(first, n):
            return ps[:, first:first + n, :].rearrange("p b c -> p (b c)")

        k = {}
        k["ident"] = sb("ident", [P, P])
        k["tab"] = sb("tab", [P, TS, TAB])
        k["gq"] = sb("gq", [P, TS, 2, HD])
        k["gk"] = sb("gk", [P, TS, 2, HD])
        k["gqp"] = sb("gqp", [P, TS, 2, PE_D])
        k["gkp"] = sb("gkp", [P, TS, 2, PE_D])
        k["gcol"] = sb("gcol", [P, G_ROWS])
        k["invn"] = sb("invn", [P, STATS + 2 * MH])
        k["minus_half"] = sb("minus_half", [P, 16])
        k["gates"] = sb("gates", [EXPERTS, SETS * CAP])
        k["idx8"] = sb("idx8", [EXPERTS, SETS * CAP], U32)

        shared_at = (nc.sbuf_base + 63) // 64 * 64
        arena = shared_at + T * P * 4

        class Map:
            def __init__(self, at):
                self.at = at

            def __call__(self, name, shape, dt=F32):
                free = int(np.prod(shape[1:])) * 4
                t = nc.alloc_sbuf_tensor_at(name, shape, dt, offset=self.at)
                self.at += (free + 63) // 64 * 64
                return t

        k["affT"] = Map(shared_at)("affT", [EXPERTS, T * P])
        rows = Map(arena)
        pj = rows("pj", [P, TS, D_IN])
        q_rows = rows("q_rows", [P, TS, MH, QK])
        kv_rows = rows("kv_rows", [P, TS, MH, KB])
        temps_at = rows.at
        stage = Map(arena)
        w_raw = stage("w_raw", [P, KD, D_IN])
        uq_raw = stage("uq_raw", [P, 2, UQ])
        ukv_raw = stage("ukv_raw", [P, UKV])
        assert stage.at <= temps_at
        tm = Map(temps_at)
        temps = {}
        temps["x"] = [tm(f"x{i}", [P, D]) for i in range(2)]
        hi_lo_at = tm.at
        tm.at += 2 * KD * P * 4
        sq_at = tm.at
        temps["sq"] = tm("sq", [P, D_IN])
        gains_at = tm.at
        temps["gb"] = tm("gb", [P, TAB])
        temps["grow"] = tm("grow", [G_ROWS, P])
        temps["small"] = tm("small", [P, 128])
        latents_at = tm.at
        temps["chi"] = tm("chi", [P, 3, P], F32R)
        temps["clo"] = tm("clo", [P, 3, P], F32R)
        temps["ra"] = tm("ra", [P, (QH + KVH) * HD])
        squares_at = tm.at
        temps["sqk"] = tm("sqk", [P, MH * NOPE])
        temps["sqq"] = tm("sqq", [P, UQ])
        weights_at = temps_at + 33 * 1024 + 256
        wm = Map(weights_at)
        w = {}
        w["whi"] = wm("whi", [P, KD, D_IN], F32R)
        w["wlo"] = wm("wlo", [P, KD, D_IN], F32R)
        w["uqhi"] = wm("uqhi", [P, 2, UQ], F32R)
        w["uqlo"] = wm("uqlo", [P, 2, UQ], F32R)
        w["ukvhi"] = wm("ukvhi", [P, UKV], F32R)
        w["ukvlo"] = wm("ukvlo", [P, UKV], F32R)
        end = nc.sbuf_usable_end // 64 * 64
        w_end = wm.at
        hl = Map(hi_lo_at)
        temps["xhi"] = [hl("xhi0", [P, KD, P], F32R), wm("xhi1", [P, KD, P], F32R)]
        temps["xlo"] = [hl("xlo0", [P, KD, P], F32R), wm("xlo1", [P, KD, P], F32R)]
        assert wm.at <= end and tm.at <= weights_at

        am = Map(temps_at)
        att = {}
        att["hi"] = [[am(f"{n}hi{i}", [P, SEQ], F32R) for i in range(2)] for n in "qk"]
        att["lo"] = [[am(f"{n}lo{i}", [P, SEQ], F32R) for i in range(2)] for n in "qk"]
        assert am.at <= sq_at
        att["p"] = [Map(sq_at + i * SEQ * 4)(f"prob{i}", [P, SEQ]) for i in range(2)]
        am = Map(gains_at)
        att["nmax"] = am("nmax", [P, HEADS * TS])
        att["sum"] = am("psum", [P, HEADS * TS])
        att["rsum"] = am("rsum", [P, HEADS * TS])
        assert am.at <= latents_at - 512
        am = Map(latents_at)
        att["ot"] = am("ot", [VD, SEQ])
        att["otv"] = am("otv", [VD, SEQ])
        assert am.at <= squares_at
        att["pthi"] = [Map(at)(f"probThi{i}", [P, TS, 2 * P], F32R) for i, at in enumerate((shared_at, squares_at))]
        assert squares_at + 2 * TS * P * 4 <= weights_at

        om = Map(weights_at)
        wo = {}
        wo["hi"] = om("wohi", [P, KD, D], F32R)
        wo["lo"] = om("wolo", [P, KD, D], F32R)
        om2 = Map(om.at)
        wo["raw"] = om("woraw", [P, 4, D])
        assert om.at <= end
        am = Map(w_end)
        att["p"].append(am("prob2", [P, SEQ]))
        att["ptlo"] = [am(f"probTlo{i}", [P, TS, 2 * P], F32R) for i in range(2)]
        att["v"] = [am(f"v{i}", [P, TS, 2, VD], F32R) for i in range(2)]
        assert am.at <= end
        wo["othi"] = [om2(f"othi{i}", [P, KD, P], F32R) for i in range(2)]
        wo["otlo"] = [om2(f"otlo{i}", [P, KD, P], F32R) for i in range(2)]
        wo["x1"] = [om2(f"x1_{i}", [P, D]) for i in range(2)]
        wo["h2T"] = om2("h2T", [P, KD, P])
        assert om2.at <= end
        om3 = Map(temps_at)
        om4 = Map(om2.at)
        wo["o"] = [om3("o0", [P, D]), om3("o1", [P, D]), om4("o2", [P, D])]
        wo["x"] = [om3("xr0", [P, D]), om3("xr1", [P, D]), om4("xr2", [P, D])]
        assert om4.at <= end
        wo["h2"] = [om3(f"h2_{i}", [P, D]) for i in range(2)]
        wo["gffn"] = om3("gffn", [P, D])
        wo["sq"] = om3("sqo", [P, D])
        wo["wr"] = om3("wr", [P, KD, EXPERTS])
        wo["small"] = om3("smallo", [P, 128])
        assert om3.at <= weights_at, (om3.at - weights_at)

        mm = Map(arena)
        moe = {}
        moe["raw"] = [mm(f"raw{i}", [P, CHUNK]) for i in range(RING)]
        assert mm.at <= temps_at
        mm = Map(temps_at)
        moe["hi"] = [mm(f"hi{i}", [P, CHUNK], F32R) for i in range(RING)]
        moe["lo"] = [mm(f"lo{i}", [P, CHUNK], F32R) for i in range(RING)]
        moe["xe"] = mm("xe", [P, D])
        moe["xehi"] = mm("xehi", [P, KD, P], F32R)
        moe["xelo"] = mm("xelo", [P, KD, P], F32R)
        moe["silu"] = mm("silu", [P, FF])
        moe["h"] = mm("h", [P, FF])
        moe["hthi"] = mm("hthi", [P, KD, P], F32R)
        moe["htlo"] = mm("htlo", [P, KD, P], F32R)
        moe["y"] = mm("y", [P, D])
        moe["gT"] = mm("gT", [P, EXPERTS])
        moe["idxf"] = mm("idxf", [EXPERTS, SETS * CAP])
        moe["idxT"] = mm("idxT", [P, EXPERTS], U32)
        moe["take"] = mm("take", [P, 1], U32)
        moe["give"] = mm("give", [P, 1], U32)
        assert mm.at <= end, (mm.at, end)

        raw_loaded = [ctx.enter_context(nc.semaphore(f"raw_loaded{i}")) for i in range(RING)]
        o_stored = ctx.enter_context(nc.semaphore("o_stored"))
        wo_loaded = ctx.enter_context(nc.semaphore("wo_loaded"))

        for s in range(SETS):
            project_and_attend(nc, s, a, x_dram, k, temps, w, att, wo, pj, q_rows, kv_rows, w_raw, uq_raw, ukv_raw,
                               ps, banks, o_rows, o_stored, wo_loaded)
        route(nc, a, x_dram, k, wo, moe, ps, banks, o_rows, out_rows, h2_rows, raw_loaded, o_stored)
        experts(nc, a, k, moe, ps, banks, out, h2_dram, raw_loaded)


def project(phase, s, a, x_dram, k, tp, w, pj, q_rows, kv_rows, w_raw, uq_raw, ukv_raw, ps, banks, o_stored):
    first = s == 0
    x, xhi, xlo, chi, clo, sq, ra, small = (tp[n] for n in ("x", "xhi", "xlo", "chi", "clo", "sq", "ra", "small"))
    sqk, sqq = tp["sqk"], tp["sqq"]
    ssx, rx = small[:, 0:TS], small[:, TS:2 * TS]
    ssa, rsa = small[:, 8:8 + STATS], small[:, 24:24 + STATS]
    ssk, rsk = small[:, 40:40 + MH], small[:, 48:48 + MH]
    ssb, rsb = small[:, 56:56 + 2 * MH], small[:, 72:72 + 2 * MH]
    xt_ps = [banks(0, 1), banks(1, 1)]
    pj_ps, c_ps, u_ps = banks(2, 3)[:, 0:D_IN], banks(5, 1)[:, 0:3 * P], banks(6, 2)
    chunks = [(0, 512), (512, 1024), (1024, D_IN)]
    half = UQ // 2

    sem = phase.sem
    rows_ready, mla_ready = sem("rows_ready"), sem("mla_ready")
    x_loaded = [sem("x_loaded0"), sem("x_loaded1")]
    gains_loaded, const_loaded, tables_loaded = sem("gains_loaded"), sem("const_loaded"), sem("tables_loaded")
    w_loaded, u_loaded = [sem(f"w_loaded{i}") for i in range(KD if first else 0)], sem("u_loaded")
    ident_ready, rows_set, gt_ready, gcol_ready = sem("ident_ready"), sem("rows_set"), sem("gt_ready"), sem("gcol_ready")
    whi_done, wlo_done = sem("whi_done"), sem("wlo_done")
    ssx_done, rx_done = sem("ssx_done"), sem("rx_done")
    xt_ready, xhi_done, xlo_done = sem("xt_ready"), sem("xhi_done"), sem("xlo_done")
    proj_done, pj_done, c_normed = sem("proj_done"), sem("pj_done"), sem("c_normed")
    ct_ready, chi_done, clo_done = sem("ct_ready"), sem("chi_done"), sem("clo_done")
    uq_done, q_copied = sem("uq_done"), sem("q_copied")
    ukv_done, kv_done = sem("ukv_done"), sem("kv_done")
    stat_a, stat_k, stat_b = sem("stat_a"), sem("stat_k"), sem("stat_b")
    ra_done, rk_done, rb_done = sem("ra_done"), sem("rk_done"), sem("rb_done")
    vsteps, psteps = sem("vector_steps"), sem("pool_steps")

    def sync_program(sp):
        def load_x(t):
            sp.dma_start(x[t % 2][:], x_dram[TS * s + t]).then_inc(x_loaded[t % 2], 16)

        if first:
            sp.wait_ge(rows_set, 1)
            for row, name, n in ((G_ATTN, "norm_attn", D), (G_QA, "mla_q_a_norm", Q_LORA),
                                 (G_KVA, "mla_kv_a_norm", KV_LORA), (G_OUT, "out_norm_a", C_K),
                                 (G_OUT + C_K // P, "out_norm_b", MH * VD)):
                sp.dma_start(tp["grow"][row:row + n // P, :], a[name].rearrange("(r c) -> r c", c=P)).then_inc(gains_loaded, 16)
            for row, name in ((G_QN, "mla_q_nope_norm"), (G_KN, "mla_k_nope_norm")):
                sp.dma_start(tp["grow"][row:row + 1, 0:NOPE], a[name].rearrange("(r c) -> r c", r=1)).then_inc(gains_loaded, 16)
            load_x(0)
            for i in range(KD):
                if i == KD // 2:
                    load_x(1)
                sp.dma_start(w_raw[:, i, :], a["w_in"][i * P:(i + 1) * P, :]).then_inc(w_loaded[i], 16)
            sp.dma_start(uq_raw[:], a["mla_w_uq"].rearrange("(k p) n -> p k n", p=P)).then_inc(u_loaded, 16)
            sp.dma_start(ukv_raw[:], a["mla_w_ukv"]).then_inc(u_loaded, 16)
        else:
            load_x(0)
            load_x(1)
        for t in range(2, TS):
            sp.wait_ge(xt_ready, 2 * (t - 1))
            sp.wait_ge(ssx_done, t - 1)
            load_x(t)

    def gpsimd_program(pool):
        steps = Steps(pool, psteps)
        if first:
            pool.memset(tp["grow"][:], 1.0).then_inc(rows_set, 1)
            steps.did(pool.memset(k["minus_half"][:], -0.5))
            steps.did(pool.memset(k["ident"][:], 0.0))
            steps.wait()
            pool.affine_select(out=k["ident"][:], in_=k["ident"][:], compare_op=ALU.not_equal, fill=1.0,
                               base=0, pattern=[[-1, P]], channel_multiplier=1).then_inc(ident_ready, 1)
            pool.dma_start(k["invn"][:], a["invn"]).then_inc(const_loaded, 16)
            pool.dma_start(k["tab"][:], a["tab"].rearrange("(i p) c -> p i c", p=P)).then_inc(tables_loaded, 16)
            at = 0
            for name, n in (("gqa_q_norm", HD), ("gqa_k_norm", HD), ("mla_q_pe_norm", PE_D), ("mla_k_pe_norm", PE_D)):
                pool.dma_start(tp["gb"][:, at:at + n], a[name].partition_broadcast(P)).then_inc(tables_loaded, 16)
                at += n
            pool.wait_ge(const_loaded, 16)

        def inverse_root(dst, src, done):
            steps.did(pool.tensor_scalar(src, src, 1.0, EPS, ALU.mult, ALU.add))
            steps.wait()
            pool.tensor_tensor(dst, src, k["minus_half"][:, 0:src.shape[1]], ALU.pow).then_inc(done, 1)

        def mean(src, at):
            steps.did(pool.tensor_tensor(src, src, k["invn"][:, at:at + src.shape[1]], ALU.mult))
            steps.wait()

        def x_norm(t):
            pool.wait_ge(ssx_done, t + 1)
            steps.did(pool.tensor_scalar(ssx[:, t:t + 1], ssx[:, t:t + 1], 1.0 / D, EPS, ALU.mult, ALU.add))
            steps.wait()
            pool.tensor_tensor(rx[:, t:t + 1], ssx[:, t:t + 1], k["minus_half"][:, 0:1], ALU.pow).then_inc(rx_done, 1)

        x_norm(0)
        def mla_roots(u):
            pool.wait_ge(stat_k, u + 1)
            mean(ssk, 0)
            inverse_root(rsk, ssk, rk_done)
            pool.wait_ge(stat_b, u + 1)
            mean(ssb, STATS)
            inverse_root(rsb, ssb, rb_done)

        for t in range(TS):
            if t >= 2:
                mla_roots(t - 2)
            if t + 1 < TS:
                x_norm(t + 1)
            pool.wait_ge(stat_a, t + 1)
            mean(ssa, 0)
            inverse_root(rsa, ssa, ra_done)
        mla_roots(TS - 2)
        return mla_roots

    def tensor_program(pe):
        if first:
            pe.wait_ge(ident_ready, 1)
            pe.wait_ge(gains_loaded, 7 * 16)
            pe.transpose(ps[:, 5, 0:G_ROWS], tp["grow"][:], k["ident"][0:G_ROWS, 0:G_ROWS]).then_inc(gt_ready, 1)

        def x_transposes(t):
            pe.wait_ge(x_loaded[t % 2], 16 * (t // 2 + 1))
            if t:
                pe.wait_ge(xlo_done, 2 * t)
            for b in range(2):
                for i in range(4):
                    c = 4 * b + i
                    last = pe.transpose(xt_ps[b][:, i * P:(i + 1) * P], x[t % 2][:, c * P:(c + 1) * P], k["ident"][:])
                last.then_inc(xt_ready, 1)

        def latent_transposes(u):
            pe.wait_ge(c_normed, u + 1)
            if u == 0 and first:
                pe.wait_ge(gcol_ready, 1)
            if u:
                pe.wait_ge(clo_done, u)
            for i in range(3):
                last = pe.transpose(c_ps[:, i * P:(i + 1) * P], pj[:, u, C_CQ + i * P:C_CQ + (i + 1) * P], k["ident"][:])
            last.then_inc(ct_ready, 1)

        def queries(u):
            pe.wait_ge(clo_done, u + 1)
            if u:
                pe.wait_ge(kv_done, 3 * u)
            for n in range(2):
                dst = u_ps[:, n * BANK:n * BANK + half]
                for i in range(2):
                    for lhs, rhs in ((chi, "uqhi"), (chi, "uqlo"), (clo, "uqhi")):
                        last = pe.matmul(dst, lhs[:, i, :], w[rhs][:, i, n * half:(n + 1) * half],
                                         start=(i == 0 and rhs == "uqhi" and lhs is chi), stop=(i == 1 and lhs is clo))
            last.then_inc(uq_done, 1)

        def keys_values(u):
            pe.wait_ge(q_copied, 2 * (u + 1))
            for n in range(2):
                cols = slice(n * BANK, (n + 1) * BANK)
                pe.matmul(u_ps[:, cols], chi[:, 2, :], w["ukvhi"][:, cols], start=True, stop=False)
                pe.matmul(u_ps[:, cols], chi[:, 2, :], w["ukvlo"][:, cols], start=False, stop=False)
                last = pe.matmul(u_ps[:, cols], clo[:, 2, :], w["ukvhi"][:, cols], start=False, stop=True)
            last.then_inc(ukv_done, 1)

        x_transposes(0)
        for t in range(TS):
            for c in range(KD):
                if c == 2 and t + 1 < TS:
                    x_transposes(t + 1)
                if c == 4 and t:
                    latent_transposes(t - 1)
                if c == 6 and t:
                    queries(t - 1)
                pe.wait_ge(xlo_done, 2 * t + c // 4 + 1)
                if t and c == 0:
                    pe.wait_ge(pj_done, 2 * t - 1)
                if first and t == 0:
                    pe.wait_ge(wlo_done, c + 1)
                for lhs, rhs in ((xhi[t % 2], "whi"), (xhi[t % 2], "wlo"), (xlo[t % 2], "whi")):
                    for lo, up in chunks:
                        last = pe.matmul(pj_ps[:, lo:up], lhs[:, c, :], w[rhs][:, c, lo:up],
                                         start=(c == 0 and rhs == "whi" and lhs is xhi[t % 2]),
                                         stop=(c == KD - 1 and lhs is xlo[t % 2]))
            last.then_inc(proj_done, 1)
            if first and t == 0:
                pe.wait_ge(wlo_done, KD + 3)
            if t:
                keys_values(t - 1)
        latent_transposes(TS - 1)
        queries(TS - 1)
        return keys_values

    def scalar_program(act):
        def split_weights():
            act.wait_ge(gcol_ready, 2)
            for i in range(KD):
                act.wait_ge(w_loaded[i], 16)
                act.activation(w["whi"][:, i, :], w_raw[:, i, :], ACT.Copy,
                               scale=k["gcol"][:, G_ATTN + i:G_ATTN + i + 1]).then_inc(whi_done, 1)
            act.wait_ge(u_loaded, 32)
            for i in range(2):
                act.activation(w["uqhi"][:, i, :], uq_raw[:, i, :], ACT.Copy,
                               scale=k["gcol"][:, G_QA + i:G_QA + i + 1]).then_inc(whi_done, 1)
            act.activation(w["ukvhi"][:], ukv_raw[:], ACT.Copy, scale=k["gcol"][:, G_KVA:G_KVA + 1]).then_inc(whi_done, 1)

        def x_high(t):
            act.wait_ge(x_loaded[t % 2], 16 * (t // 2 + 1))
            for b in range(2):
                act.wait_ge(xt_ready, 2 * t + b + 1)
                if t >= 2 and b == 0:
                    act.wait_ge(proj_done, t - 1)
                act.activation(xhi[t % 2][:, 4 * b:4 * b + 4, :], xt_ps[b].rearrange("p (a c) -> p a c", a=4),
                               ACT.Copy).then_inc(xhi_done, 1)
            if t:
                act.wait_ge(ssx_done, t)
            if t >= 2:
                act.wait_ge(stat_a, t - 1)
                act.wait_ge(pj_done, 2 * (t - 1))
            act.activation(sq[:, 0:D], x[t % 2][:], ACT.Square, accum_out=ssx[:, t:t + 1]).then_inc(ssx_done, 1)

        x_high(0)
        if first:
            split_weights()
        def latents_high(u):
            act.wait_ge(ct_ready, u + 1)
            if u:
                act.wait_ge(ukv_done, u)
            act.activation(chi[:], c_ps.rearrange("p (a c) -> p a c", a=3), ACT.Copy).then_inc(chi_done, 1)

        def queries(u):
            act.wait_ge(uq_done, u + 1)
            act.activation(q_rows[:, u].rearrange("p (n h) c -> p n (h c)", n=2),
                           ps[:, 6:8, 0:half], ACT.Copy).then_inc(q_copied, 1)
            if u:
                act.wait_ge(stat_b, u)
            act.activation(sqq[:].rearrange("p (n c) -> p n c", n=2), ps[:, 6:8, 0:half], ACT.Square).then_inc(q_copied, 1)

        def rows(t):
            act.wait_ge(proj_done, t + 1)
            act.wait_ge(rx_done, t + 1)
            act.wait_ge(ssx_done, min(t + 2, TS))
            if t:
                act.wait_ge(stat_a, t)
            if t == 0:
                if first:
                    act.wait_ge(wlo_done, KD + 3)
                else:
                    act.wait_ge(o_stored, 16 * len(O_PARTS) * s)
            act.activation(pj[:, t, :], pj_ps, ACT.Copy, scale=rx[:, t:t + 1]).then_inc(pj_done, 1)
            act.wait_ge(pj_done, 2 * t + 1)
            act.activation(sq[:], pj[:, t, :], ACT.Square).then_inc(pj_done, 1)

        def keys_values(u):
            act.wait_ge(ukv_done, u + 1)
            nope = u_ps.rearrange("p (h c) -> p h c", h=MH)[:, :, 0:NOPE]
            value = u_ps.rearrange("p (h c) -> p h c", h=MH)[:, :, NOPE:NOPE + VD]
            act.activation(kv_rows[:, u, :, 0:NOPE], nope, ACT.Copy).then_inc(kv_done, 1)
            if u:
                act.wait_ge(stat_k, u)
            act.activation(sqk[:].rearrange("p (h c) -> p h c", h=MH), nope, ACT.Square).then_inc(kv_done, 1)
            act.activation(kv_rows[:, u, :, QK:KB], value, ACT.Copy).then_inc(kv_done, 1)

        for t in range(TS):
            if t + 1 < TS:
                x_high(t + 1)
            if t >= 1:
                latents_high(t - 1)
                queries(t - 1)
            rows(t)
            if t >= 1:
                keys_values(t - 1)
        latents_high(TS - 1)
        queries(TS - 1)
        return keys_values

    def vector_program(dve):
        steps = Steps(dve, vsteps)

        def broadcast(col, n, m):
            return col.unsqueeze(2).to_broadcast([P, n, m])

        def rotate(rows_ap, heads, rot, tab_ap, tmp):
            v = rows_ap.rearrange("p h (a b q) -> p h a b q", a=2, b=2)
            tv = tmp.rearrange("p (h a b q) -> p h a b q", h=heads, a=2, b=2)
            sin = tab_ap[:, 1, :].rearrange("p (a b q) -> p a b q", a=2, b=2)
            for b in range(2):
                for i in range(2):
                    steps.did(dve.tensor_tensor(tv[:, :, i, b, :], v[:, :, i, 1 - b, :],
                                                sin[:, i, b, :].unsqueeze(1).to_broadcast([P, heads, rot // 4]), ALU.mult))
            steps.wait()
            steps.did(dve.tensor_tensor(rows_ap, rows_ap, tab_ap[:, 0, :].unsqueeze(1).to_broadcast([P, heads, rot]), ALU.mult))
            steps.wait()
            return dve.tensor_tensor(rows_ap, rows_ap, tmp.rearrange("p (h c) -> p h c", h=heads), ALU.add)

        def split_weights():
            for i in range(KD):
                dve.wait_ge(whi_done, i + 1)
                dve.scalar_tensor_tensor(out=w["wlo"][:, i, :], in0=w_raw[:, i, :], scalar=k["gcol"][:, G_ATTN + i:G_ATTN + i + 1],
                                         in1=w["whi"][:, i, :].bitcast(F32), op0=ALU.mult, op1=ALU.subtract).then_inc(wlo_done, 1)
            for i in range(2):
                dve.wait_ge(whi_done, KD + 1 + i)
                dve.scalar_tensor_tensor(out=w["uqlo"][:, i, :], in0=uq_raw[:, i, :], scalar=k["gcol"][:, G_QA + i:G_QA + i + 1],
                                         in1=w["uqhi"][:, i, :].bitcast(F32), op0=ALU.mult, op1=ALU.subtract).then_inc(wlo_done, 1)
            dve.wait_ge(whi_done, KD + 3)
            dve.scalar_tensor_tensor(out=w["ukvlo"][:], in0=ukv_raw[:], scalar=k["gcol"][:, G_KVA:G_KVA + 1],
                                     in1=w["ukvhi"][:].bitcast(F32), op0=ALU.mult, op1=ALU.subtract).then_inc(wlo_done, 1)

        def tables():
            dve.wait_ge(tables_loaded, 5 * 16)
            at = 0
            for name, rot, c0 in (("gq", HD, 0), ("gk", HD, 0), ("gqp", PE_D, 2 * HD), ("gkp", PE_D, 2 * HD)):
                g = tp["gb"][:, at:at + rot]
                gv = g.rearrange("p (a b q) -> p a b q", a=2, b=2)
                at += rot
                cos, sin = k["tab"][:, :, c0:c0 + rot], k["tab"][:, :, c0 + rot:c0 + 2 * rot]
                steps.did(dve.tensor_tensor(k[name][:, :, 0, :], cos, g.unsqueeze(1).to_broadcast([P, TS, rot]), ALU.mult))
                sv = sin.rearrange("p i (a b q) -> p i a b q", a=2, b=2)
                ov = k[name][:, :, 1, :].rearrange("p i (a b q) -> p i a b q", a=2, b=2)
                for i in range(2):
                    for b in range(2):
                        steps.did(dve.tensor_tensor(ov[:, :, i, b, :], sv[:, :, i, b, :],
                                                    gv[:, i, 1 - b, :].unsqueeze(1).to_broadcast([P, TS, rot // 4]), ALU.mult))
            steps.wait()

        if first:
            dve.wait_ge(gt_ready, 1)
            dve.tensor_copy(k["gcol"][:], ps[:, 5, 0:G_ROWS]).then_inc(gcol_ready, 1)
            dve.wait_ge(gcol_ready, 1)
            dve.tensor_scalar(k["gcol"][:, G_QN:G_QN + 1], k["gcol"][:, G_QN:G_QN + 1], float(QK) ** -0.5, None,
                              ALU.mult).then_inc(gcol_ready, 1)

        def x_low(t):
            for b in range(2):
                dve.wait_ge(xhi_done, 2 * t + b + 1)
                cols = slice(4 * b, 4 * b + 4)
                dve.tensor_tensor(xlo[t % 2][:, cols, :], xt_ps[b].rearrange("p (a c) -> p a c", a=4),
                                  xhi[t % 2][:, cols, :].bitcast(F32), ALU.subtract).then_inc(xlo_done, 1)

        heads = QH + KVH

        def latents_low(u):
            dve.wait_ge(chi_done, u + 1)
            dve.tensor_tensor(clo[:], c_ps.rearrange("p (a c) -> p a c", a=3), chi[:].bitcast(F32),
                              ALU.subtract).then_inc(clo_done, 1)

        def row_stats(t):
            row = pj[:, t, :]
            dve.wait_ge(pj_done, 2 * t + 2)
            steps.did(dve.tensor_reduce(ssa[:, heads:heads + 1], sq[:, C_CQ:C_CKV], AX.X, ALU.add))
            steps.did(dve.tensor_reduce(ssa[:, heads + 1:heads + 2], sq[:, C_CKV:C_KPE], AX.X, ALU.add))
            steps.did(dve.tensor_reduce(ssa[:, heads + 2:heads + 3], sq[:, C_KPE:D_IN], AX.X, ALU.add))
            dve.tensor_reduce(ssa[:, 0:heads], sq[:, 0:C_V].rearrange("p (h c) -> p h c", h=heads),
                              AX.X, ALU.add).then_inc(stat_a, 1)

        def row_norms(t):
            row = pj[:, t, :]
            dve.wait_ge(ra_done, t + 1)
            steps.did(dve.tensor_scalar(row[:, C_CKV:C_KPE], row[:, C_CKV:C_KPE], rsa[:, heads + 1:heads + 2], None, ALU.mult))
            dve.tensor_scalar(row[:, C_CQ:C_CKV], row[:, C_CQ:C_CKV], rsa[:, heads:heads + 1], None, ALU.mult).then_inc(c_normed, 1)
            steps.did(dve.tensor_scalar(row[:, C_KPE:D_IN], row[:, C_KPE:D_IN], rsa[:, heads + 2:heads + 3], None, ALU.mult))
            qk = row[:, 0:C_V].rearrange("p (h c) -> p h c", h=heads)
            steps.did(dve.tensor_tensor(qk, qk, broadcast(rsa[:, 0:heads], heads, HD), ALU.mult))
            steps.wait()

        def rotations(t):
            row = pj[:, t, :]
            qk = row[:, 0:C_V].rearrange("p (h c) -> p h c", h=heads)
            kpe = row[:, C_KPE:D_IN].rearrange("p (h c) -> p h c", h=1)
            steps.did(rotate(kpe, 1, PE_D, k["gkp"][:, t], ra[:, 0:PE_D]))
            steps.wait()
            steps.did(rotate(qk[:, 0:QH], QH, HD, k["gq"][:, t], ra[:, 0:C_K]))
            rotate(qk[:, QH:], KVH, HD, k["gk"][:, t], ra[:, C_K:C_V]).then_inc(rows_ready, 1)
            steps.wait()
            dve.wait_ge(rows_ready, t + 1)

        def mla_stats(u):
            dve.wait_ge(kv_done, 3 * u + 2)
            steps.wait()
            dve.tensor_reduce(ssk, sqk[:].rearrange("p (h c) -> p h c", h=MH), AX.X, ALU.add).then_inc(stat_k, 1)
            steps.did(dve.tensor_copy(kv_rows[:, u, :, NOPE:QK],
                                      pj[:, u, C_KPE:D_IN].unsqueeze(1).to_broadcast([P, MH, PE_D])))
            dve.wait_ge(q_copied, 2 * (u + 1))
            squares = sqq[:].rearrange("p (h c) -> p h c", h=MH)
            steps.did(dve.tensor_reduce(ssb[:, 0:MH], squares[:, :, 0:NOPE], AX.X, ALU.add))
            dve.tensor_reduce(ssb[:, MH:2 * MH], squares[:, :, NOPE:QK], AX.X, ALU.add).then_inc(stat_b, 1)

        def mla_norms(u):
            kn, q = kv_rows[:, u, :, 0:NOPE], q_rows[:, u]
            dve.wait_ge(stat_b, u + 1)
            dve.wait_ge(rk_done, u + 1)
            steps.did(dve.tensor_tensor(kn, kn, broadcast(rsk, MH, NOPE), ALU.mult))
            dve.wait_ge(rb_done, u + 1)
            steps.did(dve.tensor_tensor(q[:, :, 0:NOPE], q[:, :, 0:NOPE], broadcast(rsb[:, 0:MH], MH, NOPE), ALU.mult))
            steps.did(dve.tensor_tensor(q[:, :, NOPE:QK], q[:, :, NOPE:QK], broadcast(rsb[:, MH:2 * MH], MH, PE_D), ALU.mult))
            steps.wait()
            rotate(q[:, :, NOPE:QK], MH, PE_D, k["gqp"][:, u], ra[:, 0:MH * PE_D]).then_inc(mla_ready, 1)
            dve.wait_ge(mla_ready, u + 1)

        x_low(0)
        if first:
            split_weights()
        for t in range(TS):
            if t >= 2:
                mla_stats(t - 2)
            if t + 1 < TS:
                x_low(t + 1)
            if t >= 1:
                latents_low(t - 1)
                rotations(t - 1)
            row_stats(t)
            if first and t == 0:
                tables()
            if t >= 2:
                mla_norms(t - 2)
            row_norms(t)
        latents_low(TS - 1)
        mla_stats(TS - 2)
        rotations(TS - 1)
        return mla_stats, mla_norms

    signals = {"rows_ready": rows_ready, "mla_ready": mla_ready, "xlo_done": xlo_done, "kv_done": kv_done,
               "stat_k": stat_k, "stat_b": stat_b, "stat_a": stat_a, "ukv_done": ukv_done, "pj_done": pj_done}
    return (sync_program, gpsimd_program, tensor_program, scalar_program, vector_program), signals


def attend(phase, project_signals, s, a, k, att, wo, pj, q_rows, kv_rows, ps, banks, o_rows, o_stored, wo_loaded):
    rows_ready, mla_ready, kv_done, stat_k, stat_b, ukv_done = (
        project_signals[n] for n in ("rows_ready", "mla_ready", "kv_done", "stat_k", "stat_b", "ukv_done"))
    last_set = s == SETS - 1
    STEPS = 8
    units = [(h, i) for h in range(HEADS) for i in range(TS)]
    NU = len(units)
    qhi, khi = att["hi"]
    qlo, klo = att["lo"]
    preps, key_of = [], {}
    for h in range(HEADS):
        if h >= QH or h % GROUP == 0:
            preps.append(("k", h))
        key_of[h] = sum(1 for kind, _ in preps if kind == "k") - 1
        preps.append(("q", h))
    prep_index = {p: n for n, p in enumerate(preps)}
    due = {}
    for kind, h in preps:
        due.setdefault(max(0, TS * (h - 1) + (0 if kind == "k" else 2)) if h else -1, []).append((kind, h))
    PREP, S_BANKS, T_BANKS, OT_BANK, O_BANK = 0, (1, 2, 3), (4, 5), 6, 7
    PAIRS = NU // 2
    pthi, ptlo, ot, otv = (att[n] for n in ("pthi", "ptlo", "ot", "otv"))

    sem = phase.sem
    prep_ready, prep_hi, prep_lo = sem("prep_ready"), sem("prep_hi"), sem("prep_lo")
    score_ready, max_done, exp_done = sem("score_ready"), sem("max_done"), sem("exp_done")
    pt_ready, pthi_done, ptlo_done, pv_done = sem("pt_ready"), sem("pthi_done"), sem("ptlo_done"), sem("pv_done")
    vhi_done, vlo_done, ot_copied, o_ready, ot_added = sem("vhi_done"), sem("vlo_done"), sem("ot_copied"), sem("o_ready"), sem("ot_added")
    rsum_done, o_done = sem("rsum_done"), sem("o_done")
    wo_hi, wo_scaled, wo_lo = sem("wo_hi"), sem("wo_scaled"), sem("wo_lo")

    def value_of(h):
        if h < QH:
            c = C_V + h // GROUP * HD
            return pj[:, :, c:c + HD]
        return kv_rows[:, :, h - QH, QK:KB]

    def pair_cols(u):
        return slice(u % 2 * P, (u % 2 + 1) * P)

    def sync_program(sp):
        if last_set:
            sp.wait_ge(ukv_done, TS)
            for i in range(KD // 2):
                if i >= 2:
                    sp.wait_ge(wo_lo, 2 * (i - 1))
                sp.dma_start(wo["raw"][:, 2 * (i % 2):2 * (i % 2) + 2, :],
                             a["w_o"].rearrange("(k p) n -> p k n", p=P)[:, 2 * i:2 * i + 2, :]).then_inc(wo_loaded, 16)
        for h0, h1 in O_PARTS:
            cols = slice(h0 * VD, h1 * VD)
            sp.wait_ge(o_done, h1)
            sp.dma_start(o_rows[TS * s:TS * (s + 1), :, cols].rearrange("t p d -> p t d"), pj[:, :, cols]).then_inc(o_stored, 16)

    def gpsimd_program(pool, mla_roots):
        def split_output_weights(pool, i):
            gain, raw = k["gcol"][:, G_OUT + i:G_OUT + i + 1], wo["raw"][:, i % 4, :]
            pool.wait_ge(wo_hi, i + 1)
            pool.tensor_scalar(raw, raw, gain, None, ALU.mult).then_inc(wo_scaled, 1)
            pool.wait_ge(wo_scaled, i + 1)
            pool.tensor_tensor(wo["lo"][:, i, :], raw, wo["hi"][:, i, :].bitcast(F32), ALU.subtract).then_inc(wo_lo, 1)

        keys = [h for kind, h in preps if kind == "k"]
        pool.wait_ge(rows_ready, TS)
        for n, h in enumerate(keys):
            if h == QH:
                pool.wait_ge(mla_ready, TS)
            if n >= 2:
                pool.wait_ge(pv_done, TS // 2 * keys[n - 1])
            v = att["v"][n % 2]
            pool.tensor_copy(v[:, :, 0, :], value_of(h)).then_inc(vhi_done, 1)
            pool.wait_ge(vhi_done, n + 1)
            pool.tensor_tensor(v[:, :, 1, :], value_of(h), v[:, :, 0, :].bitcast(F32), ALU.subtract).then_inc(vlo_done, 1)
            if n == 0:
                mla_roots(TS - 1)
            if last_set and n == 1:
                for i in range(KD):
                    split_output_weights(pool, i)

    def tensor_program(pe, keys_values):
        def prepare(kind, h):
            n = prep_index[kind, h]
            if n:
                pe.wait_ge(prep_lo, n)
            for i in range(TS):
                if h < QH:
                    c = h * HD if kind == "q" else C_K + h // GROUP * HD
                    src, dst = pj[:, i, c:c + HD], ps[0:HD, PREP, i * P:(i + 1) * P]
                else:
                    src = q_rows[:, i, h - QH, :] if kind == "q" else kv_rows[:, i, h - QH, 0:QK]
                    dst = ps[0:QK, PREP, i * P:(i + 1) * P]
                last = pe.transpose(dst, src, k["ident"][:])
            last.then_inc(prep_ready, 1)

        def scores(u):
            h, i = units[u]
            if i == 0:
                pe.wait_ge(prep_lo, prep_index["q", h] + 1)
            if u >= 3:
                pe.wait_ge(exp_done, u - 2)
            dst, q, kk, cols = ps[:, S_BANKS[u % 3], :], h % 2, key_of[h] % 2, slice(i * P, (i + 1) * P)
            if h < QH:
                pe.matmul(dst, qhi[q][:, cols], khi[kk][:], start=True, stop=False)
                last = pe.matmul(dst, qhi[q][:, cols], klo[kk][:], start=False, stop=True)
            else:
                pe.matmul(dst, qhi[q][0:QK, cols], khi[kk][0:QK, :], start=True, stop=False)
                pe.matmul(dst, qhi[q][0:QK, cols], klo[kk][0:QK, :], start=False, stop=False)
                last = pe.matmul(dst, qlo[q][0:QK, cols], khi[kk][0:QK, :], start=False, stop=True)
            last.then_inc(score_ready, 1)

        def transpose_probs(u):
            pe.wait_ge(exp_done, u + 1)
            if u >= 2:
                pe.wait_ge(ptlo_done, u - 1)
            for i in range(TS):
                cols = slice(i * P, (i + 1) * P)
                last = pe.transpose(ps[:, T_BANKS[u % 2], cols], att["p"][u % 3][:, cols], k["ident"][:])
            last.then_inc(pt_ready, 1)

        def values(m):
            h, qi = units[2 * m]
            pe.wait_ge(ptlo_done, 2 * m + 2)
            if qi == 0:
                pe.wait_ge(vlo_done, key_of[h] + 1)
                if h == 0:
                    pe.wait_ge(kv_done, 3 * TS)
                if h:
                    pe.wait_ge(ot_added, h)
            v = att["v"][key_of[h] % 2]
            cols = slice(qi * P, (qi + 2) * P)
            for part, i in [("hi", 0)] + [("lo", i) for i in range(TS)] + [("hi", i) for i in range(1, TS)]:
                if part == "hi":
                    last = pe.matmul(ps[:, OT_BANK, cols], v[:, i].rearrange("p a c -> p (a c)"), pthi[m % 2][:, i, :],
                                     start=(i == 0), stop=(i == TS - 1))
                else:
                    pe.matmul(ps[0:VD, OT_BANK, cols], v[:, i, 0, :], ptlo[m % 2][:, i, :], start=False, stop=False)
            last.then_inc(pv_done, 1)

        def transpose_output(h):
            pe.wait_ge(ot_added, h + 1)
            if h:
                pe.wait_ge(o_done, h)
            for i in range(TS):
                last = pe.transpose(ps[:, O_BANK, i * VD:(i + 1) * VD], ot[:, i * P:(i + 1) * P], k["ident"][0:VD, 0:VD])
            last.then_inc(o_ready, 1)

        pe.wait_ge(rows_ready, TS)
        for kind, h in due.get(-1, []):
            prepare(kind, h)
        keys_values(TS - 1)
        for u in range(NU + STEPS):
            for kind, h in due.get(u, []):
                if (kind, h) == ("k", QH):
                    pe.wait_ge(mla_ready, TS)
                prepare(kind, h)
            if u < NU:
                scores(u)
            if 0 <= u - 3 < NU:
                transpose_probs(u - 3)
            if u >= 10 and (u - 10) % TS == 0:
                transpose_output((u - 10) // TS)
            if u >= 6 and u % 2 == 0 and (u - 6) // 2 < PAIRS:
                values((u - 6) // 2)

    def scalar_program(act, keys_values):
        def prepare(kind, h):
            n = prep_index[kind, h]
            act.wait_ge(prep_ready, n + 1)
            if kind == "q":
                dst = qhi[h % 2]
                if h >= 2:
                    act.wait_ge(score_ready, TS * (h - 1))
            else:
                dst = khi[key_of[h] % 2]
                if key_of[h] >= 2:
                    act.wait_ge(score_ready, TS * (h - 1))
            src = ps[:, PREP, :]
            if h < QH and kind == "q":
                act.activation(dst[0:HD, :], src[0:HD, :], ACT.Copy, scale=float(HD) ** -0.5).then_inc(prep_hi, 1)
            elif h < QH:
                act.activation(dst[0:HD, :], src[0:HD, :], ACT.Copy)
                act.activation(dst[HD:P, :], src[0:HD, :], ACT.Copy).then_inc(prep_hi, 1)
            else:
                g = G_QN if kind == "q" else G_KN
                act.activation(dst[0:QK, :], src[0:QK, :], ACT.Copy, scale=k["gcol"][0:QK, g:g + 1]).then_inc(prep_hi, 1)

        for kind, h in due.get(-1, []):
            prepare(kind, h)
        keys_values(TS - 1)
        for u in range(NU + STEPS):
            if u >= 9 and (u - 9) % TS == 0:
                h = (u - 9) // TS
                act.wait_ge(pv_done, TS // 2 * (h + 1))
                if h:
                    act.wait_ge(ot_added, h)
                act.activation(otv[:], ps[VD:P, OT_BANK, :], ACT.Copy).then_inc(ot_copied, 1)
            for kind, h in due.get(u, []):
                prepare(kind, h)
            if 1 <= u <= NU:
                v = u - 1
                act.wait_ge(max_done, v + 1)
                if v >= 3:
                    act.wait_ge(pt_ready, v - 2)
                act.activation(att["p"][v % 3][:], ps[:, S_BANKS[v % 3], :], ACT.Exp, bias=att["nmax"][:, v:v + 1],
                               accum_out=att["sum"][:, v:v + 1]).then_inc(exp_done, 1)
            if 0 <= u - 3 < NU:
                v = u - 3
                act.wait_ge(pt_ready, v + 1)
                if v == 2:
                    act.wait_ge(stat_k, TS)
                    act.wait_ge(stat_b, TS)
                if v >= 4:
                    act.wait_ge(pv_done, v // 2 - 1)
                act.activation(pthi[v // 2 % 2][:, :, pair_cols(v)],
                               ps[:, T_BANKS[v % 2], :].rearrange("p (a c) -> p a c", a=TS), ACT.Copy).then_inc(pthi_done, 1)
            if last_set and u % 4 == 2 and 1 <= u // 4 <= KD:
                i = u // 4 - 1
                act.wait_ge(wo_loaded, 16 * (KD // 2) if i >= KD - 4 else 16 * 2)
                act.activation(wo["hi"][:, i, :], wo["raw"][:, i % 4, :], ACT.Copy,
                               scale=k["gcol"][:, G_OUT + i:G_OUT + i + 1]).then_inc(wo_hi, 1)

    def vector_program(dve, mla_stats, mla_norms):
        def prepare(kind, h):
            n = prep_index[kind, h]
            dve.wait_ge(prep_hi, n + 1)
            src = ps[:, PREP, :]
            if h < QH and kind == "q":
                dst = qhi[h % 2]
                dve.scalar_tensor_tensor(out=dst[HD:P, :], in0=src[0:HD, :], scalar=float(HD) ** -0.5,
                                         in1=dst[0:HD, :].bitcast(F32), op0=ALU.mult, op1=ALU.subtract).then_inc(prep_lo, 1)
            elif h < QH:
                kk = key_of[h] % 2
                for rows in (slice(0, HD), slice(HD, P)):
                    last = dve.tensor_tensor(klo[kk][rows, :], src[0:HD, :], khi[kk][rows, :].bitcast(F32), ALU.subtract)
                last.then_inc(prep_lo, 1)
            else:
                hi, lo = (qhi[h % 2], qlo[h % 2]) if kind == "q" else (khi[key_of[h] % 2], klo[key_of[h] % 2])
                g = G_QN if kind == "q" else G_KN
                dve.scalar_tensor_tensor(out=lo[0:QK, :], in0=src[0:QK, :], scalar=k["gcol"][0:QK, g:g + 1],
                                         in1=hi[0:QK, :].bitcast(F32), op0=ALU.mult, op1=ALU.subtract).then_inc(prep_lo, 1)

        for kind, h in due.get(-1, []):
            prepare(kind, h)
        for u in range(NU + STEPS):
            if u >= 9 and (u - 9) % TS == 0:
                h = (u - 9) // TS
                dve.wait_ge(ot_copied, h + 1)
                if h:
                    dve.wait_ge(o_ready, h)
                dve.tensor_tensor(ot[:], ps[0:VD, OT_BANK, :], otv[:], ALU.add).then_inc(ot_added, 1)
            if 0 <= u - 4 < NU:
                v = u - 4
                dve.wait_ge(pthi_done, v + 1)
                cols = pair_cols(v)
                dve.tensor_tensor(ptlo[v // 2 % 2][:, :, cols], ps[:, T_BANKS[v % 2], :].rearrange("p (a c) -> p a c", a=TS),
                                  pthi[v // 2 % 2][:, :, cols].bitcast(F32), ALU.subtract).then_inc(ptlo_done, 1)
            if u < NU:
                dve.wait_ge(score_ready, u + 1)
                dve.tensor_reduce(att["nmax"][:, u:u + 1], ps[:, S_BANKS[u % 3], :], AX.X, ALU.max,
                                  negate=True).then_inc(max_done, 1)
            for kind, h in due.get(u, []):
                prepare(kind, h)
            if u >= 10 and (u - 10) % TS == 0:
                h = (u - 10) // TS
                cols = slice(TS * h, TS * (h + 1))
                dve.wait_ge(exp_done, TS * (h + 1))
                dve.reciprocal(att["rsum"][:, cols], att["sum"][:, cols]).then_inc(rsum_done, 1)
                dve.wait_ge(o_ready, h + 1)
                dve.wait_ge(rsum_done, h + 1)
                dve.tensor_tensor(pj[:, :, h * VD:(h + 1) * VD],
                                  ps[:, O_BANK, 0:TS * VD].rearrange("p (i c) -> p i c", i=TS),
                                  att["rsum"][:, cols].unsqueeze(2).to_broadcast([P, TS, VD]), ALU.mult).then_inc(o_done, 1)
            if u == 1:
                mla_norms(TS - 2)
            elif u == 2:
                mla_stats(TS - 1)
            elif u == 6:
                mla_norms(TS - 1)

    return sync_program, gpsimd_program, tensor_program, scalar_program, vector_program


def project_and_attend(nc, s, a, x_dram, k, temps, w, att, wo, pj, q_rows, kv_rows, w_raw, uq_raw, ukv_raw,
                       ps, banks, o_rows, o_stored, wo_loaded):
    with Phase(nc, s) as phase:
        project_programs, signals = project(phase, s, a, x_dram, k, temps, w, pj, q_rows, kv_rows, w_raw, uq_raw, ukv_raw,
                                            ps, banks, o_stored)
        attend_programs = attend(phase, signals, s, a, k, att, wo, pj, q_rows, kv_rows, ps, banks, o_rows, o_stored, wo_loaded)
        with nc.Block() as block:

            @block.sync
            def _(sp):
                project_programs[0](sp)
                attend_programs[0](sp)

            @block.gpsimd
            def _(pool):
                attend_programs[1](pool, project_programs[1](pool))

            @block.tensor
            def _(pe):
                attend_programs[2](pe, project_programs[2](pe))

            @block.scalar
            def _(act):
                attend_programs[3](act, project_programs[3](act))

            @block.vector
            def _(dve):
                attend_programs[4](dve, *project_programs[4](dve))


def load_chunk(sp, a, moe, raw_loaded, e, j):
    slot = moe["raw"][j % RING]
    if j < 8:
        half, group, name = j // 4, j % 4 // 2, "w_gate" if j % 2 == 0 else "w_up"
        src = a[name][bass.ds(e, 1), group * CK * P:(group + 1) * CK * P, half * BANK:(half + 1) * BANK]
        src = src.rearrange("e (k p) n -> p (e k) n", p=P)
        dst = slot[:].rearrange("p (k n) -> p k n", k=CK)
    else:
        i = 2 * (j - 8)
        src = a["w_down"][bass.ds(e, 1), i * P:(i + 2) * P, :].rearrange("e (k p) n -> p (e k) n", p=P)
        dst = slot[:].rearrange("p (k n) -> p k n", k=2)
    sp.dma_start(dst, src).then_inc(raw_loaded[j % RING], 16)


def route(nc, a, x_dram, k, wo, moe, ps, banks, o_rows, out_rows, h2_rows, raw_loaded, o_stored):
    o, xr, h2, gffn, sq, wr, small = (wo[n] for n in ("o", "x", "h2", "gffn", "sq", "wr", "small"))
    othi, otlo, x1, h2T = (wo[n] for n in ("othi", "otlo", "x1", "h2T"))
    column = lambda at, t, n=1: small[:, at + n * t:at + n * t + n]
    sso, ro = (lambda t: column(0, t, 2)), (lambda t: column(16, t, 2))
    ss2, r2 = (lambda t: column(32, t)), (lambda t: column(40, t))
    lmax, lsum, lrec = (lambda t: column(48, t)), (lambda t: column(56, t)), (lambda t: column(64, t))
    aff = small[:, 72:72 + EXPERTS]
    OT, WO, HT, LG, AT = (0, 1), banks(2, 2), (4, 5), ps[:, 6, 0:EXPERTS], ps[0:EXPERTS, 7, 0:P]

    with Phase(nc, "m") as phase:
        sem = phase.sem
        o_loaded, xr_loaded = [sem(f"o_loaded{i}") for i in range(3)], [sem(f"xr_loaded{i}") for i in range(3)]
        small_loaded, x1_stored, h2_stored = sem("small_loaded"), [sem("x1_stored0"), sem("x1_stored1")], [sem("h2_stored0"), sem("h2_stored1")]
        sso_done, ro_done, on_done = sem("sso_done"), sem("ro_done"), sem("on_done")
        ot_ready, othi_done, otlo_done = sem("ot_ready"), sem("othi_done"), sem("otlo_done")
        wo_done, x1_done, ss2_done, r2_done, h2_done = sem("wo_done"), sem("x1_done"), sem("ss2_done"), sem("r2_done"), sem("h2_done")
        ht_ready, ht_copied, lg_ready = sem("ht_ready"), sem("ht_copied"), sem("lg_ready")
        lmax_done, lexp_done, lrec_done, aff_done = sem("lmax_done"), sem("lexp_done"), sem("lrec_done"), sem("aff_done")
        at_ready, at_done, psteps, vsteps = sem("at_ready"), sem("at_done"), sem("pool_steps_r"), sem("vector_steps_r")
        with nc.Block() as block:

            @block.sync
            def _(sp):
                for t in range(T):
                    if t >= 3:
                        sp.wait_ge(ot_ready, 2 * (t - 2))
                        sp.wait_ge(x1_done, 2 * (t - 2))
                    sp.wait_ge(o_stored, 16 * len(O_PARTS) * (t // TS + 1))
                    sp.dma_start(o[t % 3][:], o_rows[t]).then_inc(o_loaded[t % 3], 16)
                    sp.dma_start(xr[t % 3][:], x_dram[t]).then_inc(xr_loaded[t % 3], 16)
                    if t == 0:
                        sp.dma_start(gffn[:], a["norm_ffn"].partition_broadcast(P)).then_inc(small_loaded, 16)
                        sp.dma_start(wr[:], a["w_router"].rearrange("(k p) e -> p k e", p=P)).then_inc(small_loaded, 16)
                    if t == 1:
                        sp.wait_ge(o_stored, 16 * len(O_PARTS) * SETS)
                    if 1 <= t <= RING:
                        load_chunk(sp, a, moe, raw_loaded, 0, t - 1)

            @block.gpsimd
            def _(pool):
                steps = Steps(pool, psteps)

                def inverse_root(dst, src, n, done):
                    steps.did(pool.tensor_scalar(src, src, 1.0 / n, EPS, ALU.mult, ALU.add))
                    steps.wait()
                    pool.tensor_tensor(dst, src, k["minus_half"][:, 0:src.shape[1]], ALU.pow).then_inc(done, 1)

                def group_norm(t):
                    pool.wait_ge(sso_done, 2 * t + 2)
                    inverse_root(ro(t), sso(t), C_K, ro_done)

                group_norm(0)
                for t in range(T + 1):
                    if t + 1 < T:
                        group_norm(t + 1)
                    if t >= 1:
                        u = t - 1
                        pool.wait_ge(ss2_done, u + 1)
                        inverse_root(r2(u), ss2(u), D, r2_done)
                        pool.dma_start(out_rows[u], x1[u % 2][:]).then_inc(x1_stored[u % 2], 16)
                        pool.wait_ge(h2_done, u + 1)
                        pool.dma_start(h2_rows[u], h2[u % 2][:]).then_inc(h2_stored[u % 2], 16)
                for i in range(2):
                    pool.wait_ge(x1_stored[i], 16 * T // 2)
                    pool.wait_ge(h2_stored[i], 16 * T // 2)

            @block.tensor
            def _(pe):
                def h2_transposes(u):
                    pe.wait_ge(h2_done, u + 1)
                    if u:
                        pe.wait_ge(ht_copied, 2 * u)
                    for b in range(2):
                        for i in range(4):
                            c = 4 * b + i
                            last = pe.transpose(ps[:, HT[b], i * P:(i + 1) * P], h2[u % 2][:, c * P:(c + 1) * P], k["ident"][:])
                        last.then_inc(ht_ready, 1)

                for t in range(T + 3):
                    if 1 <= t <= T:
                        u = t - 1
                        pe.wait_ge(otlo_done, 2 * u + 2)
                        if u:
                            pe.wait_ge(x1_done, 2 * u)
                        for c in range(KD):
                            if c == KD // 2 and t >= 2:
                                h2_transposes(t - 2)
                            for lhs, rhs in ((othi[u % 2], "hi"), (othi[u % 2], "lo"), (otlo[u % 2], "hi")):
                                for n in range(2):
                                    cols = slice(n * BANK, (n + 1) * BANK)
                                    last = pe.matmul(WO[:, cols], lhs[:, c, :], wo[rhs][:, c, cols],
                                                     start=(c == 0 and rhs == "hi" and lhs is othi[u % 2]),
                                                     stop=(c == KD - 1 and lhs is otlo[u % 2]))
                        last.then_inc(wo_done, 1)
                    if t < T:
                        pe.wait_ge(on_done, 2 * t + 2)
                        if t:
                            pe.wait_ge(otlo_done, 2 * t)
                        for b in range(2):
                            for i in range(4):
                                c = 4 * b + i
                                last = pe.transpose(ps[:, OT[b], i * P:(i + 1) * P], o[t % 3][:, c * P:(c + 1) * P], k["ident"][:])
                            last.then_inc(ot_ready, 1)
                    if 2 <= t <= T + 1:
                        u = t - 2
                        if t > T:
                            h2_transposes(u)
                        if u == 0:
                            pe.wait_ge(small_loaded, 32)
                        else:
                            pe.wait_ge(lexp_done, u)
                        for c in range(KD):
                            pe.wait_ge(ht_copied, 2 * u + c // 4 + 1)
                            last = pe.matmul(LG, h2T[:, c, :], wr[:, c, :], start=(c == 0), stop=(c == KD - 1))
                        last.then_inc(lg_ready, 1)
                    if t >= 3:
                        u = t - 3
                        pe.wait_ge(aff_done, u + 1)
                        if u:
                            pe.wait_ge(at_done, u)
                        pe.transpose(AT, aff, k["ident"][:]).then_inc(at_ready, 1)

            @block.scalar
            def _(act):
                def squares(t):
                    act.wait_ge(o_loaded[t % 3], 16 * (t // 3 + 1))
                    if t:
                        act.wait_ge(sso_done, 2 * t)
                        if t >= 3:
                            act.wait_ge(ss2_done, t - 2)
                    for n in range(2):
                        cols = slice(n * C_K, (n + 1) * C_K)
                        act.activation(sq[:, cols], o[t % 3][:, cols], ACT.Square, accum_out=sso(t)[:, n:n + 1]).then_inc(sso_done, 1)

                squares(0)
                for t in range(T + 2):
                    if t + 1 < T:
                        squares(t + 1)
                    if t >= 2:
                        u = t - 2
                        for b in range(2):
                            act.wait_ge(ht_ready, 2 * u + b + 1)
                            if u and b == 0:
                                act.wait_ge(lg_ready, u)
                            act.activation(h2T[:, 4 * b:4 * b + 4, :], ps[:, HT[b], :].rearrange("p (a c) -> p a c", a=4),
                                           ACT.Copy).then_inc(ht_copied, 1)
                    if t < T:
                        for b in range(2):
                            act.wait_ge(ot_ready, 2 * t + b + 1)
                            if t >= 2 and b == 0:
                                act.wait_ge(wo_done, t - 1)
                            act.activation(othi[t % 2][:, 4 * b:4 * b + 4, :], ps[:, OT[b], :].rearrange("p (a c) -> p a c", a=4),
                                           ACT.Copy).then_inc(othi_done, 1)
                    if 1 <= t <= T:
                        u = t - 1
                        act.wait_ge(x1_done, 2 * u + 2)
                        act.wait_ge(sso_done, 2 * min(t + 2, T))
                        act.activation(sq[:], x1[u % 2][:], ACT.Square, accum_out=ss2(u)).then_inc(ss2_done, 1)
                    if t >= 2:
                        u = t - 2
                        act.wait_ge(lmax_done, u + 1)
                        if u:
                            act.wait_ge(at_ready, u)
                        act.activation(aff, LG, ACT.Exp, bias=lmax(u), accum_out=lsum(u)).then_inc(lexp_done, 1)

            @block.vector
            def _(dve):
                steps = Steps(dve, vsteps)
                def group_rows(t):
                    dve.wait_ge(ro_done, t + 1)
                    for n in range(2):
                        cols = slice(n * C_K, (n + 1) * C_K)
                        dve.tensor_scalar(o[t % 3][:, cols], o[t % 3][:, cols], ro(t)[:, n:n + 1], None, ALU.mult).then_inc(on_done, 1)

                group_rows(0)
                for t in range(T + 3):
                    if 1 <= t <= T:
                        u = t - 1
                        dve.wait_ge(wo_done, u + 1)
                        dve.wait_ge(xr_loaded[u % 3], 16 * (u // 3 + 1))
                        if u >= 2:
                            dve.wait_ge(x1_stored[u % 2], 16 * (u // 2))
                            dve.wait_ge(h2_done, u - 1)
                        for n in range(2):
                            cols = slice(n * BANK, (n + 1) * BANK)
                            dve.tensor_tensor(x1[u % 2][:, cols], WO[:, cols], xr[u % 3][:, cols], ALU.add).then_inc(x1_done, 1)
                    if t < T:
                        for b in range(2):
                            dve.wait_ge(othi_done, 2 * t + b + 1)
                            dve.tensor_tensor(otlo[t % 2][:, 4 * b:4 * b + 4, :], ps[:, OT[b], :].rearrange("p (a c) -> p a c", a=4),
                                              othi[t % 2][:, 4 * b:4 * b + 4, :].bitcast(F32), ALU.subtract).then_inc(otlo_done, 1)
                    if t + 1 < T:
                        group_rows(t + 1)
                    if 1 <= t <= T:
                        if u == 0:
                            dve.wait_ge(small_loaded, 32)
                        if u >= 2:
                            dve.wait_ge(h2_stored[u % 2], 16 * (u // 2))
                        dve.wait_ge(x1_done, 2 * u + 2)
                        dve.wait_ge(r2_done, u + 1)
                        dve.scalar_tensor_tensor(out=h2[u % 2][:], in0=x1[u % 2][:], scalar=r2(u), in1=gffn[:],
                                                 op0=ALU.mult, op1=ALU.mult).then_inc(h2_done, 1)
                    if 2 <= t <= T + 1:
                        u = t - 2
                        dve.wait_ge(lg_ready, u + 1)
                        dve.tensor_reduce(lmax(u), LG, AX.X, ALU.max, negate=True).then_inc(lmax_done, 1)
                        dve.wait_ge(lexp_done, u + 1)
                        dve.reciprocal(lrec(u), lsum(u)).then_inc(lrec_done, 1)
                        dve.wait_ge(lrec_done, u + 1)
                        dve.tensor_scalar(aff, aff, lrec(u), None, ALU.mult).then_inc(aff_done, 1)
                    if t >= 3:
                        u = t - 3
                        dve.wait_ge(at_ready, u + 1)
                        dve.tensor_copy(k["affT"][:, u * P:(u + 1) * P], AT).then_inc(at_done, 1)
                        if u >= TS - 1:
                            dve.wait_ge(at_done, u + 1)
                            for r in range(3 * (u - TS + 1), min(3 * (u - TS + 2), CAP // 8)):
                                top_eight(dve, k, 0, r, steps)


def top_eight(dve, k, s, r, steps):
    aff = k["affT"][:, s * SEQ:(s + 1) * SEQ]
    cols = slice(s * CAP + 8 * r, s * CAP + 8 * r + 8)
    steps.did(dve.max(k["gates"][:, cols], aff))
    steps.wait()
    steps.did(dve.max_index(k["idx8"][:, cols], k["gates"][:, cols], aff))
    steps.wait()
    steps.did(dve.match_replace(aff, k["gates"][:, cols], aff, -1.0))
    steps.wait()


def experts(nc, a, k, moe, ps, banks, out, h2_dram, raw_loaded):
    raw, hi, lo = moe["raw"], moe["hi"], moe["lo"]
    xe, xehi, xelo, silu, h, hthi, htlo, y = (moe[n] for n in ("xe", "xehi", "xelo", "silu", "h", "hthi", "htlo", "y"))
    X, G, U, Y = (0, 1), (2, 3), (4, 5), (6, 7)
    LAST = EXPERTS - 1
    POOL_LO = 3

    with Phase(nc, "m") as phase:
        sem = phase.sem
        hi_done, lo_done, chunk_used = sem("hi_done"), sem("lo_done"), sem("chunk_used")
        idx_float, route_ready, gates_ready, idx_ready = sem("idx_float"), sem("route_ready"), sem("gates_ready"), sem("idx_ready")
        xe_loaded, xt_ready, xehi_done, xelo_done = sem("xe_loaded"), sem("xe_transposed"), sem("xehi_done"), sem("xelo_done")
        gu_done, silu_done, h_done = sem("gu_done"), sem("silu_done"), sem("h_done")
        ht_ready, hthi_done, htlo_done = sem("h_transposed"), sem("hthi_done"), sem("htlo_done")
        y_ready, y_done, y_free, added = sem("y_ready"), sem("y_done"), sem("y_free"), sem("added")
        vsteps, psteps = sem("vector_steps_e"), sem("pool_steps_e")
        with nc.Block() as block:

            @block.sync
            def _(sp):
                need_split = sp.alloc_register("need_split")

                def load(e, j, c):
                    sp.reg_mov(need_split, c - RING + 1)
                    sp.wait_ge(raw_loaded[0], 16)
                    sp.wait_ge(lo_done, need_split)
                    load_chunk(sp, a, moe, raw_loaded, e, j)

                with sp.Fori(0, LAST) as e:
                    for j in range(RING, CHUNKS):
                        load(e, j, e * CHUNKS + j)
                    for j in range(RING):
                        load(e + 1, j, e * CHUNKS + CHUNKS + j)
                for j in range(RING, CHUNKS):
                    load(LAST, j, LAST * CHUNKS + j)

            @block.gpsimd
            def _(pool):
                need_copied, need_free, need_output = (pool.alloc_register(n) for n in ("need_copied", "need_free", "need_output"))

                def gather(e, turn):
                    pool.tensor_copy(moe["take"][:], moe["idxT"][:, bass.ds(e, 1)]).then_inc(psteps, 1)
                    pool.reg_mov(need_copied, turn + 1)
                    pool.wait_ge(idx_ready, 1)
                    pool.wait_ge(psteps, need_copied)
                    pool.indirect_dma_start(xe[:, :], None, h2_dram, bass.IndirectOffsetOnAxis(moe["take"][:, 0:1], 0)).then_inc(xe_loaded, 16)

                def add_rows(e):
                    pool.tensor_copy(moe["give"][:], moe["idxT"][:, bass.ds(e, 1)]).then_inc(y_free, 1)
                    pool.reg_mov(need_free, e + 1)
                    pool.reg_mov(need_output, 2 * e + 2)
                    pool.wait_ge(idx_ready, 1)
                    pool.wait_ge(y_free, need_free)
                    pool.wait_ge(y_done, need_output)
                    pool.indirect_dma_start(out, bass.IndirectOffsetOnAxis(moe["give"][:, 0:1], 0), y[:, :], None,
                                            compute_op=ALU.add).then_inc(added, 16)
                    pool.wait_ge(added, 16 * e + 16)

                for j in range(POOL_LO):
                    pool.wait_ge(hi_done, j + 1)
                    pool.tensor_tensor(lo[j][:], raw[j][:], hi[j][:].bitcast(F32), ALU.subtract).then_inc(lo_done, 1)
                pool.wait_ge(idx_ready, 1)
                gather(0, 0)
                pool.wait_ge(xt_ready, 2)
                pool.wait_ge(xe_loaded, 16)
                gather(1, 1)
                with pool.Fori(1, LAST) as e:
                    pool.wait_ge(xt_ready, 2 * e + 2)
                    pool.wait_ge(xe_loaded, 16 * e + 16)
                    gather(e + 1, e + 1)
                    add_rows(e - 1)
                add_rows(LAST - 1)
                add_rows(LAST)

            @block.tensor
            def _(pe):
                def transposes(src, bank, cols, ready):
                    for i in range(4):
                        last = pe.transpose(ps[:, bank, i * P:(i + 1) * P], src[:, cols + i * P:cols + (i + 1) * P], k["ident"][:])
                    last.then_inc(ready, 1)

                def gate_up(e, j):
                    half, group = j // 4, j % 4 // 2
                    pe.wait_ge(xelo_done, 2 * e + group + 1)
                    pe.wait_ge(lo_done, e * CHUNKS + j + 2)
                    g, u = j % RING, (j + 1) % RING
                    for i in range(CK):
                        c = group * CK + i
                        cols = slice(i * BANK, (i + 1) * BANK)
                        start, stop = c == 0, c == KD - 1
                        for bank, w in ((G[half], g), (U[half], u)):
                            pe.matmul(ps[:, bank, :], xehi[:, c, :], hi[w][:, cols], start=start, stop=False)
                            pe.matmul(ps[:, bank, :], xehi[:, c, :], lo[w][:, cols], start=False, stop=False)
                        for bank, w in ((G[half], g), (U[half], u)):
                            last = pe.matmul(ps[:, bank, :], xelo[:, c, :], hi[w][:, cols], start=False, stop=stop)
                            if i == CK - 1 and not (stop and bank == U[half]):
                                last.then_inc(chunk_used, 1)
                    if c == KD - 1:
                        last.then_inc(gu_done, 1)

                def down(e, j):
                    pe.wait_ge(lo_done, e * CHUNKS + j + 1)
                    w = j % RING
                    for i in range(2):
                        f = 2 * (j - 8) + i
                        for lhs, part in ((hthi, hi), (hthi, lo), (htlo, hi)):
                            for n in range(2):
                                cols = slice(i * D + n * BANK, i * D + (n + 1) * BANK)
                                last = pe.matmul(ps[:, Y[n], :], lhs[:, f, :], part[w][:, cols],
                                                 start=(f == 0 and part is hi and lhs is hthi), stop=(f == KD - 1 and lhs is htlo))
                    last.then_inc(y_ready if j == CHUNKS - 1 else chunk_used, 1)

                def expert(e, more):
                    gate_up(e, 0)
                    gate_up(e, 2)
                    gate_up(e, 4)
                    pe.wait_ge(h_done, 2 * e + 1)
                    transposes(h, X[0], 0, ht_ready)
                    gate_up(e, 6)
                    pe.wait_ge(htlo_done, 2 * e + 1)
                    down(e, 8)
                    pe.wait_ge(h_done, 2 * e + 2)
                    transposes(h, X[1], BANK, ht_ready)
                    down(e, 9)
                    if more:
                        pe.wait_ge(xe_loaded, 16 * e + 32)
                        transposes(xe, X[0], 0, xt_ready)
                    pe.wait_ge(htlo_done, 2 * e + 2)
                    down(e, 10)
                    if more:
                        transposes(xe, X[1], BANK, xt_ready)
                    down(e, 11)

                pe.wait_ge(route_ready, 1)
                pe.transpose(ps[:, Y[0], 0:EXPERTS], k["gates"][:], k["ident"][0:EXPERTS, 0:EXPERTS])
                pe.transpose(ps[:, Y[0], P:P + EXPERTS], moe["idxf"][:], k["ident"][0:EXPERTS, 0:EXPERTS]).then_inc(route_ready, 1)
                pe.wait_ge(xe_loaded, 16)
                transposes(xe, X[0], 0, xt_ready)
                transposes(xe, X[1], BANK, xt_ready)
                with pe.Fori(0, LAST) as e:
                    expert(e, True)
                expert(LAST, False)

            def wait_used(eng, e, j):
                c = j - RING
                if c < 0:
                    c += CHUNKS
                    e = e - 1
                if c == 3:
                    eng.wait_ge(gu_done, 2 * e + 1)
                elif c == 7:
                    eng.wait_ge(gu_done, 2 * e + 2)
                elif c == CHUNKS - 1:
                    eng.wait_ge(y_ready, e + 1)
                else:
                    n = c + 1 - (c > 3) - (c > 7)
                    eng.wait_ge(chunk_used, e * (CHUNKS - 3) + n)

            @block.scalar
            def _(act):
                def split(e, j, wait=True):
                    act.wait_ge(raw_loaded[j % RING], 16 * (e * (CHUNKS // RING) + j // RING + 1))
                    if wait:
                        wait_used(act, e, j)
                    act.activation(hi[j % RING][:], raw[j % RING][:], ACT.Copy).then_inc(hi_done, 1)

                def high(dst, b, ready, n, done):
                    act.wait_ge(ready, n)
                    act.activation(dst[:, 4 * b:4 * b + 4, :], ps[:, X[b], :].rearrange("p (a c) -> p a c", a=4), ACT.Copy).then_inc(done, 1)

                def gate(e, half):
                    act.wait_ge(gu_done, 2 * e + half + 1)
                    act.activation(silu[:, half * BANK:(half + 1) * BANK], ps[:, G[half], :], ACT.Silu).then_inc(silu_done, 1)

                def expert(e, more):
                    split(e, 6)
                    split(e, 7)
                    gate(e, 0)
                    split(e, 8)
                    split(e, 9)
                    high(hthi, 0, ht_ready, 2 * e + 1, hthi_done)
                    split(e, 10)
                    split(e, 11)
                    gate(e, 1)
                    if more:
                        split(e + 1, 0)
                        split(e + 1, 1)
                    high(hthi, 1, ht_ready, 2 * e + 2, hthi_done)
                    if more:
                        split(e + 1, 2)
                        high(xehi, 0, xt_ready, 2 * e + 3, xehi_done)
                        split(e + 1, 3)
                        high(xehi, 1, xt_ready, 2 * e + 4, xehi_done)
                        split(e + 1, 4)
                        split(e + 1, 5)
                    act.wait_ge(y_ready, e + 1)
                    act.wait_ge(y_free, e + 1)
                    for n in range(2):
                        act.activation(y[:, n * BANK:(n + 1) * BANK], ps[:, Y[n], :], ACT.Copy,
                                       scale=moe["gT"][:, bass.ds(e, 1)]).then_inc(y_done, 1)

                for j in range(RING):
                    split(0, j, wait=False)
                for b in range(2):
                    high(xehi, b, xt_ready, b + 1, xehi_done)
                act.wait_ge(gates_ready, 1)
                with act.Fori(0, LAST) as e:
                    expert(e, True)
                expert(LAST, False)

            @block.vector
            def _(dve):
                steps = Steps(dve, vsteps)

                def split(e, j):
                    dve.wait_ge(hi_done, e * CHUNKS + j + 1)
                    dve.tensor_tensor(lo[j % RING][:], raw[j % RING][:], hi[j % RING][:].bitcast(F32), ALU.subtract).then_inc(lo_done, 1)

                def low(dst, part, b, ready, n, done):
                    dve.wait_ge(ready, n)
                    cols = slice(4 * b, 4 * b + 4)
                    dve.tensor_tensor(dst[:, cols, :], ps[:, X[b], :].rearrange("p (a c) -> p a c", a=4),
                                      part[:, cols, :].bitcast(F32), ALU.subtract).then_inc(done, 1)

                def product(e, half):
                    cols = slice(half * BANK, (half + 1) * BANK)
                    dve.wait_ge(silu_done, 2 * e + half + 1)
                    dve.tensor_tensor(h[:, cols], ps[:, U[half], :], silu[:, cols], ALU.mult).then_inc(h_done, 1)

                def expert(e, more):
                    split(e, 6)
                    split(e, 7)
                    product(e, 0)
                    split(e, 8)
                    split(e, 9)
                    low(htlo, hthi, 0, hthi_done, 2 * e + 1, htlo_done)
                    split(e, 10)
                    split(e, 11)
                    product(e, 1)
                    if more:
                        split(e + 1, 0)
                        split(e + 1, 1)
                    low(htlo, hthi, 1, hthi_done, 2 * e + 2, htlo_done)
                    if more:
                        split(e + 1, 2)
                        low(xelo, xehi, 0, xehi_done, 2 * e + 3, xelo_done)
                        split(e + 1, 3)
                        low(xelo, xehi, 1, xehi_done, 2 * e + 4, xelo_done)
                        split(e + 1, 4)
                        split(e + 1, 5)

                for r in range(CAP // 8):
                    top_eight(dve, k, 1, r, steps)
                steps.did(dve.tensor_copy(moe["idxf"][:], k["idx8"][:]))
                steps.wait()
                dve.tensor_scalar(moe["idxf"][:, CAP:2 * CAP], moe["idxf"][:, CAP:2 * CAP], float(SEQ), None, ALU.add).then_inc(route_ready, 1)
                dve.wait_ge(route_ready, 2)
                dve.tensor_copy(moe["idxT"][:], ps[:, Y[0], P:P + EXPERTS]).then_inc(idx_ready, 1)
                dve.tensor_copy(moe["gT"][:], ps[:, Y[0], 0:EXPERTS]).then_inc(gates_ready, 1)
                dve.wait_ge(lo_done, POOL_LO)
                split(0, POOL_LO)
                for b in range(2):
                    low(xelo, xehi, b, xehi_done, b + 1, xelo_done)
                for j in range(POOL_LO + 1, RING):
                    split(0, j)
                with dve.Fori(0, LAST) as e:
                    expert(e, True)
                expert(LAST, False)


_WEIGHTS = ["norm_attn", "w_in", "gqa_q_norm", "gqa_k_norm", "mla_q_a_norm", "mla_w_uq", "mla_q_nope_norm",
            "mla_q_pe_norm", "mla_kv_a_norm", "mla_w_ukv", "mla_k_nope_norm", "mla_k_pe_norm", "out_norm_a",
            "out_norm_b", "w_o", "norm_ffn", "w_router", "w_gate", "w_up", "w_down"]


def kernel(x_prompt, x_sample, **weights):
    import numpy as _np
    import concourse.bacc as _bacc
    from concourse import mybir as _mybir
    from concourse.bass_utils import run_bass_kernel_spmd as _run

    nc = _bacc.Bacc("TRN2", target_bir_lowering=False, num_devices=1)
    named = {"x": _np.concatenate([_np.asarray(x_prompt).reshape(SEQ, D), _np.asarray(x_sample).reshape(SEQ, D)]),
             "tab": rotary_tables(), "invn": inverse_counts()}
    for name in _WEIGHTS:
        named[name] = _np.ascontiguousarray(weights[name])
    aps = {n: nc.dram_tensor(f"in_{n}", v.shape, _mybir.dt.from_np(v.dtype), kind="ExternalInput").ap() for n, v in named.items()}
    out = nc.dram_tensor("out", (SETS * SEQ, D), _mybir.dt.float32, kind="ExternalOutput").ap()
    build(nc, aps, out)
    r = _run(nc, [{f"in_{n}": v for n, v in named.items()}], core_ids=[0])
    got = r.results[0]["out"]
    return got[0:SEQ].reshape(1, SEQ, D), got[SEQ:].reshape(1, SEQ, D)
```
